# Optimizing a Trainium2 kernel written in Bass

```python
import math
import jax, jax.numpy as jnp
from jax import lax
import numpy as np

D_MODEL = 2048
BATCH = 1
SEQ = 512
DEPTH = 1
DEC_BATCH = 8
DEC_SEQ = 1
PAST_LEN = 4096
PAGE_SIZE = 128

SSD_EXPAND = 2
D_INNER = SSD_EXPAND * D_MODEL
SSD_HEADDIM = 64
SSD_HEADS = D_INNER // SSD_HEADDIM
SSD_GROUPS = 8
SSD_STATE = 128
SSD_CONV = 4
SSD_CHUNK = 128
CONV_DIM = D_INNER + 2 * SSD_GROUPS * SSD_STATE
MLP_CHUNK = 128
D_GATE = D_MODEL
MLP_GROUPS = 16
MLP_GROUP_DIM = D_GATE // MLP_GROUPS
PEER_HEADS = 8
PEER_KEYS = 128
PEER_EXPERTS = PEER_KEYS * PEER_KEYS
PEER_DKEY = 256
PEER_TOPK = 16
PEER_BLOCK = 128
DN_ALPHA = (2.0 * DEPTH) ** 0.25
DN_BETA = (8.0 * DEPTH) ** -0.25
LN_EPS = 1e-5
RMS_EPS = 1e-5
D_IN_PROJ = D_INNER + CONV_DIM + SSD_HEADS + 2 * D_GATE + 2 * D_MODEL
IN_SPLITS = (D_INNER, D_INNER + CONV_DIM, D_INNER + CONV_DIM + SSD_HEADS,
             D_INNER + CONV_DIM + SSD_HEADS + 2 * D_GATE)

kernel_name = "hybrid_ssd_chunkmlp_peer_step"

def layer_norm(x, g, b):
    xf = x.astype(jnp.float32)
    mu = jnp.mean(xf, axis=-1, keepdims=True)
    xc = xf - mu
    var = jnp.mean(xc * xc, axis=-1, keepdims=True)
    return (xc * lax.rsqrt(var + LN_EPS) * g + b).astype(x.dtype)

def causal_conv(xbc, conv_state, conv_w, conv_b):
    L = xbc.shape[1]
    xp = jnp.concatenate([conv_state.astype(xbc.dtype), xbc], axis=1)
    out = conv_b + sum(xp[:, k:k + L] * conv_w[k] for k in range(SSD_CONV))
    return out, xp[:, L:]

def ssd_scan(xh, dt, A, Bm, Cm, init_state):
    b, L = xh.shape[:2]
    G, R, P, N = SSD_GROUPS, SSD_HEADS // SSD_GROUPS, SSD_HEADDIM, SSD_STATE
    Q = min(SSD_CHUNK, L)
    Lp = -(-L // Q) * Q
    nc = Lp // Q
    pad = Lp - L
    f32 = jnp.float32
    xh = jnp.pad(xh.astype(f32), ((0, 0), (0, pad), (0, 0), (0, 0)))
    dt = jnp.pad(dt.astype(f32), ((0, 0), (0, pad), (0, 0)))
    Bm = jnp.pad(Bm.astype(f32), ((0, 0), (0, pad), (0, 0), (0, 0)))
    Cm = jnp.pad(Cm.astype(f32), ((0, 0), (0, pad), (0, 0), (0, 0)))
    x_c = xh.reshape(b, nc, Q, G, R, P)
    dt_c = dt.reshape(b, nc, Q, G, R)
    B_c = Bm.reshape(b, nc, Q, G, N)
    C_c = Cm.reshape(b, nc, Q, G, N)
    acum = jnp.cumsum(dt_c * A.reshape(G, R), axis=2)
    xdt = x_c * dt_c[..., None]
    seg = acum[:, :, :, None] - acum[:, :, None, :]
    causal = jnp.tril(jnp.ones((Q, Q), dtype=bool))[None, None, :, :, None, None]
    decay = jnp.exp(jnp.where(causal, seg, -jnp.inf))
    cb = jnp.einsum('bcign,bcjgn->bcijg', C_c, B_c)
    y_diag = jnp.einsum('bcijg,bcijgr,bcjgrp->bcigrp', cb, decay, xdt)
    decay_to_end = jnp.exp(acum[:, :, -1:] - acum)
    chunk_states = jnp.einsum('bcjgn,bcjgr,bcjgrp->bcgrpn', B_c, decay_to_end, xdt)
    chunk_decay = jnp.exp(acum[:, :, -1])

    def step(carry, inp):
        st, dcy = inp
        return carry * dcy[..., None, None] + st, carry

    init = init_state.astype(f32).reshape(b, G, R, P, N)
    final, states_in = lax.scan(step, init, (jnp.moveaxis(chunk_states, 1, 0),
                                             jnp.moveaxis(chunk_decay, 1, 0)))
    states_in = jnp.moveaxis(states_in, 0, 1)
    y_off = jnp.einsum('bcign,bcgrpn,bcigr->bcigrp', C_c, states_in, jnp.exp(acum))
    y = (y_diag + y_off).reshape(b, Lp, SSD_HEADS, P)[:, :L]
    return y, final.reshape(b, SSD_HEADS, P, N).astype(init_state.dtype)

def ssd_branch(z, xbc, dt_raw, conv_state, ssm_state, conv_w, conv_b, dt_bias, a_log, d_skip, norm_w):
    b, L = z.shape[:2]
    xbc_c, new_conv = causal_conv(xbc, conv_state, conv_w, conv_b)
    xbc_c = jax.nn.silu(xbc_c)
    xs, Bm, Cm = jnp.split(xbc_c, (D_INNER, D_INNER + SSD_GROUPS * SSD_STATE), axis=-1)
    dt = jax.nn.softplus(dt_raw.astype(jnp.float32) + dt_bias.astype(jnp.float32))
    A = -jnp.exp(a_log.astype(jnp.float32))
    xh = xs.reshape(b, L, SSD_HEADS, SSD_HEADDIM)
    y, new_ssm = ssd_scan(xh, dt, A, Bm.reshape(b, L, SSD_GROUPS, SSD_STATE),
                          Cm.reshape(b, L, SSD_GROUPS, SSD_STATE), ssm_state)
    y = y + d_skip.astype(jnp.float32)[:, None] * xh.astype(jnp.float32)
    yg = (y.reshape(b, L, D_INNER) * jax.nn.silu(z.astype(jnp.float32)))
    yg = yg.reshape(b, L, SSD_GROUPS, D_INNER // SSD_GROUPS)
    yg = yg * lax.rsqrt(jnp.mean(yg * yg, axis=-1, keepdims=True) + RMS_EPS)
    y_out = (yg.reshape(b, L, D_INNER) * norm_w).astype(z.dtype)
    return y_out, new_conv, new_ssm

def chunk_sgu_branch(uv, ln_g, ln_b, w_s, b_s):
    b, L = uv.shape[:2]
    uv = jax.nn.gelu(uv, approximate=False)
    u, v = jnp.split(uv, 2, axis=-1)
    v = layer_norm(v, ln_g, ln_b)
    Lp = -(-L // MLP_CHUNK) * MLP_CHUNK
    nc = Lp // MLP_CHUNK
    vc = jnp.pad(v, ((0, 0), (0, Lp - L), (0, 0))).reshape(b, nc, MLP_CHUNK, MLP_GROUPS, MLP_GROUP_DIM)
    w = w_s * jnp.tril(jnp.ones((MLP_CHUNK, MLP_CHUNK), dtype=w_s.dtype))
    s = jnp.einsum('gij,bcjgd->bcigd', w, vc) + b_s.T[None, None, :, :, None]
    s = s.reshape(b, Lp, D_GATE)[:, :L]
    n_last = L - MLP_CHUNK * ((L - 1) // MLP_CHUNK)
    return u * s, v[:, L - n_last:]

def peer(h, w_q, sub_keys, u_tab, v_tab):
    b, L, D = h.shape
    T = b * L
    t = h.reshape(T, D)
    K = PEER_TOPK
    q = (t @ w_q).astype(jnp.float32).reshape(T, PEER_HEADS, 2, PEER_DKEY // 2)
    s = jnp.einsum('thsd,hskd->thsk', q, sub_keys.astype(jnp.float32))
    top_s, top_i = lax.top_k(s, K)
    cand = (top_s[:, :, 0, :, None] + top_s[:, :, 1, None, :]).reshape(T, PEER_HEADS, K * K)
    best_s, best_c = lax.top_k(cand, K)
    i1 = jnp.take_along_axis(top_i[:, :, 0], best_c // K, axis=-1)
    i2 = jnp.take_along_axis(top_i[:, :, 1], best_c % K, axis=-1)
    expert = i1 * PEER_KEYS + i2
    gate = jax.nn.softmax(best_s, axis=-1).astype(h.dtype)
    nb = -(-T // PEER_BLOCK)
    Tp = nb * PEER_BLOCK
    pad = Tp - T
    t_b = jnp.pad(t, ((0, pad), (0, 0))).reshape(nb, PEER_BLOCK, D)
    e_b = jnp.pad(expert, ((0, pad), (0, 0), (0, 0))).reshape(nb, PEER_BLOCK, PEER_HEADS, K)
    g_b = jnp.pad(gate, ((0, pad), (0, 0), (0, 0))).reshape(nb, PEER_BLOCK, PEER_HEADS, K)

    def block(args):
        tb, eb, gb = args
        ue = u_tab[eb]
        ve = v_tab[eb]
        act = jax.nn.gelu(jnp.einsum('td,thkd->thk', tb, ue), approximate=False)
        return jnp.einsum('thk,thkd->td', gb * act, ve)

    out = lax.map(block, (t_b, e_b, g_b))
    return out.reshape(Tp, D)[:T].reshape(b, L, D)

def trunk(x, conv_states, ssm_states, w_in, conv_w, conv_b, dt_bias, a_log, d_skip, ssd_norm_w,
          sgu_ln_g, sgu_ln_b, sgu_w, sgu_b, w_branch_a, w_branch_b, w_out, ln1_g, ln1_b,
          peer_wq, peer_keys, peer_u, peer_v, ln2_g, ln2_b):
    new_conv, new_ssm, new_v = [], [], []
    for i in range(DEPTH):
        proj = x @ w_in[i]
        z, xbc, dt_raw, uv, gates = jnp.split(proj, IN_SPLITS, axis=-1)
        y_a, c_i, s_i = ssd_branch(z, xbc, dt_raw, conv_states[i], ssm_states[i], conv_w[i], conv_b[i],
                                   dt_bias[i], a_log[i], d_skip[i], ssd_norm_w[i])
        y_b, v_i = chunk_sgu_branch(uv, sgu_ln_g[i], sgu_ln_b[i], sgu_w[i], sgu_b[i])
        g_a, g_b = jnp.split(jax.nn.sigmoid(gates), 2, axis=-1)
        merged = g_a * (y_a @ w_branch_a[i]) + g_b * (y_b @ w_branch_b[i])
        mix = merged @ w_out[i]
        h = layer_norm(DN_ALPHA * x + mix, ln1_g[i], ln1_b[i])
        x = layer_norm(DN_ALPHA * h + peer(h, peer_wq[i], peer_keys[i], peer_u[i], peer_v[i]),
                       ln2_g[i], ln2_b[i])
        new_conv.append(c_i)
        new_ssm.append(s_i)
        new_v.append(v_i)
    return x, jnp.stack(new_conv), jnp.stack(new_ssm), jnp.stack(new_v)

def setup_inputs(seed: int = 0) -> dict:
    key = jax.random.key(seed)
    ks = jax.random.split(key, 32)
    nrm = lambda k, shape, s: jax.random.normal(k, shape, jnp.float32) * s
    dt0 = jnp.exp(jax.random.uniform(ks[5], (DEPTH, SSD_HEADS), jnp.float32,
                                     minval=math.log(1e-3), maxval=math.log(1e-1)))
    return {
        "x_prompt": nrm(ks[0], (BATCH, SEQ, D_MODEL), 1.0),
        "x_sample": nrm(ks[1], (DEC_BATCH, DEC_SEQ, D_MODEL), 1.0),
        "state_conv": nrm(ks[2], (DEPTH, DEC_BATCH, SSD_CONV - 1, CONV_DIM), 1.0),
        "state_ssm": nrm(ks[3], (DEPTH, DEC_BATCH, SSD_HEADS, SSD_HEADDIM, SSD_STATE), 0.5),
        "w_in": nrm(ks[4], (DEPTH, D_MODEL, D_IN_PROJ), D_MODEL ** -0.5),
        "conv_w": nrm(ks[6], (DEPTH, SSD_CONV, CONV_DIM), SSD_CONV ** -0.5),
        "conv_b": nrm(ks[7], (DEPTH, CONV_DIM), 0.01),
        "dt_bias": dt0 + jnp.log(-jnp.expm1(-dt0)),
        "a_log": jnp.log(jax.random.uniform(ks[8], (DEPTH, SSD_HEADS), jnp.float32, minval=1.0, maxval=16.0)),
        "d_skip": 1.0 + nrm(ks[9], (DEPTH, SSD_HEADS), 0.1),
        "ssd_norm_w": 1.0 + nrm(ks[10], (DEPTH, D_INNER), 0.01),
        "sgu_ln_g": 1.0 + nrm(ks[11], (DEPTH, D_GATE), 0.01),
        "sgu_ln_b": nrm(ks[12], (DEPTH, D_GATE), 0.01),
        "sgu_w": nrm(ks[13], (DEPTH, MLP_GROUPS, MLP_CHUNK, MLP_CHUNK), MLP_CHUNK ** -0.5),
        "sgu_b": 1.0 + nrm(ks[14], (DEPTH, MLP_GROUPS, MLP_CHUNK), 0.01),
        "w_branch_a": nrm(ks[15], (DEPTH, D_INNER, D_MODEL), D_INNER ** -0.5),
        "w_branch_b": nrm(ks[16], (DEPTH, D_GATE, D_MODEL), D_GATE ** -0.5),
        "w_out": nrm(ks[17], (DEPTH, D_MODEL, D_MODEL), DN_BETA * D_MODEL ** -0.5),
        "ln1_g": 1.0 + nrm(ks[18], (DEPTH, D_MODEL), 0.01),
        "ln1_b": nrm(ks[19], (DEPTH, D_MODEL), 0.01),
        "peer_wq": nrm(ks[20], (DEPTH, D_MODEL, PEER_HEADS * PEER_DKEY), D_MODEL ** -0.5),
        "peer_keys": nrm(ks[21], (DEPTH, PEER_HEADS, 2, PEER_KEYS, PEER_DKEY // 2), (PEER_DKEY // 2) ** -0.5),
        "peer_u": nrm(ks[22], (DEPTH, PEER_EXPERTS, D_MODEL), D_MODEL ** -0.5),
        "peer_v": nrm(ks[23], (DEPTH, PEER_EXPERTS, D_MODEL), DN_BETA),
        "ln2_g": 1.0 + nrm(ks[24], (DEPTH, D_MODEL), 0.01),
        "ln2_b": nrm(ks[25], (DEPTH, D_MODEL), 0.01),
    }

def reference(x_prompt, x_sample, state_conv, state_ssm, w_in, conv_w, conv_b, dt_bias, a_log, d_skip,
              ssd_norm_w, sgu_ln_g, sgu_ln_b, sgu_w, sgu_b, w_branch_a, w_branch_b, w_out, ln1_g, ln1_b,
              peer_wq, peer_keys, peer_u, peer_v, ln2_g, ln2_b):
    b_p = x_prompt.shape[0]
    conv0 = jnp.zeros((DEPTH, b_p, SSD_CONV - 1, CONV_DIM), x_prompt.dtype)
    ssm0 = jnp.zeros((DEPTH, b_p, SSD_HEADS, SSD_HEADDIM, SSD_STATE), state_ssm.dtype)
    y_prompt, conv_prompt, ssm_prompt, sgu_v_prompt = trunk(
        x_prompt, conv0, ssm0, w_in, conv_w, conv_b, dt_bias, a_log, d_skip, ssd_norm_w,
        sgu_ln_g, sgu_ln_b, sgu_w, sgu_b, w_branch_a, w_branch_b, w_out, ln1_g, ln1_b,
        peer_wq, peer_keys, peer_u, peer_v, ln2_g, ln2_b)
    y_sample, conv_sample, ssm_sample, sgu_v_sample = trunk(
        x_sample, state_conv, state_ssm, w_in, conv_w, conv_b, dt_bias, a_log, d_skip, ssd_norm_w,
        sgu_ln_g, sgu_ln_b, sgu_w, sgu_b, w_branch_a, w_branch_b, w_out, ln1_g, ln1_b,
        peer_wq, peer_keys, peer_u, peer_v, ln2_g, ln2_b)
    return (y_prompt, y_sample, conv_prompt, ssm_prompt, sgu_v_prompt, conv_sample, ssm_sample, sgu_v_sample)


_drawn_inputs = setup_inputs


def setup_inputs(seed=0):
    import zlib

    import numpy as np

    out = dict(_drawn_inputs(seed))
    spreads = {}
    factors = {'conv_b': 3.528,
     'ssd_norm_w': 16.986,
     'sgu_ln_g': 52.691,
     'sgu_ln_b': 20.497,
     'sgu_b': 15.404,
     'ln2_g': 177.221,
     'ln2_b': 171.273}
    for name, (base, spread) in spreads.items():
        noise = np.random.default_rng([zlib.crc32(name.encode()), seed]).standard_normal(out[name].shape)
        drawn = base * np.exp(spread * noise) if base else spread * noise
        out[name] = __import__('jax').numpy.asarray(drawn.astype(out[name].dtype))
    for name, factor in factors.items():
        out[name] = (out[name] * factor).astype(out[name].dtype)
    return out
```

```python
from contextlib import ExitStack, contextmanager

import numpy as np

import concourse.bass as bass
from concourse import mybir

F32 = mybir.dt.float32
U32 = mybir.dt.uint32
ALU = mybir.AluOpType
ACT = mybir.ActivationFunctionType
AX_X = mybir.AxisListType.X

P = 128
D = 2048
KB = D // P
TP = 512
NS = 8
T = TP + NS
H2 = T // 2
CH = 4
G = 8
HG = 8
HD = 64
NH = G * HG
GT = HG * HD // P
NST = 128
CT = 2 + GT
FT = D // P
EPS = 1e-5
ALPHA = 2.0 ** 0.25
PH = 8
TOPK = 16
NB = 5
NEG = -3.0e38
WCOLS = KB * P

N_SSD = G * (CT + GT)
N_V = FT
N_U = FT
N_BR_B = 2 * FT
N_BR_A = 3 * FT
N_OUT = FT
N_Q = FT
O_V = N_SSD
O_U = O_V + N_V
O_BB = O_U + N_U
O_BA = O_BB + N_BR_B
O_OUT = O_BA + N_BR_A
O_Q = O_OUT + N_OUT
N_TILES = O_Q + N_Q

SSD_DVE = 4 * CT + 1 + 2 * CH + 1
SSD_POOL = 5 * GT

GP_B = CT * 4
GP_NW = GP_B + CT
GP_D = GP_NW + GT
GP_N = GP_D + GT


class Order:

    def __init__(self, eng, sem):
        self.eng, self.sem, self.base, self.n = eng, sem, 0, 0

    def __call__(self, ins):
        ins.then_inc(self.sem, 1)
        self.n += 1
        self.eng.wait_ge(self.sem, self.base + self.n)

    @contextmanager
    def body(self, i, count, per):
        before = self.base + self.n
        self.base, self.n = before + i * per, 0
        yield
        assert self.n == per, f"{self.n} counted in the body, {per} said"
        self.base, self.n = before + count * per, 0


def bc(ap, n):
    return ap.unsqueeze(ap.ndim).to_broadcast(list(ap.shape) + [n])


def mid(ap, axis, n):
    shape = list(ap.shape)
    return ap.unsqueeze(axis).to_broadcast(shape[:axis] + [n] + shape[axis:])


class Kernel:
    def __init__(self, nc, a, o):
        self.nc, self.a, self.o = nc, a, o

    def sem(self, name):
        handle = self.nc.alloc_semaphore(name=name)
        self.phase_sems.append(handle)
        return handle

    def alone(self, eng):
        key = str(eng.engine)
        if key not in self.ticks:
            self.ticks[key] = self.sem("tick_" + key.split(".")[-1] + str(len(self.nc.allocations)))
        eng.sem_inc(self.ticks[key], 1)

    def clear_sems(self):
        self.nc.clear_and_free_semaphores(self.phase_sems)
        self.nc.all_engine_barrier()
        self.phase_sems, self.ticks = [], {}

    def stream(self, sp, ring, landed, first, total, used_at):
        R = len(landed)
        w = self.a["w_tiles"]
        for j in range(R):
            sp.dma_start(ring[:, j, :], w[first + j]).then_inc(landed[j], 16)
        with sp.Fori(0, total // R - 1) as i:
            for j in range(R):
                sp.wait_ge(*used_at(i, j))
                sp.dma_start(ring[:, j, :], w[first + R + i * R + j]).then_inc(landed[j], 16)

    def gemm(self, pe, banks, free, free_at, ready, parts):
        for h in range(2):
            pe.wait_ge(free, free_at + h)
            for j, (slot, sem, val, acts) in enumerate(parts):
                if h == 0:
                    pe.wait_ge(sem, val)
                for k in range(KB):
                    last = pe.matmul(banks[h][:, 0:H2], slot[:, k * P:(k + 1) * P],
                                     acts[:, k, h * H2:(h + 1) * H2],
                                     start=(j == 0 and k == 0),
                                     stop=(j == len(parts) - 1 and k == KB - 1))
            last.then_inc(ready, 1)

    def build(self):
        nc = self.nc
        self.root = ExitStack()
        self.phase_sems, self.ticks = [], {}
        with self.root:
            sb = lambda name, shape, dt=F32: self.root.enter_context(nc.sbuf_tensor(name, shape, dt))
            self.ident = sb("ident", [P, P])
            self.ones = sb("ones", [P, P])
            self.triu = sb("triu", [P, P])
            self.onesD = sb("onesD", [P, P])
            self.onesG = sb("onesG", [P, P])
            self.eps = sb("eps", [P, 1])
            self.lnp = sb("lnp", [P, 4, FT])
            self.psum = self.root.enter_context(nc.psum_tensor("psum", [P, 8, 512], F32))
            self.bank = [self.psum[:, i, :] for i in range(8)]
            with ExitStack() as acts:
                xT = acts.enter_context(nc.sbuf_tensor("xT", [P, KB, T], F32))
                with ExitStack() as ya:
                    yA = ya.enter_context(nc.sbuf_tensor("yA", [P, G * GT, T], F32))
                    with ExitStack() as st:
                        tabs = self.tables(st, xT)
                        self.clear_sems()
                        self.ssd(st, xT, yA, tabs)
                    self.clear_sems()
                    merged = ya.enter_context(nc.sbuf_tensor("merged", [P, FT, T], F32))
                    with ExitStack() as st:
                        yB = st.enter_context(nc.sbuf_tensor("yB", [P, FT, T], F32))
                        self.sgu(xT, merged, yB)
                        self.clear_sems()
                        self.merge_b(xT, yB, merged)
                    self.merge_a(xT, yA, merged)
                    self.clear_sems()
                    self.project_out(merged, xT)
                self.query(xT)

    def tables(self, st, xT):
        nc, a = self.nc, self.a
        tab = st.enter_context(nc.sbuf_tensor("dt_tab", [P, G, 4, CH, HG], F32))
        stab = st.enter_context(nc.sbuf_tensor("dt_smp", [P, G, 2, GT, NS], F32))
        NC = CH * NH
        W = NC + NS
        with ExitStack() as tmp:
            sb = lambda name, shape, dt=F32: tmp.enter_context(nc.sbuf_tensor(name, shape, dt))
            wdt = sb("wdt", [P, KB, NH])
            rows = sb("dt_rows", [P, 2 * NH + 2])
            v = {n: sb("sp_" + n, [P, W]) for n in ("x", "n", "u", "w", "l", "d", "m", "t")}
            dtA, acum, dte = sb("dtA", [P, W]), sb("acum", [P, NC]), sb("dte", [P, NC])
            arow = sb("arow", [P, NH + 1])
            diag = sb("dt_diag", [NH, 2, NS, NH])
            eA = sb("smp_eA", [P, NS])
            in_sem, x_in, made, dord, pord = (self.sem("t_" + n) for n in ("in", "x_in", "made", "dve", "pool"))
            proj_done, sums_done, spread_done = (self.sem("t_" + n) for n in ("proj", "sums", "spread"))
            rate_ready, u_ready, ln_ready, decay_ready = (self.sem("t_" + n) for n in ("rate", "u", "ln", "decay"))
            neg_ready, w_ready, dtA_ready, gap_ready, diag_ready = (
                self.sem("t_" + n) for n in ("neg", "w", "dtA", "gap", "diag"))
            dtp, sps, ac, bcs = self.bank[0], self.bank[1], self.bank[2], self.bank[3:5]

            with nc.Block() as block:
                @block.sync
                def _(sp):
                    sp.dma_start(xT[:], a["xT"]).then_inc(x_in, 16)
                    sp.dma_start(wdt[:], a["w_dt"]).then_inc(x_in, 16)
                    sp.dma_start(rows[:], a["dt_rows"]).then_inc(in_sem, 16)
                    sp.dma_start(self.lnp[:], a["ln_cols"]).then_inc(in_sem, 16)
                    sp.wait_ge(in_sem, 32)

                @block.gpsimd
                def _(pool):
                    o = Order(pool, pord)
                    pool.memset(self.ident[:], 0.0)
                    pool.memset(self.ones[:], 1.0)
                    pool.memset(self.onesD[:], 1.0 / D)
                    pool.memset(self.onesG[:], 1.0 / (GT * P))
                    o(pool.memset(self.eps[:], EPS))
                    pool.affine_select(out=self.ident[:], in_=self.ident[:], compare_op=ALU.not_equal,
                                       fill=1.0, base=0, pattern=[[1, P]], channel_multiplier=-1)
                    pool.affine_select(out=self.triu[:], in_=self.ones[:], compare_op=ALU.is_ge,
                                       fill=0.0, base=0, pattern=[[1, P]],
                                       channel_multiplier=-1).then_inc(made, 1)

                @block.tensor
                def _(pe):
                    pe.wait_ge(x_in, 32)
                    for c in range(CH):
                        for k in range(KB):
                            pe.matmul(dtp[:, c * NH:(c + 1) * NH], xT[:, k, c * P:(c + 1) * P],
                                      wdt[:, k, :], start=(k == 0), stop=(k == KB - 1))
                    for k in range(KB):
                        last = pe.matmul(sps[0:NH, 0:NS], wdt[:, k, :], xT[:, k, TP:T],
                                         start=(k == 0), stop=(k == KB - 1))
                    last.then_inc(proj_done, 1)
                    pe.wait_ge(made, 1)
                    pe.wait_ge(dtA_ready, 1)
                    pe.matmul(ac[:, 0:NC], self.triu[:], dtA[:, 0:NC], start=True, stop=True)
                    pe.matmul(ac[:, NC:2 * NC], self.ones[:], dtA[:, 0:NC],
                              start=True, stop=True).then_inc(sums_done, 1)
                    pe.wait_ge(diag_ready, 1)
                    for s in range(2):
                        last = pe.matmul(bcs[s][:, 0:NS * NH], self.ones[0:NH, :],
                                         diag[:, s].rearrange("p b h -> p (b h)"), start=True, stop=True)
                    last.then_inc(spread_done, 1)

                @block.scalar
                def _(act):
                    act.wait_ge(in_sem, 32)
                    act.activation(arow[:, 0:NH], rows[:, NH:2 * NH], ACT.Exp)
                    act.activation(arow[:, NH:NH + 1], rows[:, 2 * NH + 1:2 * NH + 2],
                                   ACT.Exp).then_inc(rate_ready, 1)
                    act.wait_ge(neg_ready, 1)
                    act.activation(v["u"][:], v["n"][:], ACT.Exp).then_inc(u_ready, 1)
                    act.wait_ge(w_ready, 1)
                    act.activation(v["l"][:], v["w"][:], ACT.Ln).then_inc(ln_ready, 1)
                    act.wait_ge(gap_ready, 1)
                    act.activation(dte[:], acum[:], ACT.Exp)
                    act.activation(eA[0:NH, :], dtA[0:NH, NC:W], ACT.Exp).then_inc(decay_ready, 1)

                @block.vector
                def _(dve):
                    o = Order(dve, dord)
                    x = v["x"]
                    o(dve.memset(x[:], 0.0))
                    dve.wait_ge(proj_done, 1)
                    dve.wait_ge(in_sem, 32)
                    dve.tensor_tensor(x[:, 0:NC].rearrange("p (c h) -> p c h", c=CH),
                                      dtp[:, 0:NC].rearrange("p (c h) -> p c h", c=CH),
                                      mid(rows[:, 0:NH], 1, CH), ALU.add)
                    o(dve.tensor_scalar(x[0:NH, NC:W], sps[0:NH, 0:NS], rows[0:NH, 2 * NH:2 * NH + 1],
                                        None, ALU.add))
                    dve.scalar_tensor_tensor(out=v["n"][:], in0=x[:], scalar=-1.0, in1=x[:],
                                             op0=ALU.mult, op1=ALU.min).then_inc(neg_ready, 1)
                    dve.wait_ge(u_ready, 1)
                    dve.tensor_scalar(v["w"][:], v["u"][:], 1.0, None, ALU.add).then_inc(w_ready, 1)
                    dve.wait_ge(w_ready, 1)
                    o(dve.tensor_scalar(v["d"][:], v["w"][:], -1.0, None, ALU.add))
                    o(dve.tensor_scalar(v["m"][:], v["d"][:], 0.0, None, ALU.is_equal))
                    dve.wait_ge(ln_ready, 1)
                    dve.tensor_tensor(v["l"][:], v["l"][:], v["m"][:], ALU.add)
                    o(dve.tensor_tensor(v["d"][:], v["d"][:], v["m"][:], ALU.add))
                    o(dve.reciprocal(v["t"][:], v["d"][:]))
                    o(dve.tensor_tensor(v["l"][:], v["l"][:], v["t"][:], ALU.mult))
                    o(dve.tensor_tensor(v["l"][:], v["l"][:], v["u"][:], ALU.mult))
                    dt = v["t"]
                    o(dve.scalar_tensor_tensor(out=dt[:], in0=x[:], scalar=0.0, in1=v["l"][:],
                                               op0=ALU.max, op1=ALU.add))
                    dve.wait_ge(rate_ready, 1)
                    o(dve.tensor_scalar(v["w"][:, 0:NH + 1], arow[:], -1.0, None, ALU.mult))
                    dve.tensor_scalar(dtA[0:NH, NC:W], dt[0:NH, NC:W], v["w"][0:NH, NH:NH + 1],
                                      None, ALU.mult)
                    dve.tensor_tensor(dtA[:, 0:NC].rearrange("p (c h) -> p c h", c=CH),
                                      dt[:, 0:NC].rearrange("p (c h) -> p c h", c=CH),
                                      mid(v["w"][:, 0:NH], 1, CH), ALU.mult).then_inc(dtA_ready, 1)
                    dve.wait_ge(sums_done, 1)
                    dve.wait_ge(dtA_ready, 1)
                    o(dve.tensor_copy(v["n"][:, 0:NC], ac[:, 0:NC]))
                    dve.tensor_tensor(acum[:], ac[:, NC:2 * NC], v["n"][:, 0:NC],
                                      ALU.subtract).then_inc(gap_ready, 1)
                    dve.wait_ge(decay_ready, 1)
                    o(dve.tensor_tensor(dte[:], dte[:], dt[:, 0:NC], ALU.mult))
                    for kind, src in enumerate((dt, dte, v["n"], dtA)):
                        for c in range(CH):
                            dve.tensor_copy(tab[:, :, kind, c, :],
                                            src[:, c * NH:(c + 1) * NH].rearrange("p (g h) -> p g h", g=G))
                    for s, src in enumerate((dt[0:NH, NC:W], eA[0:NH, :])):
                        last = dve.tensor_tensor(diag[:, s], mid(self.ident[0:NH, 0:NH], 1, NS),
                                                 bc(src, NH), ALU.mult)
                    last.then_inc(diag_ready, 1)
                    dve.wait_ge(spread_done, 1)
                    for s in range(2):
                        src = bcs[s][:, 0:NS * NH].rearrange("p (b g t w) -> p g t w b", b=NS, g=G, w=2)
                        for g in range(G):
                            for w in range(2):
                                last = dve.tensor_copy(stab[w * HD:(w + 1) * HD, g, s],
                                                       src[w * HD:(w + 1) * HD, g, :, w, :])
                    o(last)
        return tab, stab

    def ssd(self, st, xT, yA, tabs):
        nc, a, out = self.nc, self.a, self.o
        tab, stab = tabs
        R = 5
        NT = CT + GT
        HB = NS // 2
        NU = GT * 2
        sb = lambda name, shape, dt=F32: st.enter_context(nc.sbuf_tensor(name, shape, dt))
        ring = sb("w_ring_ssd", [P, R, WCOLS])
        raw = sb("raw", [P, 2, TP + 3])
        acc = sb("conv_acc", [P, 2, TP + NS])
        scv = sb("smp_conv", [P, 4, CT, NS])
        gpar = sb("g_par", [P, GP_N])
        cpo = sb("conv_pr_out", [P, CT, 3])
        sprod = sb("smp_prod", [P, 4, NS])
        bT, cT, xg = sb("bT", [P, T]), sb("cT", [P, T]), sb("xg", [P, GT, T])
        gt, gs = sb("g_tab", [P, 4, CH, HG]), sb("g_smp", [P, 2, GT, NS])
        xdt, xde = sb("xdt", [P, HG, HD]), sb("x_dt_decay", [P, HG, HD])
        btok, cbm = sb("b_tok", [P, P]), sb("cb_masked", [P, P])
        tri = sb("tri_rhs", [P, HG, P])
        L, eA = sb("L", [P, HG, P]), sb("eA", [P, HG, P])
        cdec = sb("chunk_decay", [P, HG])
        S = sb("state", [P, HG, HD])
        sst = sb("smp_state", [P, 2, HB, NST])
        stmp = sb("smp_tmp", [P, HB, NST])
        Bb, Cb = sb("B_bcast", [P, NS, NST]), sb("C_bcast", [P, NS, NST])
        ys = sb("smp_y", [P, GT, NS])
        gb, tpb, bcb, ab, yb, stb = (self.bank[0:2], self.bank[2], self.bank[3], self.bank[4:6],
                                     self.bank[6], self.bank[7])
        landed = [self.sem(f"s_w{j}") for j in range(R)]
        S_ = lambda *names: [self.sem("s_" + n) for n in names]
        gemm_ready, gemm_free, raw_ready, conv_done, silu_done = S_(
            "gemm_ready", "gemm_free", "raw_ready", "conv_done", "silu_done")
        par_in, conv_in, conv_out = S_("par_in", "conv_in", "conv_out")
        diag_ready, spread_done, spread_read = S_("diag_ready", "spread_done", "spread_read")
        tri_ready, a_done, seg_done, exp_done, m_ready, b_done, y_done = S_(
            "tri_ready", "a_done", "seg_done", "exp_done", "m_ready", "b_done", "y_done")
        gated, squared, rms_done, root_ready, group_done = S_(
            "gated", "squared", "rms_done", "root_ready", "group_done")
        tabs_ready, prod_ready, prod_read, fin_ready, fin_out = S_(
            "tabs_ready", "prod_ready", "prod_read", "fin_ready", "fin_out")
        st_in = [self.sem(f"s_st_in{j}") for j in range(2)]
        st_out = [self.sem(f"s_st_out{j}") for j in range(2)]
        dord, pord = S_("dve", "pool")
        state_in = a["state_ssm"].rearrange("b (t w) p n -> t (w p) b n", w=2)
        state_out = out["ssm_sample"].rearrange("b (t w) p n -> t (w p) b n", w=2)

        with nc.Block() as block:
            @block.sync
            def _(sp):
                self.stream(sp, ring, landed, 0, N_SSD, lambda i, j: (gemm_ready, 2 * (R * i + j) + 2))

            @block.tensor
            def _(pe):
                with pe.Fori(0, G) as g:
                    def project(t):
                        j = t % R
                        self.gemm(pe, gb, gemm_free, 2 * NT * g + 2 * t + 1, gemm_ready,
                                  [(ring[:, j, :], landed[j], 32 * g + 16 * (t // R) + 16, xT)])

                    def spread(n):
                        pe.wait_ge(diag_ready, 2 * g + n + 1)
                        pe.wait_ge(spread_read, 2 * g + n)
                        for h in range(2):
                            last = pe.matmul(ab[h][:], self.ones[:],
                                             tri[:, 4 * h:4 * h + 4, :].rearrange("p a b -> p (a b)"),
                                             start=True, stop=True)
                        last.then_inc(spread_done, 1)

                    def chunk_a(q):
                        s = slice(q * P, (q + 1) * P)
                        pe.wait_ge(silu_done, CT * g + CT + 2)
                        pe.wait_ge(tri_ready, CH * g + q + 1)
                        if q == 0:
                            pe.wait_ge(spread_read, 2 * g + 2)
                        for t in range(GT):
                            pe.transpose(tpb[:, t * P:(t + 1) * P], xg[:, t, s], self.ident[:])
                        pe.transpose(bcb[:, 0:P], bT[:, s], self.ident[:])
                        pe.matmul(bcb[:, P:2 * P], bT[:, s], cT[:, s], start=True, stop=True)
                        for h in range(2):
                            last = pe.matmul(ab[h][:], self.ones[:],
                                             tri[:, 4 * h:4 * h + 4, :].rearrange("p a b -> p (a b)"),
                                             start=True, stop=True)
                        last.then_inc(a_done, 1)

                    def chunk_b(q):
                        pe.wait_ge(m_ready, CH * g + q + 1)
                        pe.wait_ge(y_done, CH * g + q)
                        for t in range(GT):
                            for w in range(2):
                                h = 2 * t + w
                                o = yb[w * HD:(w + 1) * HD, t * P:(t + 1) * P]
                                pe.matmul(o, xdt[:, h, :], L[:, h, :], start=True, stop=False)
                                pe.matmul(o, S[:, h, :], eA[:, h, :], start=False, stop=True)
                        pe.matmul(stb[:], btok[:], xde[:].rearrange("p a b -> p (a b)"),
                                  start=True, stop=True).then_inc(b_done, 1)

                    for t in range(4):
                        project(t)
                        if t >= 2:
                            spread(t - 2)
                    project(4)
                    project(5)
                    for q in range(CH):
                        chunk_a(q)
                        project(CT + q)
                        chunk_b(q)
                    for t in range(GT):
                        pe.wait_ge(squared, GT * g + t + 1)
                        for h in range(2):
                            last = pe.matmul(ab[h][:, 0:H2], self.onesG[:], xg[:, t, h * H2:(h + 1) * H2],
                                             start=(t == 0), stop=(t == GT - 1))
                    last.then_inc(rms_done, 1)

            @block.scalar
            def _(act):
                act.sem_inc(gemm_free, 2)
                act.sem_inc(silu_done, 2)
                with act.Fori(0, G) as g:
                    def evac(t):
                        r = raw[:, t % 2, :]
                        act.wait_ge(conv_done, CT * g + t + 1)
                        act.wait_ge(gemm_ready, 2 * NT * g + 2 * t + 1)
                        act.copy(r[:, 3:3 + H2], gb[0][:, 0:H2]).then_inc(gemm_free, 1)
                        act.wait_ge(gemm_ready, 2 * NT * g + 2 * t + 2)
                        act.copy(r[:, 3 + H2:3 + TP], gb[1][:, 0:TP - H2]).then_inc(raw_ready, 1)
                        act.copy(scv[:, 3, t, :], gb[1][:, TP - H2:H2]).then_inc(gemm_free, 1)

                    def silu(t):
                        dst = (bT[:], cT[:])[t] if t < 2 else xg[:, t - 2, :]
                        act.wait_ge(conv_done, CT * g + t + 3)
                        act.wait_ge(par_in, 16 * g + 16)
                        if t == 0:
                            act.wait_ge(group_done, g)
                        act.activation(dst, acc[:, t % 2, :], ACT.Silu,
                                       bias=gpar[:, GP_B + t:GP_B + t + 1]).then_inc(silu_done, 1)

                    def spread_out(n):
                        act.wait_ge(spread_done, 2 * g + n + 1)
                        for h in range(2):
                            last = act.copy((Bb, Cb)[n][:, 4 * h:4 * h + 4, :].rearrange("p a b -> p (a b)"),
                                            ab[h][:])
                        last.then_inc(spread_read, 1)

                    act.wait_ge(conv_out, 32 * g)
                    evac(0)
                    for t in range(1, CT):
                        if t in (3, 4):
                            spread_out(t - 3)
                        evac(t)
                        silu(t - 1)
                    silu(CT - 1)
                    for q in range(CH):
                        act.wait_ge(m_ready, CH * g + q)
                        act.wait_ge(seg_done, CH * g + q + 1)
                        for h in range(2):
                            act.activation(eA[:, 4 * h:4 * h + 4, :].rearrange("p a b -> p (a b)"),
                                           ab[h][:], ACT.Exp)
                        act.activation(L[:], L[:], ACT.Exp).then_inc(exp_done, 1)
                        t = CT + q
                        for h in range(2):
                            act.wait_ge(gemm_ready, 2 * NT * g + 2 * t + 1 + h)
                            self.alone(act)
                            act.activation(yA[:, GT * g + q, h * H2:(h + 1) * H2], gb[h][:, 0:H2],
                                           ACT.Silu).then_inc(gemm_free, 1)
                    for t in range(GT):
                        act.wait_ge(gated, GT * g + t + 1)
                        self.alone(act)
                        act.activation(xg[:, t, :], yA[:, GT * g + t, :], ACT.Square).then_inc(squared, 1)
                    act.wait_ge(rms_done, g + 1)
                    for h in range(2):
                        last = act.activation(acc[:, 0, h * H2:(h + 1) * H2], ab[h][:, 0:H2], ACT.Sqrt,
                                              bias=self.eps[:])
                    last.then_inc(root_ready, 1)

            @block.vector
            def _(dve):
                o = Order(dve, dord)
                dve.memset(raw[:, 0, 0:3], 0.0)
                o(dve.memset(raw[:, 1, 0:3], 0.0))
                dve.sem_inc(conv_done, 2)
                with dve.Fori(0, G) as g, o.body(g, G, SSD_DVE):
                    def conv(t):
                        r, ac = raw[:, t % 2, :], acc[:, t % 2, 0:TP]
                        w = gpar[:, 4 * t:4 * t + 4]
                        dve.wait_ge(raw_ready, CT * g + t + 1)
                        dve.wait_ge(gemm_free, 2 * NT * g + 2 * t + 4)
                        dve.wait_ge(silu_done, CT * g + t + 1)
                        o(dve.tensor_scalar(ac, r[:, 0:TP], w[:, 0:1], None, ALU.mult))
                        for k in range(1, 4):
                            ins = dve.scalar_tensor_tensor(out=ac, in0=r[:, k:k + TP], scalar=w[:, k:k + 1],
                                                           in1=ac, op0=ALU.mult, op1=ALU.add)
                            if k < 3:
                                o(ins)
                        dve.tensor_copy(cpo[:, t, :], r[:, TP:TP + 3])
                        o(dve.tensor_tensor(sprod[:], scv[:, :, t, :], bc(w, NS), ALU.mult))
                        dve.tensor_reduce(acc[:, t % 2, TP:T], sprod[:].rearrange("p r b -> p b r"), AX_X, ALU.add).then_inc(conv_done, 1)
                        dve.wait_ge(conv_done, CT * g + t + 3)

                    def diagonal(n):
                        dve.wait_ge(silu_done, CT * g + n + 3)
                        if n:
                            dve.wait_ge(spread_done, 2 * g + n)
                        dve.tensor_tensor(tri[:], mid(self.ident[:], 1, NS), bc((bT, cT)[n][:, TP:T], P),
                                          ALU.mult).then_inc(diag_ready, 1)

                    def tri_rhs(q):
                        dve.tensor_tensor(tri[:], mid(self.triu[:], 1, HG), bc(gt[:, 3, q, :], P),
                                          ALU.mult).then_inc(tri_ready, 1)

                    def sum_smp(u):
                        dve.wait_ge(prod_ready, NU * g + u + 1)
                        dve.tensor_reduce(ys[:, u // 2, HB * (u % 2):HB * (u % 2) + HB], stmp[:], AX_X,
                                          ALU.add).then_inc(prod_read, 1)

                    dve.wait_ge(par_in, 16 * g + 16)
                    dve.tensor_copy(gs[:], stab[:, g])
                    dve.tensor_copy(gt[:], tab[:, g]).then_inc(tabs_ready, 1)
                    dve.wait_ge(tabs_ready, g + 1)
                    dve.wait_ge(fin_out, 16 * g)
                    dve.wait_ge(conv_out, 32 * g)
                    o(dve.memset(S[:], 0.0))
                    for t in range(CT):
                        if t == 0:
                            dve.wait_ge(conv_in, 16 * g + 16)
                        conv(t)
                        if t in (1, 2):
                            diagonal(t - 1)
                    dve.wait_ge(spread_done, 2 * g + 2)
                    tri_rhs(0)
                    for q in range(CH):
                        s = slice(q * P, (q + 1) * P)
                        dve.wait_ge(a_done, CH * g + q + 1)
                        xt = tpb[:].rearrange("p (h d) -> p h d", h=HG)
                        dve.tensor_tensor(xdt[:], xt, bc(gt[:, 0, q, :], HD), ALU.mult)
                        dve.tensor_tensor(xde[:], xt, bc(gt[:, 1, q, :], HD), ALU.mult)
                        dve.tensor_copy(btok[:], bcb[:, 0:P])
                        dve.tensor_tensor(cbm[:], bcb[:, P:2 * P], self.triu[:], ALU.mult)
                        for h in range(HG):
                            last = dve.tensor_scalar(L[:, h, :], ab[h // 4][:, (h % 4) * P:(h % 4 + 1) * P],
                                                     gt[:, 2, q, h:h + 1], 0.0, ALU.subtract, ALU.min)
                        last.then_inc(seg_done, 1)
                        if q < CH - 1:
                            tri_rhs(q + 1)
                        sum_smp(2 * q)
                        dve.wait_ge(exp_done, CH * g + q + 1)
                        o(dve.tensor_copy(cdec[:], eA[:, :, P - 1]))
                        dve.tensor_tensor(L[:], L[:], mid(cbm[:], 1, HG), ALU.mult)
                        dve.tensor_tensor(eA[:], eA[:], mid(cT[:, s], 1, HG), ALU.mult).then_inc(m_ready, 1)
                        dve.wait_ge(b_done, CH * g + q + 1)
                        o(dve.tensor_tensor(S[:], S[:], bc(cdec[:], HD), ALU.mult))
                        dve.tensor_tensor(S[:], S[:], stb[:].rearrange("p (h d) -> p h d", h=HG), ALU.add)
                        for t in range(GT):
                            last = dve.scalar_tensor_tensor(out=xg[:, t, s], in0=xg[:, t, s],
                                                            scalar=gpar[:, GP_D + t:GP_D + t + 1],
                                                            in1=yb[:, t * P:(t + 1) * P],
                                                            op0=ALU.mult, op1=ALU.add)
                        last.then_inc(y_done, 1)
                        dve.wait_ge(y_done, CH * g + q + 1)
                        sum_smp(2 * q + 1)
                    dve.wait_ge(prod_read, NU * g + NU)
                    for t in range(GT):
                        last = dve.scalar_tensor_tensor(out=xg[:, t, TP:T], in0=xg[:, t, TP:T],
                                                        scalar=gpar[:, GP_D + t:GP_D + t + 1],
                                                        in1=ys[:, t, :], op0=ALU.mult, op1=ALU.add)
                    last.then_inc(fin_ready, 1)
                    dve.wait_ge(fin_ready, g + 1)
                    for t in range(GT):
                        dve.wait_ge(gemm_free, 2 * NT * g + 2 * (CT + t) + 4)
                        dve.tensor_tensor(yA[:, GT * g + t, :], yA[:, GT * g + t, :], xg[:, t, :],
                                          ALU.mult).then_inc(gated, 1)
                    dve.wait_ge(root_ready, g + 1)
                    o(dve.reciprocal(acc[:, 0, :], acc[:, 0, :]))
                    for t in range(GT):
                        last = dve.scalar_tensor_tensor(out=yA[:, GT * g + t, :], in0=yA[:, GT * g + t, :],
                                                        scalar=gpar[:, GP_NW + t:GP_NW + t + 1],
                                                        in1=acc[:, 0, :], op0=ALU.mult, op1=ALU.mult)
                    last.then_inc(group_done, 1)
                    dve.wait_ge(group_done, g + 1)

            @block.gpsimd
            def _(pool):
                o = Order(pool, pord)
                with pool.Fori(0, G) as g, o.body(g, G, SSD_POOL):
                    def load(u):
                        if u >= 2:
                            pool.wait_ge(st_out[u % 2], 64 * g + 16 * (u // 2))
                        else:
                            pool.wait_ge(st_out[u % 2], 64 * g)
                        self.alone(pool)
                        pool.dma_start(sst[:, u % 2], state_in[GT * g + u // 2, :, HB * (u % 2):HB * (u % 2) + HB, :]
                                       ).then_inc(st_in[u % 2], 16)

                    pool.wait_ge(group_done, g)
                    pool.wait_ge(conv_out, 32 * g)
                    self.alone(pool)
                    pool.dma_start(gpar[:], a["g_par"][g]).then_inc(par_in, 16)
                    pool.dma_start(scv[:, 0:3], a["state_conv"][g]).then_inc(conv_in, 16)
                    load(0)
                    pool.wait_ge(tabs_ready, g + 1)
                    for u in range(NU):
                        t, b0 = u // 2, HB * (u % 2)
                        s = sst[:, u % 2]
                        if u < NU - 1:
                            load(u + 1)
                        if u == 4:
                            pool.wait_ge(conv_done, CT * g + CT + 2)
                            self.alone(pool)
                            pool.dma_start(out["conv_sample"][g], scv[:, 1:4]).then_inc(conv_out, 16)
                            pool.dma_start(out["conv_prompt"][g], cpo[:]).then_inc(conv_out, 16)
                        if u == 0:
                            pool.wait_ge(spread_read, 2 * g + 2)
                        if u % 2 == 0:
                            pool.wait_ge(silu_done, CT * g + t + 5)
                        pool.wait_ge(st_in[u % 2], 64 * g + 16 * (u // 2) + 16)
                        if u % 2 == 0:
                            o(pool.tensor_tensor(gs[:, 0, t, :], gs[:, 0, t, :], xg[:, t, TP:T], ALU.mult))
                        pool.tensor_tensor(s, s, bc(gs[:, 1, t, b0:b0 + HB], NST), ALU.mult)
                        pool.wait_ge(prod_read, NU * g + u)
                        o(pool.tensor_tensor(stmp[:], Bb[:, b0:b0 + HB, :], bc(gs[:, 0, t, b0:b0 + HB], NST),
                                             ALU.mult))
                        o(pool.tensor_tensor(s, s, stmp[:], ALU.add))
                        self.alone(pool)
                        pool.dma_start(state_out[GT * g + t, :, b0:b0 + HB, :], s).then_inc(st_out[u % 2], 16)
                        pool.tensor_tensor(stmp[:], s, Cb[:, b0:b0 + HB, :], ALU.mult).then_inc(prod_ready, 1)
                        pool.wait_ge(prod_ready, NU * g + u + 1)
                    pool.wait_ge(fin_ready, g + 1)
                    self.alone(pool)
                    pool.dma_start(out["ssm_prompt"][g], S[:].rearrange("p h d -> p (h d)")).then_inc(fin_out, 16)
                pool.wait_ge(fin_out, 16 * G)
                pool.wait_ge(conv_out, 32 * G)
                for j in range(2):
                    pool.wait_ge(st_out[j], 64 * G)

    def ln_pe(self, pe, v, square, s):
        mu, var = self.bank[2:4], self.bank[4:6]
        for n in range(FT):
            pe.wait_ge(s["in"], n + 1)
            for h in range(2):
                last = pe.matmul(mu[h][:, 0:H2], self.onesD[:], v[:, n, h * H2:(h + 1) * H2],
                                 start=(n == 0), stop=(n == FT - 1))
        last.then_inc(s["mean"], 1)
        for n in range(FT):
            pe.wait_ge(s["square"], n + 1)
            for h in range(2):
                last = pe.matmul(var[h][:, 0:H2], self.onesD[:], square(n)[:, h * H2:(h + 1) * H2],
                                 start=(n == 0), stop=(n == FT - 1))
        last.then_inc(s["var"], 1)

    def ln_act(self, act, v, square, root, s):
        for n in range(FT):
            act.wait_ge(s["centred"], n + 1)
            act.activation(square(n), v[:, n, :], ACT.Square).then_inc(s["square"], 1)
        act.wait_ge(s["var"], 1)
        for h in range(2):
            last = act.activation(root[:, h * H2:(h + 1) * H2], self.bank[4 + h][:, 0:H2], ACT.Sqrt,
                                  bias=self.eps[:])
        last.then_inc(s["root"], 1)

    def ln_dve(self, dve, v, root, g, b, s):
        mu = self.bank[2:4]
        dve.wait_ge(s["mean"], 1)
        for n in range(FT):
            for h in range(2):
                last = dve.tensor_tensor(v[:, n, h * H2:(h + 1) * H2], v[:, n, h * H2:(h + 1) * H2],
                                         mu[h][:, 0:H2], ALU.subtract)
            last.then_inc(s["centred"], 1)
        dve.wait_ge(s["root"], 1)
        dve.reciprocal(root[:], root[:]).then_inc(s["inv"], 1)
        dve.wait_ge(s["inv"], 1)
        for n in range(FT):
            dve.tensor_tensor(v[:, n, :], v[:, n, :], root[:], ALU.mult).then_inc(s["inv"], 1)
            dve.wait_ge(s["inv"], n + 2)
            dve.tensor_scalar(v[:, n, :], v[:, n, :], g[:, n:n + 1], b[:, n:n + 1],
                              ALU.mult, ALU.add).then_inc(s["normed"], 1)

    def ln_sems(self, name):
        return {n: self.sem(f"{name}_{n}") for n in ("in", "mean", "square", "var", "centred", "root", "inv", "normed")}

    def sgu(self, xT, v, yB):
        nc, a, out = self.nc, self.a, self.o
        R = 4
        LOOP = FT // R
        with ExitStack() as st:
            sb = lambda name, shape, dt=F32: st.enter_context(nc.sbuf_tensor(name, shape, dt))
            ring = sb("w_ring_sgu", [P, R, WCOLS])
            root = sb("v_root", [P, T])
            vst = sb("v_staged", [P, TP])
            vtok = sb("v_tok", [P, CH, P])
            ws = sb("w_spatial", [P, 2, P])
            bs = sb("b_spatial", [P, 2, P])
            w0 = sb("w_spatial0", [P, 2, FT])
            S_ = lambda *names: [self.sem("g_" + n) for n in names]
            landed = [self.sem(f"g_w{j}") for j in range(R)]
            gemm_ready, gemm_free, w0_in, v_out, masked, staged, turned, tok_ready, mixed, mix_free, gate_done = S_(
                "gemm_ready", "gemm_free", "w0_in", "v_out", "masked", "staged", "turned", "tok_ready", "mixed",
                "mix_free", "gate_done")
            ws_in = [self.sem(f"g_ws{j}") for j in range(2)]
            dord, = S_("dve")
            ln = self.ln_sems("vln")
            gb, tb, mb = self.bank[0:2], self.bank[6], self.bank[7]
            square = lambda n: yB[:, n, :]
            with nc.Block() as block:
                @block.sync
                def _(sp):
                    sp.dma_start(w0[:], a["sgu_first"]).then_inc(w0_in, 16)
                    self.stream(sp, ring, landed, O_V, N_V + N_U, lambda i, j: (gemm_ready, 2 * (R * i + j) + 2))

                @block.gpsimd
                def _(pool):
                    with pool.Fori(0, FT // 2) as i:
                        for j in range(2):
                            pool.wait_ge(gate_done, 2 * i + j)
                            self.alone(pool)
                            pool.dma_start(ws[:, j, :], a["sgu_wT"][2 * i + j]).then_inc(ws_in[j], 16)
                            pool.dma_start(bs[:, j, :], a["sgu_b"][2 * i + j]).then_inc(ws_in[j], 16)
                    pool.wait_ge(ln["normed"], FT)
                    pool.dma_start(out["v_last"], v[:, :, TP - P:T]).then_inc(v_out, 16)
                    pool.wait_ge(v_out, 16)

                @block.tensor
                def _(pe):
                    with pe.Fori(0, LOOP) as i:
                        for j in range(R):
                            self.gemm(pe, gb, gemm_free, 2 * (R * i + j) + 1, gemm_ready,
                                      [(ring[:, j, :], landed[j], 16 * i + 16, xT)])
                    self.ln_pe(pe, v, square, ln)
                    with pe.Fori(0, LOOP) as i:
                        for j in range(R):
                            n = R * i + j
                            self.gemm(pe, gb, gemm_free, 2 * n + 2 * FT + 1, gemm_ready,
                                      [(ring[:, j, :], landed[j], 16 * i + 16 * LOOP + 16, xT)])
                            pe.wait_ge(staged, n + 1)
                            pe.wait_ge(tok_ready, n)
                            for c in range(CH):
                                last = pe.transpose(tb[:, c * P:(c + 1) * P], vst[:, c * P:(c + 1) * P],
                                                    self.ident[:])
                            last.then_inc(turned, 1)
                            pe.wait_ge(tok_ready, n + 1)
                            pe.wait_ge(masked, n + 1)
                            pe.wait_ge(mix_free, n)
                            for c in range(CH):
                                last = pe.matmul(mb[:, c * P:(c + 1) * P], vtok[:, c, :], ws[:, j % 2, :],
                                                 start=True, stop=True)
                            last.then_inc(mixed, 1)

                @block.scalar
                def _(act):
                    act.sem_inc(gemm_free, 2)
                    with act.Fori(0, FT) as n:
                        for h in range(2):
                            act.wait_ge(gemm_ready, 2 * n + 1 + h)
                            self.alone(act)
                            act.activation(v[:, n, h * H2:(h + 1) * H2], gb[h][:, 0:H2],
                                           ACT.Gelu).then_inc(gemm_free, 1)
                        act.wait_ge(gemm_free, 2 * n + 4)
                        act.sem_inc(ln["in"], 1)
                    self.ln_act(act, v, square, root, ln)
                    with act.Fori(0, FT) as n:
                        for h in range(2):
                            act.wait_ge(gemm_ready, 2 * FT + 2 * n + 1 + h)
                            if h == 0:
                                act.wait_ge(ln["var"], 1)
                            self.alone(act)
                            act.activation(yB[:, n, h * H2:(h + 1) * H2], gb[h][:, 0:H2],
                                           ACT.Gelu).then_inc(gemm_free, 1)
                        act.wait_ge(turned, n + 1)
                        act.wait_ge(mixed, n)
                        act.copy(vtok[:].rearrange("p c d -> p (c d)"), tb[:]).then_inc(tok_ready, 1)

                @block.vector
                def _(dve):
                    self.ln_dve(dve, v, root, self.lnp[:, 0, :], self.lnp[:, 1, :], ln)
                    o = Order(dve, dord)
                    dve.wait_ge(w0_in, 16)
                    dve.wait_ge(ln["normed"], FT)
                    with dve.Fori(0, FT // 2) as i, o.body(i, FT // 2, 2):
                        for j in range(2):
                            n = 2 * i + j
                            dve.wait_ge(turned, n)
                            dve.tensor_copy(vst[:], v[:, n, 0:TP]).then_inc(staged, 1)
                            dve.wait_ge(ws_in[j], 32 * i + 32)
                            dve.tensor_tensor(ws[:, j, :], ws[:, j, :], self.triu[:], ALU.mult).then_inc(masked, 1)
                            o(dve.tensor_tensor(root[:, TP:T], v[:, n, TP:T],
                                                w0[:, 0, bass.ds(n, 1)].to_broadcast([P, NS]), ALU.mult))
                            dve.tensor_tensor(root[:, TP:T], root[:, TP:T],
                                              w0[:, 1, bass.ds(n, 1)].to_broadcast([P, NS]), ALU.add)
                            dve.wait_ge(mixed, n + 1)
                            dve.tensor_tensor(root[:, 0:TP].rearrange("p (c i) -> p c i", c=CH),
                                              mb.rearrange("p (c i) -> p c i", c=CH),
                                              mid(bs[:, j, :], 1, CH), ALU.add).then_inc(mix_free, 1)
                            dve.wait_ge(mix_free, n + 1)
                            dve.wait_ge(gemm_free, 2 * n + 2 * FT + 4)
                            dve.tensor_tensor(yB[:, n, :], yB[:, n, :], root[:], ALU.mult).then_inc(gate_done, 1)
                            dve.wait_ge(gate_done, n + 1)

    def merge_b(self, xT, yB, merged):
        self.merge(xT, merged, "b", O_BB, 2, [yB], add=False)

    def merge_a(self, xT, yA, merged):
        self.merge(xT, merged, "a", O_BA, 3, [yA[:, 0:KB, :], yA[:, KB:2 * KB, :]], add=True)

    def merge(self, xT, merged, name, first, per, acts, add):
        nc = self.nc
        R = 2 * per
        UN = 2
        with ExitStack() as st:
            sb = lambda name_, shape: st.enter_context(nc.sbuf_tensor(name_, shape, F32))
            ring = sb("w_ring_" + name, [P, R, WCOLS])
            gate = sb("gate_" + name, [P, 2, H2])
            S_ = lambda *names: [self.sem(f"m{name}_" + n) for n in names]
            landed = [self.sem(f"m{name}_w{j}") for j in range(R)]
            gate_ready, gate_free, prod_ready, prod_free, sig_ready, mul_done = S_(
                "gate_ready", "gate_free", "prod_ready", "prod_free", "sig_ready", "mul_done")
            gg, gp = self.bank[0:2], self.bank[2:4]
            with nc.Block() as block:
                @block.sync
                def _(sp):
                    self.stream(sp, ring, landed, first, per * FT,
                                lambda i, j: (prod_ready if j % per else gate_ready, 2 * (UN * i + j // per) + 2))

                @block.tensor
                def _(pe):
                    with pe.Fori(0, FT // UN) as i:
                        for u in range(UN):
                            n, j = UN * i + u, per * u
                            self.gemm(pe, gg, gate_free, 2 * n + 1, gate_ready,
                                      [(ring[:, j, :], landed[j], 16 * i + 16, xT)])
                            self.gemm(pe, gp, prod_free, 2 * n + 1, prod_ready,
                                      [(ring[:, j + 1 + m, :], landed[j + 1 + m], 16 * i + 16, y)
                                       for m, y in enumerate(acts)])

                @block.scalar
                def _(act):
                    act.sem_inc(gate_free, 2)
                    with act.Fori(0, FT) as n:
                        for h in range(2):
                            act.wait_ge(gate_ready, 2 * n + 1 + h)
                            act.wait_ge(mul_done, 2 * n + h + 1)
                            act.activation(gate[:, h, :], gg[h][:, 0:H2], ACT.Sigmoid).then_inc(gate_free, 1)

                @block.vector
                def _(dve):
                    dve.sem_inc(prod_free, 2)
                    dve.sem_inc(mul_done, 2)
                    with dve.Fori(0, FT) as n:
                        for h in range(2):
                            m = merged[:, n, h * H2:(h + 1) * H2]
                            dve.wait_ge(gate_free, 2 * n + 3 + h)
                            dve.wait_ge(prod_ready, 2 * n + 1 + h)
                            if not add:
                                dve.tensor_tensor(m, gate[:, h, :], gp[h][:, 0:H2], ALU.mult).then_inc(prod_free, 1)
                                dve.wait_ge(prod_free, 2 * n + 3 + h)
                                dve.sem_inc(mul_done, 1)
                            else:
                                dve.tensor_tensor(gate[:, h, :], gate[:, h, :], gp[h][:, 0:H2],
                                                  ALU.mult).then_inc(prod_free, 1)
                                dve.wait_ge(prod_free, 2 * n + 3 + h)
                                dve.tensor_tensor(m, m, gate[:, h, :], ALU.add).then_inc(mul_done, 1)

    def project_out(self, merged, xT):
        nc = self.nc
        R = 4
        with ExitStack() as st:
            ring = st.enter_context(nc.sbuf_tensor("w_ring_out", [P, R, WCOLS], F32))
            root = st.enter_context(nc.sbuf_tensor("h_root", [P, T], F32))
            S_ = lambda *names: [self.sem("o_" + n) for n in names]
            landed = [self.sem(f"o_w{j}") for j in range(R)]
            gemm_ready, gemm_free = S_("gemm_ready", "gemm_free")
            gb = self.bank[0:2]
            ln = self.ln_sems("hln")
            square = lambda n: merged[:, n, :]
            with nc.Block() as block:
                @block.sync
                def _(sp):
                    self.stream(sp, ring, landed, O_OUT, N_OUT, lambda i, j: (gemm_ready, 2 * (R * i + j) + 2))

                @block.tensor
                def _(pe):
                    with pe.Fori(0, FT // R) as i:
                        for j in range(R):
                            self.gemm(pe, gb, gemm_free, 2 * (R * i + j) + 1, gemm_ready,
                                      [(ring[:, j, :], landed[j], 16 * i + 16, merged)])
                    self.ln_pe(pe, xT, square, ln)

                @block.scalar
                def _(act):
                    self.ln_act(act, xT, square, root, ln)

                @block.vector
                def _(dve):
                    dve.sem_inc(gemm_free, 2)
                    with dve.Fori(0, FT) as n:
                        for h in range(2):
                            m = xT[:, n, h * H2:(h + 1) * H2]
                            dve.wait_ge(gemm_ready, 2 * n + 1 + h)
                            dve.scalar_tensor_tensor(out=m, in0=m, scalar=ALPHA, in1=gb[h][:, 0:H2],
                                                     op0=ALU.mult, op1=ALU.add).then_inc(gemm_free, 1)
                        dve.wait_ge(gemm_free, 2 * n + 4)
                        dve.sem_inc(ln["in"], 1)
                    self.ln_dve(dve, xT, root, self.lnp[:, 2, :], self.lnp[:, 3, :], ln)

    def query(self, hT):
        nc, a = self.nc, self.a
        R = 4
        HH = 2 * PH
        with ExitStack() as keep:
            kb = lambda name, shape, dt=F32: keep.enter_context(nc.sbuf_tensor(name, shape, dt))
            htok = kb("h_tok", [P, NB, D])
            eid, gates = kb("expert", [P, NB, P], U32), kb("gates", [P, NB, P])
            eidT, gatesT = kb("expert_smp", [P, NS], U32), kb("gates_smp", [P, NS])
            with ExitStack() as st:
                sb = lambda name, shape, dt=F32: st.enter_context(nc.sbuf_tensor(name, shape, dt))
                ring = sb("w_ring_q", [P, R, WCOLS])
                keys = sb("keys", [P, HH, P])
                qb = sb("q", [P, 2, T])
                work, cand = sb("work", [P, NB, P]), sb("cand", [P, NB, TOPK * TOPK])
                tv, ti = sb("top_s", [P, NB, 2, TOPK]), sb("top_i", [P, NB, 2, TOPK], U32)
                bv, bi = sb("best_s", [P, NB, TOPK]), sb("best_c", [P, NB, TOPK], U32)
                bvs, bis = sb("best_s_all", [P, NB, PH, TOPK]), sb("best_c_all", [P, NB, PH, TOPK], U32)
                tis = sb("top_i_all", [P, NB, PH, 2, TOPK])
                code = sb("code", [P, NB, PH * TOPK], U32)
                pick = sb("pick", [P, 2, NB, PH * TOPK])
                hot = sb("one_hot", [P, PH * TOPK, TOPK])
                side = sb("side", [P, 2, NB, PH * TOPK])
                gsum = sb("gate_sum", [P, NB, PH])
                iota = sb("iota16", [P, TOPK])
                S_ = lambda *names: [self.sem("q_" + n) for n in names]
                landed = [self.sem(f"q_w{j}") for j in range(R)]
                (gemm_ready, gemm_free, keys_in, turned, turn_read, q_ready, scored, score_read, head_done,
                 iota_ready, exp_ready, exp_done, smp_ready, smp_turned) = S_(
                    "gemm_ready", "gemm_free", "keys_in", "turned", "turn_read", "q_ready", "scored",
                    "score_read", "head_done", "iota_ready", "exp_ready", "exp_done", "smp_ready", "smp_turned")
                dord, = S_("dve")
                gb, tb = self.bank[0:2], self.bank[6:8]
                tokens = lambda b: slice(b * P, min((b + 1) * P, T))
                rows = lambda b: min((b + 1) * P, T) - b * P
                NT4 = FT // 4

                with nc.Block() as block:
                    @block.sync
                    def _(sp):
                        sp.dma_start(keys[:], a["keys"]).then_inc(keys_in, 16)
                        self.stream(sp, ring, landed, O_Q, N_Q, lambda i, j: (gemm_ready, 2 * (R * i + j) + 2))

                    @block.gpsimd
                    def _(pool):
                        pool.iota(iota[:], pattern=[[1, TOPK]], base=0, channel_multiplier=0,
                                  allow_small_or_imprecise_dtypes=True).then_inc(iota_ready, 1)

                    @block.tensor
                    def _(pe):
                        for n in range(NB * NT4):
                            b, c = n // NT4, n % NT4
                            if n >= 2:
                                pe.wait_ge(turn_read, n - 1)
                            for t in range(4):
                                last = pe.transpose(tb[n % 2][0:rows(b), t * P:(t + 1) * P],
                                                    hT[:, 4 * c + t, tokens(b)], self.ident[:])
                            last.then_inc(turned, 1)
                        with pe.Fori(0, HH // R) as i:
                            for j in range(R):
                                n = R * i + j
                                self.gemm(pe, gb, gemm_free, 2 * n + 1, gemm_ready,
                                          [(ring[:, j, :], landed[j], 16 * i + 16, hT)])
                                pe.wait_ge(q_ready, 2 * n + 2)
                                pe.wait_ge(keys_in, 16)
                                pe.wait_ge(score_read, n + 1)
                                s = self.bank[2 + 2 * (j % 2):4 + 2 * (j % 2)]
                                for b in range(NB):
                                    o = s[0][:, b * P:(b + 1) * P] if b < CH else s[1][0:NS, 0:P]
                                    last = pe.matmul(o, qb[:, j % 2, tokens(b)], keys[:, n, :],
                                                     start=True, stop=True)
                                last.then_inc(scored, 1)
                        pe.wait_ge(smp_ready, 1)
                        pe.transpose(self.bank[6][:, 0:NS], side[0:NS, 0, CH, :], self.ident[0:NS, 0:NS])
                        pe.transpose(self.bank[6][:, NS:2 * NS], gates[0:NS, CH, :],
                                     self.ident[0:NS, 0:NS]).then_inc(smp_turned, 1)

                    @block.scalar
                    def _(act):
                        for n in range(NB * NT4):
                            b, c = n // NT4, n % NT4
                            act.wait_ge(turned, n + 1)
                            act.copy(htok[0:rows(b), b, 512 * c:512 * (c + 1)],
                                     tb[n % 2][0:rows(b), :]).then_inc(turn_read, 1)
                        act.sem_inc(gemm_free, 2)
                        with act.Fori(0, HH // 2) as i:
                            for j in range(2):
                                act.wait_ge(scored, 2 * i + max(j - 1, 0))
                                for h in range(2):
                                    act.wait_ge(gemm_ready, 4 * i + 2 * j + 1 + h)
                                    act.copy(qb[:, j, h * H2:(h + 1) * H2], gb[h][:, 0:H2]).then_inc(q_ready, 1)
                                act.wait_ge(q_ready, 4 * i + 2 * j + 2)
                                act.sem_inc(gemm_free, 2)
                        act.wait_ge(exp_ready, 1)
                        act.activation(gates[:], bvs[:].rearrange("p b h k -> p b (h k)"), ACT.Exp
                                       ).then_inc(exp_done, 1)

                    @block.vector
                    def _(dve):
                        o = Order(dve, dord)
                        for x in (tv, ti, bv, bi, work, cand):
                            ins = dve.memset(x[:], 0)
                        o(ins)
                        dve.sem_inc(score_read, 2)

                        def after(ins):
                            o(ins)
                            self.alone(dve)

                        def top16(src, wk, vals, idx):
                            for s_, w_, v_, x_ in zip(src, wk, vals, idx):
                                ins = dve.max(v_[:, 0:8], s_)
                            after(ins)
                            for s_, w_, v_, x_ in zip(src, wk, vals, idx):
                                dve.max_index(x_[:, 0:8], v_[:, 0:8], s_)
                                ins = dve.match_replace(w_, v_[:, 0:8], s_, NEG)
                            after(ins)
                            for s_, w_, v_, x_ in zip(src, wk, vals, idx):
                                ins = dve.max(v_[:, 8:16], w_)
                            after(ins)
                            for s_, w_, v_, x_ in zip(src, wk, vals, idx):
                                ins = dve.max_index(x_[:, 8:16], v_[:, 8:16], w_)
                            return ins

                        with dve.Fori(0, PH) as h, o.body(h, PH, 14):
                            for s in range(2):
                                dve.wait_ge(scored, 2 * h + s + 1)
                                self.alone(dve)
                                bk = self.bank[2 + 2 * s:4 + 2 * s]
                                top16([bk[0][:, b * P:(b + 1) * P] if b < CH else bk[1][0:NS, 0:P] for b in range(NB)],
                                      [work[0:rows(b), b, :] for b in range(NB)],
                                      [tv[0:rows(b), b, s, :] for b in range(NB)],
                                      [ti[0:rows(b), b, s, :] for b in range(NB)]).then_inc(score_read, 1)
                                dve.wait_ge(score_read, 2 * h + s + 3)
                            for b in range(NB):
                                dve.tensor_copy(tis[:, b, h], ti[:, b])
                                ins = dve.tensor_tensor(cand[:, b].rearrange("p (i j) -> p i j", i=TOPK),
                                                        bc(tv[:, b, 0, :], TOPK), mid(tv[:, b, 1, :], 1, TOPK), ALU.add)
                            after(ins)
                            o(top16([cand[0:rows(b), b, :] for b in range(NB)], [cand[0:rows(b), b, :] for b in range(NB)],
                                    [bv[0:rows(b), b, :] for b in range(NB)], [bi[0:rows(b), b, :] for b in range(NB)]))
                            dve.tensor_copy(bvs[:, :, h, :], bv[:])
                            o(dve.tensor_copy(bis[:, :, h, :], bi[:]))
                            o(dve.tensor_scalar(bv[:], bv[:], 0.0, None, ALU.mult))
                            o(dve.tensor_scalar(work[:], work[:], 0.0, None, ALU.mult))

                        for b in range(NB):
                            ins = dve.tensor_tensor(pick[:, 0, b].rearrange("p (h k) -> p h k", h=PH), bvs[:, b],
                                                    bvs[:, b, :, 0:1].to_broadcast([P, PH, TOPK]), ALU.subtract)
                        o(ins)
                        dve.tensor_copy(bvs[:].rearrange("p b h k -> p b (h k)"), pick[:, 0]).then_inc(exp_ready, 1)
                        dve.wait_ge(exp_ready, 1)
                        bcode = bis[:].rearrange("p b h k -> p b (h k)")
                        for s, (op, by) in enumerate(((ALU.logical_shift_right, 4), (ALU.bitwise_and, TOPK - 1))):
                            o(dve.tensor_scalar(code[:], bcode, by, None, op))
                            o(dve.tensor_copy(pick[:, s], code[:]))
                        dve.wait_ge(iota_ready, 1)
                        for b in range(NB):
                            for s in range(2):
                                o(dve.tensor_tensor(hot[:], bc(pick[:, s, b], TOPK), mid(iota[:], 1, PH * TOPK),
                                                    ALU.is_equal))
                                h4 = hot[:].rearrange("p (h k) i -> p h k i", h=PH)
                                o(dve.tensor_tensor(h4, h4, mid(tis[:, b, :, s, :], 2, TOPK), ALU.mult))
                                o(dve.tensor_reduce(side[:, s, b], hot[:], AX_X, ALU.add))
                        o(dve.scalar_tensor_tensor(out=side[:, 0], in0=side[:, 0], scalar=float(P), in1=side[:, 1],
                                                   op0=ALU.mult, op1=ALU.add))
                        o(dve.tensor_copy(eid[:], side[:, 0]))
                        dve.wait_ge(exp_done, 1)
                        gv = gates[:].rearrange("p b (h k) -> p b h k", h=PH)
                        for b in range(NB):
                            ins = dve.tensor_reduce(gsum[:, b], gv[:, b], AX_X, ALU.add)
                        o(ins)
                        o(dve.reciprocal(gsum[:], gsum[:]))
                        for b in range(NB):
                            ins = dve.tensor_tensor(gv[:, b], gv[:, b], bc(gsum[:, b], TOPK), ALU.mult)
                        ins.then_inc(smp_ready, 1)
                        dve.wait_ge(smp_turned, 1)
                        dve.tensor_copy(eidT[:], self.bank[6][:, 0:NS])
                        o(dve.tensor_copy(gatesT[:], self.bank[6][:, NS:2 * NS]))
            self.clear_sems()
            self.experts(hT, htok, eid, gates, eidT, gatesT)

    def experts(self, hT, htok, eid, gates, eidT, gatesT):
        nc, a, out = self.nc, self.a, self.o
        NR = 8
        HR = NR // 2
        NJ = P // NR
        with ExitStack() as st:
            sb = lambda name, shape, dt=F32: st.enter_context(nc.sbuf_tensor(name, shape, dt))
            more = sb("rows", [P, 12, D])
            hflat = hT[:].rearrange("p k t -> p (k t)")
            urow = [hflat[:, i * D:(i + 1) * D] for i in range(4)] + [more[:, i, :] for i in range(4)]
            vrow = [more[:, 4 + i, :] for i in range(NR)]
            acc = sb("acc", [P, D])
            ln2 = sb("ln2", [P, 2, D])
            dots, ge, coef = sb("dots", [P, NR]), sb("gelu", [P, NR]), sb("coef", [P, NR])
            iu, iv = sb("index_u", [P, NR], U32), sb("index_v", [P, NR], U32)
            sel = sb("selector", [NS, NS, P])
            onehot = sb("onehot8", [P, NS, NS])
            coefm = sb("coef_smp", [P, NS, NS])
            stats, mv = sb("bn_stats", [P, 4, 6]), sb("bn_mv", [P, 2])
            rstd = sb("rstd", [P, 1])
            S_ = lambda *names: [self.sem("e_" + n) for n in names]
            u_in = [self.sem(f"e_u{j}") for j in range(NR)]
            v_in = [self.sem(f"e_v{j}") for j in range(NR)]
            (ln2_in, masks, h_spread, smp_dots, smp_gelu, smp_coef, smp_mixed, dot_done, gelu_done, acc_done,
             var_ready, root_ready, y_ready, y_out) = S_(
                "ln2_in", "masks", "h_spread", "smp_dots", "smp_gelu", "smp_coef", "smp_mixed", "dot_done",
                "gelu_done", "acc_done", "var_ready", "root_ready", "y_ready", "y_out")
            dord, lord, pord, qord = S_("dve", "dve_ln", "pool", "pool_idx")
            gather = lambda pool, dst, table, idx: pool.indirect_dma_start(
                out=dst, out_offset=None, in_=table, in_offset=bass.IndirectOffsetOnAxis(ap=idx, axis=0))

            def norm(dve, o, rows, n):
                x = acc[0:rows, :]
                for c in range(4):
                    ins = dve.bn_stats(stats[0:rows, c, :], x[:, 512 * c:512 * (c + 1)])
                o(ins)
                self.alone(dve)
                dve.bn_aggr(mv[0:rows, :], stats[0:rows]).then_inc(var_ready, 1)
                dve.wait_ge(root_ready, n + 1)
                o(dve.reciprocal(rstd[0:rows, :], rstd[0:rows, :]))
                o(dve.tensor_scalar(x, x, mv[0:rows, 0:1], rstd[0:rows, :], ALU.subtract, ALU.mult))
                o(dve.tensor_tensor(x, x, ln2[0:rows, 0, :], ALU.mult))
                dve.tensor_tensor(x, x, ln2[0:rows, 1, :], ALU.add).then_inc(y_ready, 1)

            with nc.Block() as block:
                @block.sync
                def _(sp):
                    sp.dma_start(ln2[:], a["ln2_rows"]).then_inc(ln2_in, 16)
                    sp.wait_ge(y_ready, 1)
                    sp.dma_start(out["y_sample"], acc[0:NS, :]).then_inc(y_out, 16)
                    with sp.Fori(0, CH) as b:
                        sp.wait_ge(y_ready, b + 2)
                        sp.dma_start(out["y_prompt"][b], acc[:]).then_inc(y_out, 16)
                    sp.wait_ge(y_out, 16 * (CH + 1))

                @block.gpsimd
                def _(pool):
                    o = Order(pool, pord)
                    pool.memset(sel[:], 0.0)
                    o(pool.memset(onehot[:], 0.0))
                    pool.affine_select(out=sel[:], in_=sel[:], compare_op=ALU.not_equal, fill=1.0, base=0,
                                       pattern=[[1, NS], [0, P]], channel_multiplier=-1)
                    pool.affine_select(out=onehot[:], in_=onehot[:], compare_op=ALU.not_equal, fill=1.0, base=0,
                                       pattern=[[1, NS], [-1, NS]], channel_multiplier=0).then_inc(masks, 1)
                    for b in range(NS):
                        gather(pool, urow[b], a["peer_u"], eidT[:, b:b + 1]).then_inc(u_in[b], 16)
                    for b in range(NS):
                        gather(pool, vrow[b], a["peer_v"], eidT[:, b:b + 1]).then_inc(v_in[b], 16)
                    o = Order(pool, qord)
                    with pool.Fori(0, CH) as b:
                        with pool.Fori(0, NJ) as j:
                            it = b * NJ + j
                            for table, rows, sem, idx, free in ((a["peer_u"], urow, u_in, iu, dot_done),
                                                                (a["peer_v"], vrow, v_in, iv, acc_done)):
                                for half in range(2):
                                    s = slice(HR * half, HR * (half + 1))
                                    pool.wait_ge(free, 2 * it + half + 1)
                                    self.alone(pool)
                                    ins = pool.tensor_copy(idx[:, s], eid[:, b, bass.ds(NR * j + HR * half, HR)])
                                    ins.then_inc(qord, 1)
                                    n = (0 if table is a["peer_u"] else 2) + half
                                    pool.wait_ge(qord, 4 * it + n + 1)
                                    self.alone(pool)
                                    for k in range(HR * half, HR * (half + 1)):
                                        gather(pool, rows[k], table, idx[:, k:k + 1]).then_inc(sem[k], 16)

                @block.tensor
                def _(pe):
                    pe.wait_ge(masks, 1)
                    for b in range(NS):
                        if b >= 1:
                            pe.wait_ge(smp_dots, b)
                        for c in range(4):
                            last = pe.matmul(self.bank[c], sel[:, b, :], htok[0:NS, CH, 512 * c:512 * (c + 1)],
                                             start=True, stop=True)
                        last.then_inc(h_spread, 1)
                    pe.wait_ge(smp_coef, 1)
                    for b in range(NS):
                        pe.wait_ge(v_in[b], 16)
                        for c in range(4):
                            last = pe.matmul(self.bank[4 + c][0:NS, :], coefm[:, b, :],
                                             vrow[b][:, 512 * c:512 * (c + 1)], start=(b == 0), stop=(b == NS - 1))
                    last.then_inc(smp_mixed, 1)

                @block.scalar
                def _(act):
                    def root(rows, n):
                        act.wait_ge(var_ready, n + 1)
                        act.activation(rstd[0:rows, :], mv[0:rows, 1:2], ACT.Sqrt,
                                       bias=self.eps[0:rows, :]).then_inc(root_ready, 1)

                    act.wait_ge(smp_dots, NS)
                    act.activation(ge[:], dots[:], ACT.Gelu).then_inc(smp_gelu, 1)
                    root(NS, 0)
                    with act.Fori(0, CH) as b:
                        with act.Fori(0, NJ) as j:
                            for half in range(2):
                                s = slice(HR * half, HR * (half + 1))
                                act.wait_ge(dot_done, 2 * (b * NJ + j) + half + 3)
                                act.activation(ge[:, s], dots[:, s], ACT.Gelu).then_inc(gelu_done, 1)
                        root(P, b + 1)

                @block.vector
                def _(dve):
                    o = Order(dve, dord)
                    for b in range(NS):
                        dve.wait_ge(u_in[b], 16)
                        dve.wait_ge(h_spread, b + 1)
                        dve.scalar_tensor_tensor(out=urow[b], in0=urow[b], scalar=1.0,
                                                 in1=self.psum[:, 0:4, :].rearrange("p a b -> p (a b)"),
                                                 op0=ALU.mult, op1=ALU.mult,
                                                 accum_out=dots[:, b:b + 1]).then_inc(smp_dots, 1)
                    dve.wait_ge(smp_dots, NS)
                    dve.sem_inc(dot_done, 2)
                    dve.wait_ge(masks, 1)
                    dve.wait_ge(smp_gelu, 1)
                    o(dve.tensor_tensor(coef[:], ge[:], gatesT[:], ALU.mult))
                    dve.tensor_tensor(coefm[:], onehot[:], bc(coef[:], NS), ALU.mult).then_inc(smp_coef, 1)
                    dve.wait_ge(smp_mixed, 1)
                    dve.sem_inc(acc_done, 2)
                    o(dve.scalar_tensor_tensor(out=acc[0:NS, :], in0=htok[0:NS, CH, :], scalar=ALPHA,
                                               in1=self.psum[0:NS, 4:8, :].rearrange("p a b -> p (a b)"),
                                               op0=ALU.mult, op1=ALU.add))
                    dve.wait_ge(ln2_in, 16)
                    norm(dve, o, NS, 0)
                    lo = Order(dve, lord)
                    acc_order = self.sem("e_acc_order")
                    with dve.Fori(0, CH) as b, lo.body(b, CH, 5):
                        dve.wait_ge(y_out, 16 * b + 16)
                        lo(dve.tensor_scalar(acc[:], htok[:, b, :], ALPHA, None, ALU.mult))
                        self.alone(dve)
                        with dve.Fori(0, NJ) as j:
                            it = b * NJ + j
                            for half in range(2):
                                for k in range(HR * half, HR * (half + 1)):
                                    dve.wait_ge(u_in[k], 16 * it + 32)
                                    last = dve.scalar_tensor_tensor(out=urow[k], in0=urow[k], scalar=1.0,
                                                                    in1=htok[:, b, :], op0=ALU.mult, op1=ALU.mult,
                                                                    accum_out=dots[:, k:k + 1])
                                last.then_inc(dot_done, 1)
                            for half in range(2):
                                s = slice(HR * half, HR * (half + 1))
                                dve.wait_ge(gelu_done, 2 * it + half + 1)
                                dve.tensor_tensor(coef[:, s], ge[:, s], gates[:, b, bass.ds(NR * j + HR * half, HR)],
                                                  ALU.mult).then_inc(acc_order, 1)
                                n = (HR) * half
                                dve.wait_ge(acc_order, NR * it + n + 1)
                                for m, k in enumerate(range(HR * half, HR * (half + 1))):
                                    dve.wait_ge(v_in[k], 16 * it + 32)
                                    ins = dve.scalar_tensor_tensor(out=acc[:], in0=vrow[k], scalar=coef[:, k:k + 1],
                                                                   in1=acc[:], op0=ALU.mult, op1=ALU.add)
                                    if m < HR - 1:
                                        ins.then_inc(acc_order, 1)
                                        dve.wait_ge(acc_order, NR * it + n + m + 2)
                                    else:
                                        ins.then_inc(acc_done, 1)
                                        dve.wait_ge(acc_done, 2 * it + half + 3)
                        norm(dve, lo, P, b + 1)


def build_program(nc, arrays, outputs):
    a = {n: nc.dram_tensor("in_" + n, v.shape, F32, kind="ExternalInput").ap() for n, v in arrays.items()}
    o = {n: nc.dram_tensor("out_" + n, shape, F32, kind="ExternalOutput").ap() for n, shape in outputs.items()}
    Kernel(nc, a, o).build()


OUTPUTS = {
    "y_prompt": (CH, P, D), "y_sample": (NS, D),
    "conv_prompt": (G, P, CT, 3), "ssm_prompt": (G, P, HG * HD), "v_last": (P, FT, P + NS),
    "conv_sample": (G, P, 3, CT, NS), "ssm_sample": (NS, NH, HD, NST),
}


def conv_layout(w):
    rows, inner = w.shape[0], G * GT * P
    x = w[:, :inner].reshape(rows, G, GT, P)
    b = w[:, inner:inner + G * P].reshape(rows, G, 1, P)
    c = w[:, inner + G * P:].reshape(rows, G, 1, P)
    return np.concatenate([b, c, x], 2).transpose(1, 3, 2, 0)


def conv_unlayout(y):
    rows = y.shape[3]
    y = y.transpose(3, 0, 2, 1)
    return np.concatenate([y[:, :, 2:].reshape(rows, -1), y[:, :, 0].reshape(rows, -1), y[:, :, 1].reshape(rows, -1)], 1)


def weight_tiles(i):
    w_in, wa, wb, wo, wq = (i[n][0] for n in ("w_in", "w_branch_a", "w_branch_b", "w_out", "peer_wq"))
    inner, gn = G * GT * P, G * NST
    z0, x0, b0, c0 = 0, inner, 2 * inner, 2 * inner + gn
    u0 = c0 + gn + NH
    v0, ga0, gb0 = u0 + D, u0 + 2 * D, u0 + 3 * D
    cols = []
    for g in range(G):
        cols += [(w_in, 0, b0 + g * P), (w_in, 0, c0 + g * P)]
        cols += [(w_in, 0, x0 + (GT * g + t) * P) for t in range(GT)]
        cols += [(w_in, 0, z0 + (GT * g + t) * P) for t in range(GT)]
    cols += [(w_in, 0, v0 + n * P) for n in range(FT)]
    cols += [(w_in, 0, u0 + n * P) for n in range(FT)]
    for n in range(FT):
        cols += [(w_in, 0, gb0 + n * P), (wb, 0, n * P)]
    for n in range(FT):
        cols += [(w_in, 0, ga0 + n * P), (wa, 0, n * P), (wa, D, n * P)]
    cols += [(wo, 0, n * P) for n in range(FT)]
    cols += [(wq, 0, n * P) for n in range(FT)]
    out = np.empty((len(cols), P, WCOLS), np.float32)
    for n, (w, r, c) in enumerate(cols):
        out[n].reshape(P, KB, P)[:] = w[r:r + D, c:c + P].reshape(KB, P, P).transpose(1, 0, 2)
    return out


def kernel(**inputs):
    import concourse.bacc as bacc
    from concourse.bass_utils import run_bass_kernel_spmd

    i = {n: np.asarray(v) for n, v in inputs.items()}
    x = np.concatenate([i["x_prompt"][0], i["x_sample"][:, 0]], 0)
    cols = lambda v: v.reshape(FT, P).T
    dt0 = 2 * G * GT * P + 2 * G * NST
    wdt = i["w_in"][0][:, dt0:dt0 + NH]
    per_head = np.broadcast_to(i["d_skip"][0].reshape(G, GT, 2, 1), (G, GT, 2, HD)).reshape(G, GT, P)
    twice = lambda v: np.concatenate([v, v])[:, None]
    rowP = lambda v: np.broadcast_to(v[None], (P,) + v.shape)
    taps = conv_layout(i["conv_w"][0])
    arrays = {
        "w_tiles": weight_tiles(i),
        "xT": x.T.reshape(KB, P, T).transpose(1, 0, 2),
        "w_dt": wdt.reshape(KB, P, NH).transpose(1, 0, 2),
        "dt_rows": np.concatenate([rowP(i["dt_bias"][0]), rowP(i["a_log"][0]),
                                   twice(i["dt_bias"][0]), twice(i["a_log"][0])], 1),
        "ln_cols": np.stack([cols(i[n][0]) for n in ("sgu_ln_g", "sgu_ln_b", "ln1_g", "ln1_b")], 1),
        "g_par": np.concatenate([taps.reshape(G, P, CT * 4), conv_layout(i["conv_b"])[..., 0],
                                 i["ssd_norm_w"][0].reshape(G, GT, P).transpose(0, 2, 1),
                                 per_head.transpose(0, 2, 1)], 2),
        "state_conv": conv_layout(i["state_conv"][0].reshape(NS * 3, -1)).reshape(G, P, CT, NS, 3)
                      .transpose(0, 1, 4, 2, 3),
        "state_ssm": i["state_ssm"][0],
        "sgu_wT": i["sgu_w"][0].transpose(0, 2, 1),
        "sgu_b": np.broadcast_to(i["sgu_b"][0][:, None, :], (FT, P, P)),
        "sgu_first": rowP(np.stack([i["sgu_w"][0][:, 0, 0], i["sgu_b"][0][:, 0]])),
        "keys": i["peer_keys"][0].reshape(2 * PH, P, P).transpose(2, 0, 1),
        "ln2_rows": rowP(np.stack([i["ln2_g"][0], i["ln2_b"][0]])),
        "peer_u": i["peer_u"][0],
        "peer_v": i["peer_v"][0],
    }
    arrays = {n: np.ascontiguousarray(v) for n, v in arrays.items()}
    nc = bacc.Bacc("TRN2", target_bir_lowering=False, num_devices=1)
    build_program(nc, arrays, OUTPUTS)
    r = run_bass_kernel_spmd(nc, [{"in_" + n: v for n, v in arrays.items()}], core_ids=[0]).results[0]
    r = {n: np.asarray(r["out_" + n]) for n in OUTPUTS}
    conv_s = conv_unlayout(r["conv_sample"].transpose(0, 1, 3, 4, 2).reshape(G, P, CT, NS * 3))
    ssm_p = r["ssm_prompt"].reshape(G, NST, HG, HD).transpose(0, 2, 3, 1).reshape(1, 1, NH, HD, NST)
    v = r["v_last"].transpose(2, 1, 0).reshape(P + NS, D)
    return (r["y_prompt"].reshape(1, TP, D), r["y_sample"].reshape(NS, 1, D),
            conv_unlayout(r["conv_prompt"]).reshape(1, 1, 3, -1), ssm_p,
            v[:P].reshape(1, 1, P, D), conv_s.reshape(1, NS, 3, -1),
            r["ssm_sample"][None], v[P:].reshape(1, NS, 1, D))
```

```python
from contextlib import ExitStack, contextmanager

import numpy as np

import concourse.bass as bass
from concourse import mybir

F32 = mybir.dt.float32
FR = mybir.dt.float32r
U32 = mybir.dt.uint32
ALU = mybir.AluOpType
ACT = mybir.ActivationFunctionType
AX_X = mybir.AxisListType.X

P = 128
D = 2048
KB = D // P
TP = 512
NS = 8
T = TP + NS
H2 = T // 2
CH = 4
G = 8
HG = 8
HD = 64
NH = G * HG
GT = HG * HD // P
NST = 128
CT = 2 + GT
FT = D // P
EPS = 1e-5
ALPHA = 2.0 ** 0.25
PH = 8
TOPK = 16
NB = 5
NEG = -3.0e38
WCOLS = KB * P

N_SSD = G * (CT + GT)
N_V = FT
N_U = FT
O_V = N_SSD
O_U = O_V + N_V
O_GATE = O_U + N_U
O_BR = O_GATE + 2 * FT
O_OUT = O_BR + 3 * FT
O_Q = O_OUT + FT
N_TILES = O_Q + FT
READY0 = 4

SSD_DVE = 4 * CT + 1 + 2 * CH + 1
SSD_POOL = 5 * GT

GP_B = CT * 4
GP_NW = GP_B + CT
GP_D = GP_NW + GT
GP_N = GP_D + GT


class Order:

    def __init__(self, eng, sem):
        self.eng, self.sem, self.base, self.n = eng, sem, 0, 0

    def __call__(self, ins):
        ins.then_inc(self.sem, 1)
        self.n += 1
        self.eng.wait_ge(self.sem, self.base + self.n)

    @contextmanager
    def body(self, i, count, per):
        before = self.base + self.n
        self.base, self.n = before + i * per, 0
        yield
        assert self.n == per, f"{self.n} counted in the body, {per} said"
        self.base, self.n = before + count * per, 0


def bc(ap, n):
    return ap.unsqueeze(ap.ndim).to_broadcast(list(ap.shape) + [n])


def mid(ap, axis, n):
    shape = list(ap.shape)
    return ap.unsqueeze(axis).to_broadcast(shape[:axis] + [n] + shape[axis:])


class Kernel:
    def __init__(self, nc, a, o):
        self.nc, self.a, self.o = nc, a, o

    def sem(self, name):
        handle = self.nc.alloc_semaphore(name=name)
        self.phase_sems.append(handle)
        return handle

    def alone(self, eng):
        key = str(eng.engine)
        if key not in self.ticks:
            self.ticks[key] = self.sem("tick_" + key.split(".")[-1] + str(len(self.nc.allocations)))
        eng.sem_inc(self.ticks[key], 1)

    def clear_sems(self):
        self.nc.clear_and_free_semaphores(self.phase_sems)
        self.nc.all_engine_barrier()
        self.phase_sems, self.ticks = [], {}

    def load_weight(self, sp, n, j):
        sp.wait_ge(self.w_split, n - 1)
        sp.dma_start(self.w_raw[:, j, :], self.a["w_tiles"][n]).then_inc(self.w_in[j], 16)

    def stream(self, sp, first, total):
        last = first + total == N_TILES
        with sp.Fori(0, total // 2 - (1 if last else 0)) as i:
            for j in range(2):
                self.load_weight(sp, 2 * i + (first + 2 + j), j)

    def hi(self, act, n):
        j, n, half = n
        act.wait_ge(self.w_in[j], half * 16 + 16)
        act.wait_ge(self.gemm_ready, 2 * n + READY0 - 2)
        act.copy(self.wh[:, j, :], self.w_raw[:, j, :]).then_inc(self.w_hi, 1)

    def lo(self, dve, n):
        j, n, half = n
        dve.wait_ge(self.w_hi, n + 1)
        dve.tensor_tensor(self.wl[:, j, :], self.w_raw[:, j, :], self.wh[:, j, :].bitcast(F32),
                          ALU.subtract).then_inc(self.w_split, 1)

    @staticmethod
    def next_tile(first, i, j):
        return (j + 1) % 2, 2 * i + (first + j + 1), i + (first // 2 + (j + 1) // 2)

    def turns(self, eng, first, total, body):
        last = 1 if first + total == N_TILES else 0
        with eng.Fori(0, total // 2 - last) as i:
            for j in range(2):
                body(2 * i + j, j, self.next_tile(first, i, j))
        if last:
            body(total - 2, 0, self.next_tile(first, total // 2 - 1, 0))
            body(total - 1, 1, None)

    def gemm(self, pe, n, j, pair_ready=None, between=None):
        for h in range(2):
            pe.wait_ge(self.gemm_free, 2 * n + 1 + h)
            if h == 0:
                pe.wait_ge(self.w_split, n + 1)
            elif between:
                between()
            hs = slice(h * H2, (h + 1) * H2)
            for k in range(KB):
                if pair_ready and h == 0:
                    pe.wait_ge(pair_ready[0], pair_ready[1] + k + 1)
                ks = slice(k * P, (k + 1) * P)
                o = self.bank[h][:, 0:H2]
                pe.matmul(o, self.wh[:, j, ks], self.ah[:, k, hs], start=(k == 0), stop=False)
                pe.matmul(o, self.wh[:, j, ks], self.al[:, k, hs], start=False, stop=False)
                last = pe.matmul(o, self.wl[:, j, ks], self.ah[:, k, hs], start=False, stop=(k == KB - 1))
            last.then_inc(self.gemm_ready, 1)

    def gemms(self, pe, first, total, pair_ready=None):
        skip = 0
        if pair_ready:
            skip = 1
            for j in range(2):
                self.gemm(pe, first + j, j, pair_ready if j == 0 else None)
        with pe.Fori(0, total // 2 - skip) as i:
            for j in range(2):
                self.gemm(pe, 2 * i + (first + 2 * skip + j), j)

    def build(self):
        nc = self.nc
        self.root = ExitStack()
        self.phase_sems, self.ticks = [], {}
        self.w_in = [nc.alloc_semaphore(name=f"w_in{j}") for j in range(2)]
        self.w_hi, self.w_split, self.gemm_ready, self.gemm_free = (
            nc.alloc_semaphore(name=n) for n in ("w_hi", "w_split", "gemm_ready", "gemm_free"))
        with self.root:
            sb = lambda name, shape, dt=F32: self.root.enter_context(nc.sbuf_tensor(name, shape, dt))
            self.ident = sb("ident", [P, P])
            self.ones = sb("ones", [P, P])
            self.triu = sb("triu", [P, P])
            self.onesD = sb("onesD", [P, P])
            self.onesG = sb("onesG", [P, P])
            self.eps = sb("eps", [P, 1])
            self.lnp = sb("lnp", [P, 4, FT])
            self.psum = self.root.enter_context(nc.psum_tensor("psum", [P, 8, 512], F32))
            self.bank = [self.psum[:, i, :] for i in range(8)]
            eid, gates = sb("expert", [P, NB, P], U32), sb("gates", [P, NB, P])
            eidT, gatesT = sb("expert_smp", [P, NS], U32), sb("gates_smp", [P, NS])
            htok = sb("shared", [P, NB, D])
            self.shared = htok[:].rearrange("p b d -> p (b d)")
            full = self.shared[:, 0:KB * T].rearrange("p (k t) -> p k t", k=KB)
            with ExitStack() as gemm:
                gs = lambda name, shape, dt=F32: gemm.enter_context(nc.sbuf_tensor(name, shape, dt))
                self.ah, self.al = gs("acts_hi", [P, KB, T], FR), gs("acts_lo", [P, KB, T], FR)
                self.w_raw = gs("w_raw", [P, 2, WCOLS])
                self.wh, self.wl = gs("w_hi_ring", [P, 2, WCOLS], FR), gs("w_lo_ring", [P, 2, WCOLS], FR)
                with ExitStack() as st:
                    tabs = self.tables(st, full)
                    self.clear_sems()
                    self.ssd(st, tabs)
                    self.clear_sems()
                self.sgu(full)
                self.clear_sems()
                self.gate_phase()
                self.clear_sems()
                self.branches(full)
                self.clear_sems()
                self.project_out(full, htok)
                self.clear_sems()
                self.query(eid, gates, eidT, gatesT)
            self.clear_sems()
            self.experts(htok, eid, gates, eidT, gatesT)

    def split_hi(self, act, src, hi_done, ready=None):
        for k in range(KB):
            if ready:
                act.wait_ge(*ready(k))
            act.copy(self.ah[:, k, :], src[:, k, :]).then_inc(hi_done, 1)

    def split_lo(self, dve, src, hi_done, pair_ready, base=0):
        for k in range(KB):
            dve.wait_ge(hi_done, base + k + 1)
            dve.tensor_tensor(self.al[:, k, :], src[:, k, :], self.ah[:, k, :].bitcast(F32),
                              ALU.subtract).then_inc(pair_ready, 1)

    def tables(self, st, xT):
        nc, a = self.nc, self.a
        tab = st.enter_context(nc.sbuf_tensor("dt_tab", [P, G, 4, CH, HG], F32))
        stab = st.enter_context(nc.sbuf_tensor("dt_smp", [P, G, 2, GT, NS], F32))
        NC = CH * NH
        W = NC + NS
        with ExitStack() as tmp:
            sb = lambda name, shape, dt=F32: tmp.enter_context(nc.sbuf_tensor(name, shape, dt))
            wdt = sb("wdt", [P, KB, NH])
            rows = sb("dt_rows", [P, 2 * NH + 2])
            v = {n: sb("sp_" + n, [P, W]) for n in ("x", "n", "u", "w", "l", "d", "m", "t")}
            dtA, acum, dte = sb("dtA", [P, W]), sb("acum", [P, NC]), sb("dte", [P, NC])
            arow = sb("arow", [P, NH + 1])
            diag = sb("dt_diag", [NH, 2, NS, NH])
            eA = sb("smp_eA", [P, NS])
            in_sem, x_in, made, dord, pord = (self.sem("t_" + n) for n in ("in", "x_in", "made", "dve", "pool"))
            proj_done, sums_done, spread_done = (self.sem("t_" + n) for n in ("proj", "sums", "spread"))
            rate_ready, u_ready, ln_ready, decay_ready = (self.sem("t_" + n) for n in ("rate", "u", "ln", "decay"))
            neg_ready, w_ready, dtA_ready, gap_ready, diag_ready, hi_done, split = (
                self.sem("t_" + n) for n in ("neg", "w", "dtA", "gap", "diag", "x_hi", "x_split"))
            dtp, sps, ac, bcs = self.bank[0], self.bank[1], self.bank[2], self.bank[3:5]

            with nc.Block() as block:
                @block.sync
                def _(sp):
                    for j in range(2):
                        sp.dma_start(self.w_raw[:, j, :], a["w_tiles"][j]).then_inc(self.w_in[j], 16)
                    sp.dma_start(xT, a["xT"]).then_inc(x_in, 16)
                    sp.dma_start(wdt[:], a["w_dt"]).then_inc(x_in, 16)
                    sp.dma_start(rows[:], a["dt_rows"]).then_inc(in_sem, 16)
                    sp.dma_start(self.lnp[:], a["ln_cols"]).then_inc(in_sem, 16)
                    sp.wait_ge(in_sem, 32)

                @block.gpsimd
                def _(pool):
                    o = Order(pool, pord)
                    pool.memset(self.ident[:], 0.0)
                    pool.memset(self.ones[:], 1.0)
                    pool.memset(self.onesD[:], 1.0 / D)
                    pool.memset(self.onesG[:], 1.0 / (GT * P))
                    o(pool.memset(self.eps[:], EPS))
                    pool.affine_select(out=self.ident[:], in_=self.ident[:], compare_op=ALU.not_equal,
                                       fill=1.0, base=0, pattern=[[1, P]], channel_multiplier=-1)
                    pool.affine_select(out=self.triu[:], in_=self.ones[:], compare_op=ALU.is_ge,
                                       fill=0.0, base=0, pattern=[[1, P]],
                                       channel_multiplier=-1).then_inc(made, 1)

                @block.tensor
                def _(pe):
                    pe.sem_inc(self.gemm_ready, READY0)
                    pe.wait_ge(x_in, 32)
                    for c in range(CH):
                        for k in range(KB):
                            pe.matmul(dtp[:, c * NH:(c + 1) * NH], xT[:, k, c * P:(c + 1) * P],
                                      wdt[:, k, :], start=(k == 0), stop=(k == KB - 1))
                    for k in range(KB):
                        last = pe.matmul(sps[0:NH, 0:NS], wdt[:, k, :], xT[:, k, TP:T],
                                         start=(k == 0), stop=(k == KB - 1))
                    last.then_inc(proj_done, 1)
                    pe.wait_ge(made, 1)
                    pe.wait_ge(dtA_ready, 1)
                    pe.matmul(ac[:, 0:NC], self.triu[:], dtA[:, 0:NC], start=True, stop=True)
                    pe.matmul(ac[:, NC:2 * NC], self.ones[:], dtA[:, 0:NC],
                              start=True, stop=True).then_inc(sums_done, 1)
                    pe.wait_ge(diag_ready, 1)
                    for s in range(2):
                        last = pe.matmul(bcs[s][:, 0:NS * NH], self.ones[0:NH, :],
                                         diag[:, s].rearrange("p b h -> p (b h)"), start=True, stop=True)
                    last.then_inc(spread_done, 1)

                @block.scalar
                def _(act):
                    act.sem_inc(self.gemm_free, 2)
                    self.hi(act, (0, 0, 0))
                    act.wait_ge(x_in, 32)
                    self.split_hi(act, xT, hi_done)
                    act.wait_ge(in_sem, 32)
                    act.activation(arow[:, 0:NH], rows[:, NH:2 * NH], ACT.Exp)
                    act.activation(arow[:, NH:NH + 1], rows[:, 2 * NH + 1:2 * NH + 2],
                                   ACT.Exp).then_inc(rate_ready, 1)
                    act.wait_ge(neg_ready, 1)
                    act.activation(v["u"][:], v["n"][:], ACT.Exp).then_inc(u_ready, 1)
                    act.wait_ge(w_ready, 1)
                    act.activation(v["l"][:], v["w"][:], ACT.Ln).then_inc(ln_ready, 1)
                    act.wait_ge(gap_ready, 1)
                    act.activation(dte[:], acum[:], ACT.Exp)
                    act.activation(eA[0:NH, :], dtA[0:NH, NC:W], ACT.Exp).then_inc(decay_ready, 1)

                @block.vector
                def _(dve):
                    o = Order(dve, dord)
                    x = v["x"]
                    o(dve.memset(x[:], 0.0))
                    self.lo(dve, (0, 0, 0))
                    self.split_lo(dve, xT, hi_done, split)
                    dve.wait_ge(split, KB)
                    dve.wait_ge(proj_done, 1)
                    dve.wait_ge(in_sem, 32)
                    dve.tensor_tensor(x[:, 0:NC].rearrange("p (c h) -> p c h", c=CH),
                                      dtp[:, 0:NC].rearrange("p (c h) -> p c h", c=CH),
                                      mid(rows[:, 0:NH], 1, CH), ALU.add)
                    o(dve.tensor_scalar(x[0:NH, NC:W], sps[0:NH, 0:NS], rows[0:NH, 2 * NH:2 * NH + 1],
                                        None, ALU.add))
                    dve.scalar_tensor_tensor(out=v["n"][:], in0=x[:], scalar=-1.0, in1=x[:],
                                             op0=ALU.mult, op1=ALU.min).then_inc(neg_ready, 1)
                    dve.wait_ge(u_ready, 1)
                    dve.tensor_scalar(v["w"][:], v["u"][:], 1.0, None, ALU.add).then_inc(w_ready, 1)
                    dve.wait_ge(w_ready, 1)
                    o(dve.tensor_scalar(v["d"][:], v["w"][:], -1.0, None, ALU.add))
                    o(dve.tensor_scalar(v["m"][:], v["d"][:], 0.0, None, ALU.is_equal))
                    dve.wait_ge(ln_ready, 1)
                    dve.tensor_tensor(v["l"][:], v["l"][:], v["m"][:], ALU.add)
                    o(dve.tensor_tensor(v["d"][:], v["d"][:], v["m"][:], ALU.add))
                    o(dve.reciprocal(v["t"][:], v["d"][:]))
                    o(dve.tensor_tensor(v["l"][:], v["l"][:], v["t"][:], ALU.mult))
                    o(dve.tensor_tensor(v["l"][:], v["l"][:], v["u"][:], ALU.mult))
                    dt = v["t"]
                    o(dve.scalar_tensor_tensor(out=dt[:], in0=x[:], scalar=0.0, in1=v["l"][:],
                                               op0=ALU.max, op1=ALU.add))
                    dve.wait_ge(rate_ready, 1)
                    o(dve.tensor_scalar(v["w"][:, 0:NH + 1], arow[:], -1.0, None, ALU.mult))
                    dve.tensor_scalar(dtA[0:NH, NC:W], dt[0:NH, NC:W], v["w"][0:NH, NH:NH + 1],
                                      None, ALU.mult)
                    dve.tensor_tensor(dtA[:, 0:NC].rearrange("p (c h) -> p c h", c=CH),
                                      dt[:, 0:NC].rearrange("p (c h) -> p c h", c=CH),
                                      mid(v["w"][:, 0:NH], 1, CH), ALU.mult).then_inc(dtA_ready, 1)
                    dve.wait_ge(sums_done, 1)
                    dve.wait_ge(dtA_ready, 1)
                    o(dve.tensor_copy(v["n"][:, 0:NC], ac[:, 0:NC]))
                    dve.tensor_tensor(acum[:], ac[:, NC:2 * NC], v["n"][:, 0:NC],
                                      ALU.subtract).then_inc(gap_ready, 1)
                    dve.wait_ge(decay_ready, 1)
                    o(dve.tensor_tensor(dte[:], dte[:], dt[:, 0:NC], ALU.mult))
                    for kind, src in enumerate((dt, dte, v["n"], dtA)):
                        for c in range(CH):
                            dve.tensor_copy(tab[:, :, kind, c, :],
                                            src[:, c * NH:(c + 1) * NH].rearrange("p (g h) -> p g h", g=G))
                    for s, src in enumerate((dt[0:NH, NC:W], eA[0:NH, :])):
                        last = dve.tensor_tensor(diag[:, s], mid(self.ident[0:NH, 0:NH], 1, NS),
                                                 bc(src, NH), ALU.mult)
                    last.then_inc(diag_ready, 1)
                    dve.wait_ge(spread_done, 1)
                    for s in range(2):
                        src = bcs[s][:, 0:NS * NH].rearrange("p (b g t w) -> p g t w b", b=NS, g=G, w=2)
                        for g in range(G):
                            for w in range(2):
                                last = dve.tensor_copy(stab[w * HD:(w + 1) * HD, g, s],
                                                       src[w * HD:(w + 1) * HD, g, :, w, :])
                    o(last)
        return tab, stab

    def ssd(self, st, tabs):
        nc, a, out = self.nc, self.a, self.o
        tab, stab = tabs
        NT = CT + GT
        HB = NS // 2
        NU = GT * 2
        sb = lambda name, shape, dt=F32: st.enter_context(nc.sbuf_tensor(name, shape, dt))
        used = [0]

        def region(*shape):
            n = int(np.prod(shape))
            part = self.shared[:, used[0]:used[0] + n]
            used[0] += n
            names = " ".join("abc"[:len(shape)])
            return part if len(shape) == 1 else part.rearrange(
                f"p ({names}) -> p {names}", **{"abc"[i]: d for i, d in enumerate(shape)})

        raw = sb("raw", [P, 2, TP + 3])
        acc = sb("conv_acc", [P, 2, TP + NS])
        scv = sb("smp_conv", [P, 4, CT, NS])
        gpar = sb("g_par", [P, GP_N])
        cpo = sb("conv_pr_out", [P, CT, 3])
        sprod = sb("smp_prod", [P, 4, NS])
        bT, cT, xg, yg = region(T), region(T), region(GT, T), region(GT, T)
        gt, gs = sb("g_tab", [P, 4, CH, HG]), sb("g_smp", [P, 2, GT, NS])
        xdt, xde = sb("xdt", [P, HG, HD]), sb("x_dt_decay", [P, HG, HD])
        btok, cbm = sb("b_tok", [P, P]), sb("cb_masked", [P, P])
        tri = region(HG, P)
        L, eA = region(HG, P), region(HG, P)
        cdec = sb("chunk_decay", [P, HG])
        S = sb("state", [P, HG, HD])
        sst = sb("smp_state", [P, 2, HB, NST])
        stmp = sb("smp_tmp", [P, HB, NST])
        Bb, Cb = region(NS, NST), sb("C_bcast", [P, NS, NST])
        ys = sb("smp_y", [P, GT, NS])
        gb, tpb, bcb, ab, yb, stb = (self.bank[0:2], self.bank[2], self.bank[3], self.bank[4:6],
                                     self.bank[6], self.bank[7])
        S_ = lambda *names: [self.sem("s_" + n) for n in names]
        gemm_ready, gemm_free = self.gemm_ready, self.gemm_free
        raw_ready, conv_done, silu_done, stored, y_out, y_stored = S_(
            "raw_ready", "conv_done", "silu_done", "stored", "y_out", "y_stored")
        par_in, conv_in, conv_out = S_("par_in", "conv_in", "conv_out")
        diag_ready, spread_done, spread_read = S_("diag_ready", "spread_done", "spread_read")
        tri_ready, a_done, seg_done, exp_done, m_ready, b_done, y_done = S_(
            "tri_ready", "a_done", "seg_done", "exp_done", "m_ready", "b_done", "y_done")
        gated, squared, rms_done, root_ready, group_done = S_(
            "gated", "squared", "rms_done", "root_ready", "group_done")
        tabs_ready, prod_ready, prod_read, fin_ready, fin_out = S_(
            "tabs_ready", "prod_ready", "prod_read", "fin_ready", "fin_out")
        st_in = [self.sem(f"s_st_in{j}") for j in range(2)]
        st_out = [self.sem(f"s_st_out{j}") for j in range(2)]
        dord, pord = S_("dve", "pool")
        state_in = a["state_ssm"].rearrange("b (t w) p n -> t (w p) b n", w=2)
        state_out = out["ssm_sample"].rearrange("b (t w) p n -> t (w p) b n", w=2)

        with nc.Block() as block:
            @block.sync
            def _(sp):
                self.stream(sp, 0, N_SSD)

            @block.tensor
            def _(pe):
                with pe.Fori(0, G) as g:
                    def project(t):
                        self.gemm(pe, NT * g + t, t % 2)

                    def spread(n):
                        pe.wait_ge(diag_ready, 2 * g + n + 1)
                        pe.wait_ge(spread_read, 2 * g + n + 1)
                        for h in range(2):
                            last = pe.matmul(ab[h][:], self.ones[:],
                                             tri[:, 4 * h:4 * h + 4, :].rearrange("p a b -> p (a b)"),
                                             start=True, stop=True)
                        last.then_inc(spread_done, 1)

                    def chunk_a(q):
                        s = slice(q * P, (q + 1) * P)
                        pe.wait_ge(silu_done, CT * g + CT + 2)
                        pe.wait_ge(tri_ready, CH * g + q + 1)
                        if q == 0:
                            pe.wait_ge(spread_read, 2 * g + 3)
                        for t in range(GT):
                            pe.transpose(tpb[:, t * P:(t + 1) * P], xg[:, t, s], self.ident[:])
                        pe.transpose(bcb[:, 0:P], bT[:, s], self.ident[:])
                        pe.matmul(bcb[:, P:2 * P], bT[:, s], cT[:, s], start=True, stop=True)
                        for h in range(2):
                            last = pe.matmul(ab[h][:], self.ones[:],
                                             tri[:, 4 * h:4 * h + 4, :].rearrange("p a b -> p (a b)"),
                                             start=True, stop=True)
                        last.then_inc(a_done, 1)

                    def chunk_b(q):
                        pe.wait_ge(m_ready, CH * g + q + 2)
                        pe.wait_ge(y_done, CH * g + q + 1)
                        for t in range(GT):
                            for w in range(2):
                                h = 2 * t + w
                                o = yb[w * HD:(w + 1) * HD, t * P:(t + 1) * P]
                                pe.matmul(o, xdt[:, h, :], L[:, h, :], start=True, stop=False)
                                pe.matmul(o, S[:, h, :], eA[:, h, :], start=False, stop=True)
                        pe.matmul(stb[:], btok[:], xde[:].rearrange("p a b -> p (a b)"),
                                  start=True, stop=True).then_inc(b_done, 1)

                    for t in range(4):
                        project(t)
                        if t >= 2:
                            spread(t - 2)
                    project(4)
                    project(5)
                    for q in range(CH):
                        chunk_a(q)
                        project(CT + q)
                        chunk_b(q)
                    for t in range(GT):
                        pe.wait_ge(squared, GT * g + t + 1)
                        for h in range(2):
                            last = pe.matmul(ab[h][:, 0:H2], self.onesG[:], xg[:, t, h * H2:(h + 1) * H2],
                                             start=(t == 0), stop=(t == GT - 1))
                    last.then_inc(rms_done, 1)

            @block.scalar
            def _(act):
                act.sem_inc(silu_done, 2)
                act.sem_inc(spread_read, 1)
                with act.Fori(0, G) as g:
                    def evac(t):
                        r = raw[:, t % 2, :]
                        act.wait_ge(conv_done, CT * g + t + 1)
                        act.wait_ge(gemm_ready, READY0 + 2 * NT * g + 2 * t + 1)
                        act.copy(r[:, 3:3 + H2], gb[0][:, 0:H2]).then_inc(gemm_free, 1)
                        act.wait_ge(gemm_ready, READY0 + 2 * NT * g + 2 * t + 2)
                        act.copy(r[:, 3 + H2:3 + TP], gb[1][:, 0:TP - H2]).then_inc(raw_ready, 1)
                        act.copy(scv[:, 3, t, :], gb[1][:, TP - H2:H2]).then_inc(gemm_free, 1)

                    def silu(t):
                        dst = (bT, cT)[t] if t < 2 else xg[:, t - 2, :]
                        act.wait_ge(conv_done, CT * g + t + 3)
                        act.wait_ge(par_in, 16 * g + 16)
                        if t == 0:
                            act.wait_ge(group_done, g + 1)
                        act.activation(dst, acc[:, t % 2, :], ACT.Silu,
                                       bias=gpar[:, GP_B + t:GP_B + t + 1]).then_inc(silu_done, 1)

                    def spread_out(n):
                        act.wait_ge(spread_done, 2 * g + n + 1)
                        for h in range(2):
                            last = act.copy((Bb, Cb)[n][:, 4 * h:4 * h + 4, :].rearrange("p a b -> p (a b)"),
                                            ab[h][:])
                        last.then_inc(spread_read, 1)

                    self.hi(act, (1, NT * g + 1, NT // 2 * g))
                    act.wait_ge(stored, g + 1)
                    evac(0)
                    for t in range(1, CT):
                        self.hi(act, ((t + 1) % 2, NT * g + t + 1, NT // 2 * g + (t + 1) // 2))
                        if t in (3, 4):
                            spread_out(t - 3)
                        evac(t)
                        silu(t - 1)
                    silu(CT - 1)
                    act.wait_ge(y_stored, g + 1)
                    for q in range(CH):
                        t = CT + q + 1
                        self.hi(act, (t % 2, NT * g + t, NT // 2 * g + t // 2))
                        act.wait_ge(m_ready, CH * g + q + 1)
                        act.wait_ge(seg_done, CH * g + q + 1)
                        for h in range(2):
                            act.activation(eA[:, 4 * h:4 * h + 4, :].rearrange("p a b -> p (a b)"),
                                           ab[h][:], ACT.Exp)
                        act.activation(L[:], L[:], ACT.Exp).then_inc(exp_done, 1)
                        t = CT + q
                        for h in range(2):
                            act.wait_ge(gemm_ready, READY0 + 2 * NT * g + 2 * t + 1 + h)
                            act.activation(yg[:, q, h * H2:(h + 1) * H2], gb[h][:, 0:H2],
                                           ACT.Silu).then_inc(gemm_free, 1)
                    for t in range(GT):
                        act.wait_ge(gated, GT * g + t + 1)
                        act.activation(xg[:, t, :], yg[:, t, :], ACT.Square).then_inc(squared, 1)
                    act.wait_ge(rms_done, g + 1)
                    for h in range(2):
                        last = act.activation(acc[:, 0, h * H2:(h + 1) * H2], ab[h][:, 0:H2], ACT.Sqrt,
                                              bias=self.eps[:])
                    last.then_inc(root_ready, 1)

            @block.vector
            def _(dve):
                o = Order(dve, dord)
                dve.memset(raw[:, 0, 0:3], 0.0)
                o(dve.memset(raw[:, 1, 0:3], 0.0))
                dve.sem_inc(conv_done, 2)
                for s in (m_ready, y_done, group_done, prod_read):
                    dve.sem_inc(s, 1)
                with dve.Fori(0, G) as g, o.body(g, G, SSD_DVE):
                    def conv(t):
                        r, ac = raw[:, t % 2, :], acc[:, t % 2, 0:TP]
                        w = gpar[:, 4 * t:4 * t + 4]
                        dve.wait_ge(raw_ready, CT * g + t + 1)
                        dve.wait_ge(gemm_free, 2 * NT * g + 2 * t + 4)
                        dve.wait_ge(silu_done, CT * g + t + 1)
                        o(dve.tensor_scalar(ac, r[:, 0:TP], w[:, 0:1], None, ALU.mult))
                        for k in range(1, 4):
                            ins = dve.scalar_tensor_tensor(out=ac, in0=r[:, k:k + TP], scalar=w[:, k:k + 1],
                                                           in1=ac, op0=ALU.mult, op1=ALU.add)
                            if k < 3:
                                o(ins)
                        dve.tensor_copy(cpo[:, t, :], r[:, TP:TP + 3])
                        o(dve.tensor_tensor(sprod[:], scv[:, :, t, :], bc(w, NS), ALU.mult))
                        dve.tensor_reduce(acc[:, t % 2, TP:T], sprod[:].rearrange("p r b -> p b r"), AX_X, ALU.add).then_inc(conv_done, 1)
                        dve.wait_ge(conv_done, CT * g + t + 3)

                    def diagonal(n):
                        dve.wait_ge(silu_done, CT * g + n + 3)
                        if n:
                            dve.wait_ge(spread_done, 2 * g + n)
                        dve.tensor_tensor(tri[:], mid(self.ident[:], 1, NS), bc((bT, cT)[n][:, TP:T], P),
                                          ALU.mult).then_inc(diag_ready, 1)

                    def tri_rhs(q):
                        dve.tensor_tensor(tri[:], mid(self.triu[:], 1, HG), bc(gt[:, 3, q, :], P),
                                          ALU.mult).then_inc(tri_ready, 1)

                    def sum_smp(u):
                        dve.wait_ge(prod_ready, NU * g + u + 1)
                        dve.tensor_reduce(ys[:, u // 2, HB * (u % 2):HB * (u % 2) + HB], stmp[:], AX_X,
                                          ALU.add).then_inc(prod_read, 1)

                    dve.wait_ge(par_in, 16 * g + 16)
                    dve.tensor_copy(gs[:], stab[:, g])
                    dve.tensor_copy(gt[:], tab[:, g]).then_inc(tabs_ready, 1)
                    dve.wait_ge(tabs_ready, g + 1)
                    dve.wait_ge(stored, g + 1)
                    o(dve.memset(S[:], 0.0))
                    for t in range(CT):
                        self.lo(dve, ((t + 1) % 2, NT * g + t + 1, None))
                        if t == 0:
                            dve.wait_ge(conv_in, 16 * g + 16)
                        conv(t)
                        if t in (1, 2):
                            diagonal(t - 1)
                    dve.wait_ge(spread_done, 2 * g + 2)
                    tri_rhs(0)
                    for q in range(CH):
                        s = slice(q * P, (q + 1) * P)
                        dve.wait_ge(a_done, CH * g + q + 1)
                        xt = tpb[:].rearrange("p (h d) -> p h d", h=HG)
                        dve.tensor_tensor(xdt[:], xt, bc(gt[:, 0, q, :], HD), ALU.mult)
                        dve.tensor_tensor(xde[:], xt, bc(gt[:, 1, q, :], HD), ALU.mult)
                        dve.tensor_copy(btok[:], bcb[:, 0:P])
                        dve.tensor_tensor(cbm[:], bcb[:, P:2 * P], self.triu[:], ALU.mult)
                        for h in range(HG):
                            last = dve.tensor_scalar(L[:, h, :], ab[h // 4][:, (h % 4) * P:(h % 4 + 1) * P],
                                                     gt[:, 2, q, h:h + 1], 0.0, ALU.subtract, ALU.min)
                        last.then_inc(seg_done, 1)
                        self.lo(dve, ((q + 1) % 2, NT * g + CT + q + 1, None))
                        if q < CH - 1:
                            tri_rhs(q + 1)
                        sum_smp(2 * q)
                        dve.wait_ge(exp_done, CH * g + q + 1)
                        o(dve.tensor_copy(cdec[:], eA[:, :, P - 1]))
                        dve.tensor_tensor(L[:], L[:], mid(cbm[:], 1, HG), ALU.mult)
                        dve.tensor_tensor(eA[:], eA[:], mid(cT[:, s], 1, HG), ALU.mult).then_inc(m_ready, 1)
                        dve.wait_ge(b_done, CH * g + q + 1)
                        o(dve.tensor_tensor(S[:], S[:], bc(cdec[:], HD), ALU.mult))
                        dve.tensor_tensor(S[:], S[:], stb[:].rearrange("p (h d) -> p h d", h=HG), ALU.add)
                        for t in range(GT):
                            last = dve.scalar_tensor_tensor(out=xg[:, t, s], in0=xg[:, t, s],
                                                            scalar=gpar[:, GP_D + t:GP_D + t + 1],
                                                            in1=yb[:, t * P:(t + 1) * P],
                                                            op0=ALU.mult, op1=ALU.add)
                        last.then_inc(y_done, 1)
                        dve.wait_ge(y_done, CH * g + q + 2)
                        sum_smp(2 * q + 1)
                    dve.wait_ge(prod_read, NU * g + NU + 1)
                    for t in range(GT):
                        last = dve.scalar_tensor_tensor(out=xg[:, t, TP:T], in0=xg[:, t, TP:T],
                                                        scalar=gpar[:, GP_D + t:GP_D + t + 1],
                                                        in1=ys[:, t, :], op0=ALU.mult, op1=ALU.add)
                    last.then_inc(fin_ready, 1)
                    dve.wait_ge(fin_ready, g + 1)
                    for t in range(GT):
                        dve.wait_ge(gemm_free, 2 * NT * g + 2 * (CT + t) + 4)
                        dve.tensor_tensor(yg[:, t, :], yg[:, t, :], xg[:, t, :],
                                          ALU.mult).then_inc(gated, 1)
                    dve.wait_ge(root_ready, g + 1)
                    o(dve.reciprocal(acc[:, 0, :], acc[:, 0, :]))
                    for t in range(GT):
                        last = dve.scalar_tensor_tensor(out=yg[:, t, :], in0=yg[:, t, :],
                                                        scalar=gpar[:, GP_NW + t:GP_NW + t + 1],
                                                        in1=acc[:, 0, :], op0=ALU.mult, op1=ALU.mult)
                    last.then_inc(group_done, 1)
                    dve.wait_ge(group_done, g + 2)

            @block.gpsimd
            def _(pool):
                o = Order(pool, pord)
                pool.sem_inc(stored, 1)
                pool.sem_inc(y_stored, 1)
                with pool.Fori(0, G) as g, o.body(g, G, SSD_POOL):
                    def load(u):
                        if u >= 2:
                            pool.wait_ge(st_out[u % 2], 64 * g + 16 * (u // 2))
                        self.alone(pool)
                        pool.dma_start(sst[:, u % 2], state_in[GT * g + u // 2, :, HB * (u % 2):HB * (u % 2) + HB, :]
                                       ).then_inc(st_in[u % 2], 16)

                    pool.wait_ge(group_done, g + 1)
                    self.alone(pool)
                    pool.dma_start(gpar[:], a["g_par"][g]).then_inc(par_in, 16)
                    pool.dma_start(scv[:, 0:3], a["state_conv"][g]).then_inc(conv_in, 16)
                    load(0)
                    pool.wait_ge(tabs_ready, g + 1)
                    for u in range(NU):
                        t, b0 = u // 2, HB * (u % 2)
                        s = sst[:, u % 2]
                        if u < NU - 1:
                            load(u + 1)
                        if u == 4:
                            pool.wait_ge(conv_done, CT * g + CT + 2)
                            self.alone(pool)
                            pool.dma_start(out["conv_sample"][g], scv[:, 1:4]).then_inc(conv_out, 16)
                            pool.dma_start(out["conv_prompt"][g], cpo[:]).then_inc(conv_out, 16)
                        if u == 0:
                            pool.wait_ge(spread_read, 2 * g + 3)
                        if u % 2 == 0:
                            pool.wait_ge(silu_done, CT * g + t + 5)
                        pool.wait_ge(st_in[u % 2], 64 * g + 16 * (u // 2) + 16)
                        if u % 2 == 0:
                            o(pool.tensor_tensor(gs[:, 0, t, :], gs[:, 0, t, :], xg[:, t, TP:T], ALU.mult))
                        pool.tensor_tensor(s, s, bc(gs[:, 1, t, b0:b0 + HB], NST), ALU.mult)
                        pool.wait_ge(prod_read, NU * g + u + 1)
                        o(pool.tensor_tensor(stmp[:], Bb[:, b0:b0 + HB, :], bc(gs[:, 0, t, b0:b0 + HB], NST),
                                             ALU.mult))
                        o(pool.tensor_tensor(s, s, stmp[:], ALU.add))
                        self.alone(pool)
                        pool.dma_start(state_out[GT * g + t, :, b0:b0 + HB, :], s).then_inc(st_out[u % 2], 16)
                        pool.tensor_tensor(stmp[:], s, Cb[:, b0:b0 + HB, :], ALU.mult).then_inc(prod_ready, 1)
                        pool.wait_ge(prod_ready, NU * g + u + 1)
                    pool.wait_ge(fin_ready, g + 1)
                    self.alone(pool)
                    pool.dma_start(out["ssm_prompt"][g], S[:].rearrange("p h d -> p (h d)")).then_inc(fin_out, 16)
                    pool.wait_ge(fin_out, 16 * g + 16)
                    pool.wait_ge(conv_out, 32 * g + 32)
                    for j in range(2):
                        pool.wait_ge(st_out[j], 64 * g + 64)
                    pool.sem_inc(stored, 1)
                    pool.wait_ge(group_done, g + 2)
                    self.alone(pool)
                    pool.dma_start(self.ys.rearrange("n p t -> p n t")[:, bass.ds(GT * g, GT), :], yg).then_inc(y_out, 16)
                    pool.wait_ge(y_out, 16 * g + 16)
                    pool.sem_inc(y_stored, 1)

    def ln_pe(self, pe, v, square, s):
        mu, var = self.bank[2:4], self.bank[4:6]
        for n in range(FT):
            pe.wait_ge(s["in"], n + 1)
            for h in range(2):
                last = pe.matmul(mu[h][:, 0:H2], self.onesD[:], v[:, n, h * H2:(h + 1) * H2],
                                 start=(n == 0), stop=(n == FT - 1))
        last.then_inc(s["mean"], 1)
        for n in range(FT):
            pe.wait_ge(s["square"], n + 1)
            for h in range(2):
                last = pe.matmul(var[h][:, 0:H2], self.onesD[:], square[:, n % 2, h * H2:(h + 1) * H2],
                                 start=(n == 0), stop=(n == FT - 1))
            last.then_inc(s["summed"], 1)

    def ln_act(self, act, v, square, root, s):
        for n in range(FT):
            act.wait_ge(s["centred"], n + 1)
            if n >= 2:
                act.wait_ge(s["summed"], n - 1)
            act.activation(square[:, n % 2, :], v[:, n, :], ACT.Square).then_inc(s["square"], 1)
        act.wait_ge(s["summed"], FT)
        for h in range(2):
            last = act.activation(root[:, h * H2:(h + 1) * H2], self.bank[4 + h][:, 0:H2], ACT.Sqrt,
                                  bias=self.eps[:])
        last.then_inc(s["root"], 1)

    def ln_dve(self, dve, v, root, g, b, s, after=None):
        mu = self.bank[2:4]
        dve.wait_ge(s["mean"], 1)
        for n in range(FT):
            for h in range(2):
                last = dve.tensor_tensor(v[:, n, h * H2:(h + 1) * H2], v[:, n, h * H2:(h + 1) * H2],
                                         mu[h][:, 0:H2], ALU.subtract)
            last.then_inc(s["centred"], 1)
        dve.wait_ge(s["root"], 1)
        dve.reciprocal(root[:], root[:]).then_inc(s["inv"], 1)
        dve.wait_ge(s["inv"], 1)
        for n in range(FT):
            dve.tensor_tensor(v[:, n, :], v[:, n, :], root[:], ALU.mult).then_inc(s["inv"], 1)
            dve.wait_ge(s["inv"], n + 2)
            dve.tensor_scalar(v[:, n, :], v[:, n, :], g[:, n:n + 1], b[:, n:n + 1],
                              ALU.mult, ALU.add).then_inc(s["normed"], 1)
            if after:
                after(n)

    def ln_sems(self, name):
        return {n: self.sem(f"{name}_{n}") for n in ("in", "mean", "square", "summed", "centred", "root", "inv", "normed")}

    def sgu(self, v):
        nc, a, out = self.nc, self.a, self.o
        with ExitStack() as st:
            sb = lambda name, shape, dt=F32: st.enter_context(nc.sbuf_tensor(name, shape, dt))
            ub = sb("u_gated", [P, 2, T])
            root = sb("v_root", [P, T])
            square = sb("v_square", [P, 2, T])
            vst = sb("v_staged", [P, TP])
            vtok = sb("v_tok", [P, CH, P])
            ws = sb("w_spatial", [P, FT, P])
            bs = sb("b_spatial", [P, FT, P])
            w0 = sb("w_spatial0", [P, 2, FT])
            S_ = lambda *names: [self.sem("g_" + n) for n in names]
            par_in, v_out, masked, staged, turned, tok_ready, mixed, mix_free, gate_done, y_out, ub_free = S_(
                "par_in", "v_out", "masked", "staged", "turned", "tok_ready", "mixed",
                "mix_free", "gate_done", "y_out", "ub_free")
            dord, = S_("dve")
            ln = self.ln_sems("vln")
            gb, tb, mb = self.bank[0:2], self.bank[6], self.bank[7]
            with nc.Block() as block:
                @block.sync
                def _(sp):
                    sp.dma_start(w0[:], a["sgu_first"]).then_inc(par_in, 16)
                    sp.dma_start(ws[:], a["sgu_wT"]).then_inc(par_in, 16)
                    sp.dma_start(bs[:], a["sgu_b"]).then_inc(par_in, 16)
                    self.stream(sp, O_V, 2 * FT)

                @block.gpsimd
                def _(pool):
                    pool.sem_inc(ub_free, 2)
                    pool.wait_ge(ln["normed"], FT)
                    pool.dma_start(out["v_last"], v[:, :, TP - P:T]).then_inc(v_out, 16)
                    with pool.Fori(0, FT // 2) as i:
                        for j in range(2):
                            n = 2 * i + j
                            pool.wait_ge(gate_done, n + 1)
                            self.alone(pool)
                            pool.dma_start(self.ys[n + G * GT], ub[:, j, :]).then_inc(y_out, 16)
                            pool.wait_ge(y_out, 16 * n + 16)
                            pool.sem_inc(ub_free, 1)
                    pool.wait_ge(v_out, 16)

                @block.tensor
                def _(pe):
                    pe.sem_inc(mixed, 1)
                    pe.sem_inc(turned, 1)
                    self.gemms(pe, O_V, FT)
                    self.ln_pe(pe, v, square, ln)
                    with pe.Fori(0, FT // 2) as i:
                        for j in range(2):
                            n = 2 * i + j

                            def turn():
                                pe.wait_ge(staged, n + 1)
                                for c in range(CH):
                                    last = pe.transpose(tb[:, c * P:(c + 1) * P], vst[:, c * P:(c + 1) * P],
                                                        self.ident[:])
                                last.then_inc(turned, 1)

                            self.gemm(pe, 2 * i + (O_U + j), j, between=turn)
                            pe.wait_ge(tok_ready, n + 1)
                            pe.wait_ge(masked, 1)
                            pe.wait_ge(mix_free, n + 1)
                            for c in range(CH):
                                last = pe.matmul(mb[:, c * P:(c + 1) * P], vtok[:, c, :],
                                                 ws[:, n, :], start=True, stop=True)
                            last.then_inc(mixed, 1)

                @block.scalar
                def _(act):
                    def gelu_v(n, j, nxt):
                        self.hi(act, nxt)
                        for h in range(2):
                            act.wait_ge(self.gemm_ready, 2 * n + (READY0 + 2 * O_V + 1 + h))
                            self.alone(act)
                            act.activation(v[:, n, h * H2:(h + 1) * H2], gb[h][:, 0:H2],
                                           ACT.Gelu).then_inc(self.gemm_free, 1)
                        act.wait_ge(self.gemm_free, 2 * n + (2 * O_V + 4))
                        act.sem_inc(ln["in"], 1)

                    def gelu_u(n, j, nxt):
                        self.hi(act, nxt)
                        act.wait_ge(ub_free, n + 1)
                        for h in range(2):
                            act.wait_ge(self.gemm_ready, 2 * n + (READY0 + 2 * O_U + 1 + h))
                            act.activation(ub[:, j, h * H2:(h + 1) * H2], gb[h][:, 0:H2],
                                           ACT.Gelu).then_inc(self.gemm_free, 1)
                            if h == 0:
                                act.wait_ge(turned, n + 2)
                                act.wait_ge(mixed, n + 1)
                                act.copy(vtok[:].rearrange("p c d -> p (c d)"), tb[:]).then_inc(tok_ready, 1)

                    self.turns(act, O_V, FT, gelu_v)
                    self.ln_act(act, v, square, root, ln)
                    self.turns(act, O_U, FT, gelu_u)

                @block.vector
                def _(dve):
                    dve.sem_inc(mix_free, 1)
                    dve.wait_ge(par_in, 48)
                    dve.tensor_tensor(ws[:], ws[:], mid(self.triu[:], 1, FT), ALU.mult).then_inc(masked, 1)
                    self.turns(dve, O_V, FT, lambda n, j, nxt: self.lo(dve, nxt))
                    self.ln_dve(dve, v, root, self.lnp[:, 0, :], self.lnp[:, 1, :], ln)
                    o = Order(dve, dord)
                    dve.wait_ge(ln["normed"], FT)
                    with dve.Fori(0, FT // 2) as i, o.body(i, FT // 2, 2):
                        for j in range(2):
                            n = 2 * i + j
                            self.lo(dve, self.next_tile(O_U, i, j))
                            dve.wait_ge(turned, n + 1)
                            dve.tensor_copy(vst[:], v[:, n, 0:TP]).then_inc(staged, 1)
                            o(dve.tensor_tensor(root[:, TP:T], v[:, n, TP:T],
                                                w0[:, 0, bass.ds(n, 1)].to_broadcast([P, NS]), ALU.mult))
                            dve.tensor_tensor(root[:, TP:T], root[:, TP:T],
                                              w0[:, 1, bass.ds(n, 1)].to_broadcast([P, NS]), ALU.add)
                            dve.wait_ge(mixed, n + 2)
                            dve.tensor_tensor(root[:, 0:TP].rearrange("p (c i) -> p c i", c=CH),
                                              mb.rearrange("p (c i) -> p c i", c=CH),
                                              bs[:, bass.ds(n, 1), :].to_broadcast([P, CH, P]),
                                              ALU.add).then_inc(mix_free, 1)
                            dve.wait_ge(mix_free, n + 2)
                            dve.wait_ge(self.gemm_free, 2 * n + (2 * O_U + 4))
                            dve.tensor_tensor(ub[:, j, :], ub[:, j, :], root[:], ALU.mult).then_inc(gate_done, 1)
                            dve.wait_ge(gate_done, n + 1)

    def gate_phase(self):
        nc = self.nc
        with ExitStack() as st:
            stage = st.enter_context(nc.sbuf_tensor("gate_stage", [P, 2, T], F32))
            gate_out, stage_free = self.sem("s_gate_out"), self.sem("s_gate_free")
            with nc.Block() as block:
                @block.sync
                def _(sp):
                    self.stream(sp, O_GATE, 2 * FT)

                @block.tensor
                def _(pe):
                    self.gemms(pe, O_GATE, 2 * FT)

                @block.scalar
                def _(act):
                    def sigmoid(n, j, nxt):
                        self.hi(act, nxt)
                        act.wait_ge(stage_free, n + 1)
                        for h in range(2):
                            act.wait_ge(self.gemm_ready, 2 * n + (READY0 + 2 * O_GATE + 1 + h))
                            act.activation(stage[:, j, h * H2:(h + 1) * H2], self.bank[h][:, 0:H2],
                                           ACT.Sigmoid).then_inc(self.gemm_free, 1)

                    self.turns(act, O_GATE, 2 * FT, sigmoid)

                @block.vector
                def _(dve):
                    self.turns(dve, O_GATE, 2 * FT, lambda n, j, nxt: self.lo(dve, nxt))

                @block.gpsimd
                def _(pool):
                    pool.sem_inc(stage_free, 2)
                    with pool.Fori(0, FT) as i:
                        for j in range(2):
                            n = 2 * i + j
                            pool.wait_ge(self.gemm_free, 2 * n + (2 * O_GATE + 4))
                            self.alone(pool)
                            pool.dma_start(self.gates_dram[n], stage[:, j, :]).then_inc(gate_out, 16)
                            pool.wait_ge(gate_out, 16 * n + 16)
                            pool.sem_inc(stage_free, 1)

    def branches(self, merged):
        nc = self.nc
        with ExitStack() as st:
            sb = lambda name, shape: st.enter_context(nc.sbuf_tensor(name, shape, F32))
            y = sb("branch_in", [P, KB, T])
            gate = sb("gate_ring", [P, 2, T])
            S_ = lambda *names: [self.sem("b_" + n) for n in names]
            hi_done, split, gate_used = S_("y_hi", "y_split", "gate_used")
            NQ = 4
            y_in = [self.sem(f"b_y_in{i}") for i in range(NQ)]
            gate_in = [self.sem(f"b_gate_in{j}") for j in range(2)]
            passes = range(3)
            with nc.Block() as block:
                @block.sync
                def _(sp):
                    self.stream(sp, O_BR, 3 * FT)

                @block.gpsimd
                def _(pool):
                    def load_y(p):
                        for i in range(NQ):
                            s = slice(NQ * i, NQ * (i + 1))
                            src = self.ys[FT * p + NQ * i:FT * p + NQ * (i + 1)]
                            pool.dma_start(y[:, s, :], src.rearrange("k p t -> p k t")).then_inc(y_in[i], 16)

                    load_y(0)
                    for p in passes:
                        if p < 2:
                            pool.wait_ge(split, KB * (p + 1))
                            load_y(p + 1)
                        with pool.Fori(0, FT // 2) as i:
                            for j in range(2):
                                pool.wait_ge(gate_used, 2 * i + (FT * p + j + 1))
                                self.alone(pool)
                                src = self.gates_dram[2 * i + (j if p < 2 else FT + j)]
                                pool.dma_start(gate[:, j, :], src).then_inc(gate_in[j], 16)

                @block.tensor
                def _(pe):
                    for p in passes:
                        self.gemms(pe, O_BR + FT * p, FT, (split, KB * p))

                @block.scalar
                def _(act):
                    for p in passes:
                        act.wait_ge(self.gemm_ready, READY0 + 2 * (O_BR + FT * p))
                        self.split_hi(act, y, hi_done, lambda k: (y_in[k // NQ], 16 * p + 16))
                        self.turns(act, O_BR + FT * p, FT, lambda n, j, nxt: self.hi(act, nxt))

                @block.vector
                def _(dve):
                    dve.sem_inc(gate_used, 2)
                    for p in passes:
                        self.split_lo(dve, y, hi_done, split, KB * p)
                        first = O_BR + FT * p
                        with dve.Fori(0, FT // 2) as i:
                            for j in range(2):
                                n = 2 * i + j
                                self.lo(dve, self.next_tile(first, i, j))
                                dve.wait_ge(gate_in[j], 16 * i + (8 * FT * p + 16))
                                for h in range(2):
                                    s = slice(h * H2, (h + 1) * H2)
                                    m = merged[:, n, s]
                                    dve.wait_ge(self.gemm_ready, 2 * n + (READY0 + 2 * first + 1 + h))
                                    dve.tensor_tensor(m if p == 0 else gate[:, j, s], gate[:, j, s],
                                                      self.bank[h][:, 0:H2], ALU.mult).then_inc(self.gemm_free, 1)
                                    dve.wait_ge(self.gemm_free, 2 * n + (2 * first + 3 + h))
                                    if p:
                                        last = dve.tensor_tensor(m, m, gate[:, j, s], ALU.add)
                                if p:
                                    last.then_inc(gate_used, 1)
                                    dve.wait_ge(gate_used, n + (FT * p + 3))
                                else:
                                    dve.sem_inc(gate_used, 1)

    def project_out(self, merged, htok):
        nc = self.nc
        with ExitStack() as st:
            sb = lambda name, shape: st.enter_context(nc.sbuf_tensor(name, shape, F32))
            h = sb("h", [P, KB, T])
            root = sb("h_root", [P, T])
            square = sb("h_square", [P, 2, T])
            S_ = lambda *names: [self.sem("o_" + n) for n in names]
            x_in, hi_done, split, turned, turn_read = S_("x_in", "hi", "split", "turned", "turn_read")
            gb, tb = self.bank[0:2], self.bank[6:8]
            ln = self.ln_sems("hln")
            tokens = lambda b: slice(b * P, min((b + 1) * P, T))
            rows = lambda b: min((b + 1) * P, T) - b * P
            with nc.Block() as block:
                @block.sync
                def _(sp):
                    sp.dma_start(h[:], self.a["xT"]).then_inc(x_in, 16)
                    self.stream(sp, O_OUT, FT)

                @block.tensor
                def _(pe):
                    self.gemms(pe, O_OUT, FT, (split, 0))
                    self.ln_pe(pe, h, square, ln)
                    for c in range(FT // 4):
                        pe.wait_ge(ln["normed"], 4 * c + 4)
                        for b in range(NB):
                            m = NB * c + b
                            if m >= 2:
                                pe.wait_ge(turn_read, m - 1)
                            for t in range(4):
                                last = pe.transpose(tb[m % 2][0:rows(b), t * P:(t + 1) * P],
                                                    h[:, 4 * c + t, tokens(b)], self.ident[:])
                            last.then_inc(turned, 1)

                @block.scalar
                def _(act):
                    self.split_hi(act, merged, hi_done)
                    self.turns(act, O_OUT, FT, lambda n, j, nxt: self.hi(act, nxt))
                    self.ln_act(act, h, square, root, ln)
                    for c in range(FT // 4):
                        for k in range(4 * c, 4 * c + 4):
                            act.wait_ge(ln["normed"], k + 1)
                            act.copy(self.ah[:, k, :], h[:, k, :]).then_inc(hi_done, 1)
                        for b in range(NB):
                            m = NB * c + b
                            act.wait_ge(turned, m + 1)
                            act.copy(htok[0:rows(b), b, 512 * c:512 * (c + 1)],
                                     tb[m % 2][0:rows(b), :]).then_inc(turn_read, 1)

                @block.vector
                def _(dve):
                    self.split_lo(dve, merged, hi_done, split)
                    dve.wait_ge(x_in, 16)
                    with dve.Fori(0, FT // 2) as i:
                        for j in range(2):
                            n = 2 * i + j
                            self.lo(dve, self.next_tile(O_OUT, i, j))
                            for hf in range(2):
                                m = h[:, n, hf * H2:(hf + 1) * H2]
                                dve.wait_ge(self.gemm_ready, 2 * n + (READY0 + 2 * O_OUT + 1 + hf))
                                dve.scalar_tensor_tensor(out=m, in0=m, scalar=ALPHA, in1=gb[hf][:, 0:H2],
                                                         op0=ALU.mult, op1=ALU.add).then_inc(self.gemm_free, 1)
                            dve.wait_ge(self.gemm_free, 2 * n + (2 * O_OUT + 4))
                            dve.sem_inc(ln["in"], 1)

                    def lo_h(n):
                        dve.wait_ge(hi_done, KB + n + 1)
                        dve.tensor_tensor(self.al[:, n, :], h[:, n, :], self.ah[:, n, :].bitcast(F32),
                                          ALU.subtract).then_inc(split, 1)

                    LAG = 6
                    self.ln_dve(dve, h, root, self.lnp[:, 2, :], self.lnp[:, 3, :], ln,
                                lambda n: lo_h(n - LAG) if n >= LAG else None)
                    for n in range(FT - LAG, FT):
                        lo_h(n)

    def query(self, eid, gates, eidT, gatesT):
        nc, a = self.nc, self.a
        HH = 2 * PH
        with ExitStack() as st:
                sb = lambda name, shape, dt=F32: st.enter_context(nc.sbuf_tensor(name, shape, dt))
                keys = sb("keys", [P, HH, P])
                qb = sb("q", [P, 2, T])
                work, cand = sb("work", [P, NB, P]), sb("cand", [P, NB, TOPK * TOPK])
                tv, ti = sb("top_s", [P, NB, 2, TOPK]), sb("top_i", [P, NB, 2, TOPK], U32)
                bv, bi = sb("best_s", [P, NB, TOPK]), sb("best_c", [P, NB, TOPK], U32)
                bvs, bis = sb("best_s_all", [P, NB, PH, TOPK]), sb("best_c_all", [P, NB, PH, TOPK], U32)
                tis = sb("top_i_all", [P, NB, PH, 2, TOPK])
                code = sb("code", [P, NB, PH * TOPK], U32)
                pick = sb("pick", [P, 2, NB, PH * TOPK])
                hot = self.w_raw[:, 0, :].rearrange("p (k i) -> p k i", i=TOPK)
                side = sb("side", [P, 2, NB, PH * TOPK])
                gsum = sb("gate_sum", [P, NB, PH])
                iota = sb("iota16", [P, TOPK])
                S_ = lambda *names: [self.sem("q_" + n) for n in names]
                gemm_ready, gemm_free = self.gemm_ready, self.gemm_free
                (keys_in, q_ready, scored, score_read, head_done,
                 iota_ready, exp_ready, exp_done, smp_ready, smp_turned) = S_(
                    "keys_in", "q_ready", "scored",
                    "score_read", "head_done", "iota_ready", "exp_ready", "exp_done", "smp_ready", "smp_turned")
                dord, = S_("dve")
                gb = self.bank[0:2]
                tokens = lambda b: slice(b * P, min((b + 1) * P, T))
                rows = lambda b: min((b + 1) * P, T) - b * P

                with nc.Block() as block:
                    @block.sync
                    def _(sp):
                        sp.dma_start(keys[:], a["keys"]).then_inc(keys_in, 16)
                        self.stream(sp, O_Q, FT)

                    @block.gpsimd
                    def _(pool):
                        pool.iota(iota[:], pattern=[[1, TOPK]], base=0, channel_multiplier=0,
                                  allow_small_or_imprecise_dtypes=True).then_inc(iota_ready, 1)
                        self.turns(pool, O_Q, FT, lambda n, j, nxt: self.lo(pool, nxt) if nxt else None)

                    @block.tensor
                    def _(pe):
                        pe.sem_inc(scored, 2)
                        pe.wait_ge(keys_in, 16)

                        def score(n, j):
                            pe.wait_ge(q_ready, 2 * n + 2)
                            pe.wait_ge(score_read, n + 1)
                            s = self.bank[2 + 2 * j:4 + 2 * j]
                            for b in range(NB):
                                o = s[0][:, b * P:(b + 1) * P] if b < CH else s[1][0:NS, 0:P]
                                last = pe.matmul(o, qb[:, j, tokens(b)], keys[:, n, :],
                                                 start=True, stop=True)
                            last.then_inc(scored, 1)

                        self.gemm(pe, O_Q, 0)
                        self.gemm(pe, O_Q + 1, 1, between=lambda: score(0, 0))
                        with pe.Fori(0, FT // 2 - 1) as i:
                            for j in range(2):
                                self.gemm(pe, 2 * i + (O_Q + 2 + j), j,
                                          between=lambda: score(2 * i + (1 + j), (1 + j) % 2))
                        score(HH - 1, 1)
                        pe.wait_ge(smp_ready, 1)
                        pe.transpose(self.bank[6][:, 0:NS], side[0:NS, 0, CH, :], self.ident[0:NS, 0:NS])
                        pe.transpose(self.bank[6][:, NS:2 * NS], gates[0:NS, CH, :],
                                     self.ident[0:NS, 0:NS]).then_inc(smp_turned, 1)

                    @block.scalar
                    def _(act):
                        def queries(n, j, nxt):
                            if nxt:
                                self.hi(act, nxt)
                            act.wait_ge(scored, n + 1)
                            for h in range(2):
                                act.wait_ge(gemm_ready, 2 * n + (READY0 + 2 * O_Q + 1 + h))
                                act.copy(qb[:, j, h * H2:(h + 1) * H2], gb[h][:, 0:H2]).then_inc(q_ready, 1)
                            act.wait_ge(q_ready, 2 * n + 2)
                            act.sem_inc(gemm_free, 2)

                        self.turns(act, O_Q, FT, queries)
                        act.wait_ge(exp_ready, 1)
                        act.activation(gates[:], bvs[:].rearrange("p b h k -> p b (h k)"), ACT.Exp
                                       ).then_inc(exp_done, 1)

                    @block.vector
                    def _(dve):
                        o = Order(dve, dord)
                        for x in (tv, ti, bv, bi, work, cand):
                            ins = dve.memset(x[:], 0)
                        o(ins)
                        dve.sem_inc(score_read, 2)

                        def after(ins):
                            o(ins)
                            self.alone(dve)

                        def top16(src, wk, vals, idx):
                            for s_, w_, v_, x_ in zip(src, wk, vals, idx):
                                ins = dve.max(v_[:, 0:8], s_)
                            after(ins)
                            for s_, w_, v_, x_ in zip(src, wk, vals, idx):
                                dve.max_index(x_[:, 0:8], v_[:, 0:8], s_)
                                ins = dve.match_replace(w_, v_[:, 0:8], s_, NEG)
                            after(ins)
                            for s_, w_, v_, x_ in zip(src, wk, vals, idx):
                                ins = dve.max(v_[:, 8:16], w_)
                            after(ins)
                            for s_, w_, v_, x_ in zip(src, wk, vals, idx):
                                ins = dve.max_index(x_[:, 8:16], v_[:, 8:16], w_)
                            return ins

                        with dve.Fori(0, PH) as h, o.body(h, PH, 14):
                            for s in range(2):
                                dve.wait_ge(scored, 2 * h + s + 3)
                                self.alone(dve)
                                bk = self.bank[2 + 2 * s:4 + 2 * s]
                                top16([bk[0][:, b * P:(b + 1) * P] if b < CH else bk[1][0:NS, 0:P] for b in range(NB)],
                                      [work[0:rows(b), b, :] for b in range(NB)],
                                      [tv[0:rows(b), b, s, :] for b in range(NB)],
                                      [ti[0:rows(b), b, s, :] for b in range(NB)]).then_inc(score_read, 1)
                                dve.wait_ge(score_read, 2 * h + s + 3)
                            for b in range(NB):
                                dve.tensor_copy(tis[:, b, h], ti[:, b])
                                ins = dve.tensor_tensor(cand[:, b].rearrange("p (i j) -> p i j", i=TOPK),
                                                        bc(tv[:, b, 0, :], TOPK), mid(tv[:, b, 1, :], 1, TOPK), ALU.add)
                            after(ins)
                            o(top16([cand[0:rows(b), b, :] for b in range(NB)], [cand[0:rows(b), b, :] for b in range(NB)],
                                    [bv[0:rows(b), b, :] for b in range(NB)], [bi[0:rows(b), b, :] for b in range(NB)]))
                            dve.tensor_copy(bvs[:, :, h, :], bv[:])
                            o(dve.tensor_copy(bis[:, :, h, :], bi[:]))
                            o(dve.tensor_scalar(bv[:], bv[:], 0.0, None, ALU.mult))
                            o(dve.tensor_scalar(work[:], work[:], 0.0, None, ALU.mult))

                        for b in range(NB):
                            ins = dve.tensor_tensor(pick[:, 0, b].rearrange("p (h k) -> p h k", h=PH), bvs[:, b],
                                                    bvs[:, b, :, 0:1].to_broadcast([P, PH, TOPK]), ALU.subtract)
                        o(ins)
                        dve.tensor_copy(bvs[:].rearrange("p b h k -> p b (h k)"), pick[:, 0]).then_inc(exp_ready, 1)
                        dve.wait_ge(exp_ready, 1)
                        bcode = bis[:].rearrange("p b h k -> p b (h k)")
                        for s, (op, by) in enumerate(((ALU.logical_shift_right, 4), (ALU.bitwise_and, TOPK - 1))):
                            o(dve.tensor_scalar(code[:], bcode, by, None, op))
                            o(dve.tensor_copy(pick[:, s], code[:]))
                        dve.wait_ge(iota_ready, 1)
                        dve.wait_ge(self.w_split, N_TILES)
                        for b in range(NB):
                            for s in range(2):
                                o(dve.tensor_tensor(hot, bc(pick[:, s, b], TOPK), mid(iota[:], 1, PH * TOPK),
                                                    ALU.is_equal))
                                h4 = hot.rearrange("p (h k) i -> p h k i", h=PH)
                                o(dve.tensor_tensor(h4, h4, mid(tis[:, b, :, s, :], 2, TOPK), ALU.mult))
                                o(dve.tensor_reduce(side[:, s, b], hot, AX_X, ALU.add))
                        o(dve.scalar_tensor_tensor(out=side[:, 0], in0=side[:, 0], scalar=float(P), in1=side[:, 1],
                                                   op0=ALU.mult, op1=ALU.add))
                        o(dve.tensor_copy(eid[:], side[:, 0]))
                        dve.wait_ge(exp_done, 1)
                        gv = gates[:].rearrange("p b (h k) -> p b h k", h=PH)
                        for b in range(NB):
                            ins = dve.tensor_reduce(gsum[:, b], gv[:, b], AX_X, ALU.add)
                        o(ins)
                        o(dve.reciprocal(gsum[:], gsum[:]))
                        for b in range(NB):
                            ins = dve.tensor_tensor(gv[:, b], gv[:, b], bc(gsum[:, b], TOPK), ALU.mult)
                        ins.then_inc(smp_ready, 1)
                        dve.wait_ge(smp_turned, 1)
                        dve.tensor_copy(eidT[:], self.bank[6][:, 0:NS])
                        o(dve.tensor_copy(gatesT[:], self.bank[6][:, NS:2 * NS]))

    def experts(self, htok, eid, gates, eidT, gatesT):
        nc, a, out = self.nc, self.a, self.o
        NR = 8
        HR = NR // 2
        NJ = P // NR
        with ExitStack() as st:
            sb = lambda name, shape, dt=F32: st.enter_context(nc.sbuf_tensor(name, shape, dt))
            rows = sb("rows", [P, 2 * NR, D])
            urow = [rows[:, i, :] for i in range(NR)]
            vrow = [rows[:, NR + i, :] for i in range(NR)]
            acc = sb("acc", [P, D])
            ln2 = sb("ln2", [P, 2, D])
            dots, ge, coef = sb("dots", [P, NR]), sb("gelu", [P, NR]), sb("coef", [P, NR])
            iu, iv = sb("index_u", [P, NR], U32), sb("index_v", [P, NR], U32)
            sel = sb("selector", [NS, NS, P])
            onehot = sb("onehot8", [P, NS, NS])
            coefm = sb("coef_smp", [P, NS, NS])
            stats, mv = sb("bn_stats", [P, 4, 6]), sb("bn_mv", [P, 2])
            rstd = sb("rstd", [P, 1])
            S_ = lambda *names: [self.sem("e_" + n) for n in names]
            u_in = [self.sem(f"e_u{j}") for j in range(NR)]
            v_in = [self.sem(f"e_v{j}") for j in range(NR)]
            (ln2_in, masks, h_spread, smp_dots, smp_gelu, smp_coef, smp_mixed, dot_done, gelu_done, acc_done,
             var_ready, root_ready, y_ready, y_out) = S_(
                "ln2_in", "masks", "h_spread", "smp_dots", "smp_gelu", "smp_coef", "smp_mixed", "dot_done",
                "gelu_done", "acc_done", "var_ready", "root_ready", "y_ready", "y_out")
            dord, lord, pord, qord = S_("dve", "dve_ln", "pool", "pool_idx")
            gather = lambda pool, dst, table, idx: pool.indirect_dma_start(
                out=dst, out_offset=None, in_=table, in_offset=bass.IndirectOffsetOnAxis(ap=idx, axis=0))

            def norm(dve, o, rows, n):
                x = acc[0:rows, :]
                for c in range(4):
                    ins = dve.bn_stats(stats[0:rows, c, :], x[:, 512 * c:512 * (c + 1)])
                o(ins)
                self.alone(dve)
                dve.bn_aggr(mv[0:rows, :], stats[0:rows]).then_inc(var_ready, 1)
                dve.wait_ge(root_ready, n + 1)
                o(dve.reciprocal(rstd[0:rows, :], rstd[0:rows, :]))
                o(dve.tensor_scalar(x, x, mv[0:rows, 0:1], rstd[0:rows, :], ALU.subtract, ALU.mult))
                o(dve.tensor_tensor(x, x, ln2[0:rows, 0, :], ALU.mult))
                dve.tensor_tensor(x, x, ln2[0:rows, 1, :], ALU.add).then_inc(y_ready, 1)

            with nc.Block() as block:
                @block.sync
                def _(sp):
                    sp.dma_start(ln2[:], a["ln2_rows"]).then_inc(ln2_in, 16)
                    sp.wait_ge(y_ready, 1)
                    sp.dma_start(out["y_sample"], acc[0:NS, :]).then_inc(y_out, 16)
                    with sp.Fori(0, CH) as b:
                        sp.wait_ge(y_ready, b + 2)
                        sp.dma_start(out["y_prompt"][b], acc[:]).then_inc(y_out, 16)
                    sp.wait_ge(y_out, 16 * (CH + 1))

                @block.gpsimd
                def _(pool):
                    o = Order(pool, pord)
                    pool.memset(sel[:], 0.0)
                    o(pool.memset(onehot[:], 0.0))
                    pool.affine_select(out=sel[:], in_=sel[:], compare_op=ALU.not_equal, fill=1.0, base=0,
                                       pattern=[[1, NS], [0, P]], channel_multiplier=-1)
                    pool.affine_select(out=onehot[:], in_=onehot[:], compare_op=ALU.not_equal, fill=1.0, base=0,
                                       pattern=[[1, NS], [-1, NS]], channel_multiplier=0).then_inc(masks, 1)
                    for b in range(NS):
                        gather(pool, urow[b], a["peer_u"], eidT[:, b:b + 1]).then_inc(u_in[b], 16)
                    for b in range(NS):
                        gather(pool, vrow[b], a["peer_v"], eidT[:, b:b + 1]).then_inc(v_in[b], 16)
                    o = Order(pool, qord)
                    with pool.Fori(0, CH) as b:
                        with pool.Fori(0, NJ) as j:
                            it = b * NJ + j
                            for table, slots, sem, idx, free in ((a["peer_u"], urow, u_in, iu, dot_done),
                                                                (a["peer_v"], vrow, v_in, iv, acc_done)):
                                for half in range(2):
                                    s = slice(HR * half, HR * (half + 1))
                                    pool.wait_ge(free, 2 * it + half + 1)
                                    self.alone(pool)
                                    ins = pool.tensor_copy(idx[:, s], eid[:, b, bass.ds(NR * j + HR * half, HR)])
                                    ins.then_inc(qord, 1)
                                    n = (0 if table is a["peer_u"] else 2) + half
                                    pool.wait_ge(qord, 4 * it + n + 1)
                                    self.alone(pool)
                                    for k in range(HR * half, HR * (half + 1)):
                                        gather(pool, slots[k], table, idx[:, k:k + 1]).then_inc(sem[k], 16)

                @block.tensor
                def _(pe):
                    pe.wait_ge(masks, 1)
                    for b in range(NS):
                        if b >= 1:
                            pe.wait_ge(smp_dots, b)
                        for c in range(4):
                            last = pe.matmul(self.bank[c], sel[:, b, :], htok[0:NS, CH, 512 * c:512 * (c + 1)],
                                             start=True, stop=True)
                        last.then_inc(h_spread, 1)
                    pe.wait_ge(smp_coef, 1)
                    for b in range(NS):
                        pe.wait_ge(v_in[b], 16)
                        for c in range(4):
                            last = pe.matmul(self.bank[4 + c][0:NS, :], coefm[:, b, :],
                                             vrow[b][:, 512 * c:512 * (c + 1)], start=(b == 0), stop=(b == NS - 1))
                    last.then_inc(smp_mixed, 1)

                @block.scalar
                def _(act):
                    def root(rows, n):
                        act.wait_ge(var_ready, n + 1)
                        act.activation(rstd[0:rows, :], mv[0:rows, 1:2], ACT.Sqrt,
                                       bias=self.eps[0:rows, :]).then_inc(root_ready, 1)

                    act.wait_ge(smp_dots, NS)
                    act.activation(ge[:], dots[:], ACT.Gelu).then_inc(smp_gelu, 1)
                    root(NS, 0)
                    with act.Fori(0, CH) as b:
                        with act.Fori(0, NJ) as j:
                            for half in range(2):
                                s = slice(HR * half, HR * (half + 1))
                                act.wait_ge(dot_done, 2 * (b * NJ + j) + half + 3)
                                act.activation(ge[:, s], dots[:, s], ACT.Gelu).then_inc(gelu_done, 1)
                        root(P, b + 1)

                @block.vector
                def _(dve):
                    o = Order(dve, dord)
                    for b in range(NS):
                        dve.wait_ge(u_in[b], 16)
                        dve.wait_ge(h_spread, b + 1)
                        dve.scalar_tensor_tensor(out=urow[b], in0=urow[b], scalar=1.0,
                                                 in1=self.psum[:, 0:4, :].rearrange("p a b -> p (a b)"),
                                                 op0=ALU.mult, op1=ALU.mult,
                                                 accum_out=dots[:, b:b + 1]).then_inc(smp_dots, 1)
                    dve.wait_ge(smp_dots, NS)
                    dve.sem_inc(dot_done, 2)
                    dve.wait_ge(masks, 1)
                    dve.wait_ge(smp_gelu, 1)
                    o(dve.tensor_tensor(coef[:], ge[:], gatesT[:], ALU.mult))
                    dve.tensor_tensor(coefm[:], onehot[:], bc(coef[:], NS), ALU.mult).then_inc(smp_coef, 1)
                    dve.wait_ge(smp_mixed, 1)
                    dve.sem_inc(acc_done, 2)
                    o(dve.scalar_tensor_tensor(out=acc[0:NS, :], in0=htok[0:NS, CH, :], scalar=ALPHA,
                                               in1=self.psum[0:NS, 4:8, :].rearrange("p a b -> p (a b)"),
                                               op0=ALU.mult, op1=ALU.add))
                    dve.wait_ge(ln2_in, 16)
                    norm(dve, o, NS, 0)
                    lo = Order(dve, lord)
                    acc_order = self.sem("e_acc_order")
                    with dve.Fori(0, CH) as b, lo.body(b, CH, 5):
                        dve.wait_ge(y_out, 16 * b + 16)
                        lo(dve.tensor_scalar(acc[:], htok[:, b, :], ALPHA, None, ALU.mult))
                        self.alone(dve)
                        with dve.Fori(0, NJ) as j:
                            it = b * NJ + j
                            for half in range(2):
                                for k in range(HR * half, HR * (half + 1)):
                                    dve.wait_ge(u_in[k], 16 * it + 32)
                                    last = dve.scalar_tensor_tensor(out=urow[k], in0=urow[k], scalar=1.0,
                                                                    in1=htok[:, b, :], op0=ALU.mult, op1=ALU.mult,
                                                                    accum_out=dots[:, k:k + 1])
                                last.then_inc(dot_done, 1)
                            for half in range(2):
                                s = slice(HR * half, HR * (half + 1))
                                dve.wait_ge(gelu_done, 2 * it + half + 1)
                                dve.tensor_tensor(coef[:, s], ge[:, s], gates[:, b, bass.ds(NR * j + HR * half, HR)],
                                                  ALU.mult).then_inc(acc_order, 1)
                                n = (HR) * half
                                dve.wait_ge(acc_order, NR * it + n + 1)
                                for m, k in enumerate(range(HR * half, HR * (half + 1))):
                                    dve.wait_ge(v_in[k], 16 * it + 32)
                                    ins = dve.scalar_tensor_tensor(out=acc[:], in0=vrow[k], scalar=coef[:, k:k + 1],
                                                                   in1=acc[:], op0=ALU.mult, op1=ALU.add)
                                    if m < HR - 1:
                                        ins.then_inc(acc_order, 1)
                                        dve.wait_ge(acc_order, NR * it + n + m + 2)
                                    else:
                                        ins.then_inc(acc_done, 1)
                                        dve.wait_ge(acc_done, 2 * it + half + 3)
                        norm(dve, lo, P, b + 1)


def build_program(nc, arrays, outputs):
    a = {n: nc.dram_tensor("in_" + n, v.shape, F32, kind="ExternalInput").ap() for n, v in arrays.items()}
    o = {n: nc.dram_tensor("out_" + n, shape, F32, kind="ExternalOutput").ap() for n, shape in outputs.items()}
    k = Kernel(nc, a, o)
    k.ys = nc.dram_tensor("branch_acts", [G * GT + FT, P, T], F32).ap()
    k.gates_dram = nc.dram_tensor("branch_gates", [2 * FT, P, T], F32).ap()
    k.build()


OUTPUTS = {
    "y_prompt": (CH, P, D), "y_sample": (NS, D),
    "conv_prompt": (G, P, CT, 3), "ssm_prompt": (G, P, HG * HD), "v_last": (P, FT, P + NS),
    "conv_sample": (G, P, 3, CT, NS), "ssm_sample": (NS, NH, HD, NST),
}


def conv_layout(w):
    rows, inner = w.shape[0], G * GT * P
    x = w[:, :inner].reshape(rows, G, GT, P)
    b = w[:, inner:inner + G * P].reshape(rows, G, 1, P)
    c = w[:, inner + G * P:].reshape(rows, G, 1, P)
    return np.concatenate([b, c, x], 2).transpose(1, 3, 2, 0)


def conv_unlayout(y):
    rows = y.shape[3]
    y = y.transpose(3, 0, 2, 1)
    return np.concatenate([y[:, :, 2:].reshape(rows, -1), y[:, :, 0].reshape(rows, -1), y[:, :, 1].reshape(rows, -1)], 1)


def weight_tiles(i):
    w_in, wa, wb, wo, wq = (i[n][0] for n in ("w_in", "w_branch_a", "w_branch_b", "w_out", "peer_wq"))
    inner, gn = G * GT * P, G * NST
    z0, x0, b0, c0 = 0, inner, 2 * inner, 2 * inner + gn
    u0 = c0 + gn + NH
    v0, ga0, gb0 = u0 + D, u0 + 2 * D, u0 + 3 * D
    cols = []
    for g in range(G):
        cols += [(w_in, 0, b0 + g * P), (w_in, 0, c0 + g * P)]
        cols += [(w_in, 0, x0 + (GT * g + t) * P) for t in range(GT)]
        cols += [(w_in, 0, z0 + (GT * g + t) * P) for t in range(GT)]
    cols += [(w_in, 0, v0 + n * P) for n in range(FT)]
    cols += [(w_in, 0, u0 + n * P) for n in range(FT)]
    for n in range(FT):
        cols.append((w_in, 0, ga0 + n * P))
    for n in range(FT):
        cols.append((w_in, 0, gb0 + n * P))
    for w, r in ((wa, 0), (wa, D), (wb, 0)):
        cols += [(w, r, n * P) for n in range(FT)]
    cols += [(wo, 0, n * P) for n in range(FT)]
    cols += [(wq, 0, n * P) for n in range(FT)]
    out = np.empty((len(cols), P, WCOLS), np.float32)
    for n, (w, r, c) in enumerate(cols):
        out[n].reshape(P, KB, P)[:] = w[r:r + D, c:c + P].reshape(KB, P, P).transpose(1, 0, 2)
    return out


def kernel(**inputs):
    import concourse.bacc as bacc
    from concourse.bass_utils import run_bass_kernel_spmd

    i = {n: np.asarray(v) for n, v in inputs.items()}
    x = np.concatenate([i["x_prompt"][0], i["x_sample"][:, 0]], 0)
    cols = lambda v: v.reshape(FT, P).T
    dt0 = 2 * G * GT * P + 2 * G * NST
    wdt = i["w_in"][0][:, dt0:dt0 + NH]
    per_head = np.broadcast_to(i["d_skip"][0].reshape(G, GT, 2, 1), (G, GT, 2, HD)).reshape(G, GT, P)
    twice = lambda v: np.concatenate([v, v])[:, None]
    rowP = lambda v: np.broadcast_to(v[None], (P,) + v.shape)
    taps = conv_layout(i["conv_w"][0])
    arrays = {
        "w_tiles": weight_tiles(i),
        "xT": x.T.reshape(KB, P, T).transpose(1, 0, 2),
        "w_dt": wdt.reshape(KB, P, NH).transpose(1, 0, 2),
        "dt_rows": np.concatenate([rowP(i["dt_bias"][0]), rowP(i["a_log"][0]),
                                   twice(i["dt_bias"][0]), twice(i["a_log"][0])], 1),
        "ln_cols": np.stack([cols(i[n][0]) for n in ("sgu_ln_g", "sgu_ln_b", "ln1_g", "ln1_b")], 1),
        "g_par": np.concatenate([taps.reshape(G, P, CT * 4), conv_layout(i["conv_b"])[..., 0],
                                 i["ssd_norm_w"][0].reshape(G, GT, P).transpose(0, 2, 1),
                                 per_head.transpose(0, 2, 1)], 2),
        "state_conv": conv_layout(i["state_conv"][0].reshape(NS * 3, -1)).reshape(G, P, CT, NS, 3)
                      .transpose(0, 1, 4, 2, 3),
        "state_ssm": i["state_ssm"][0],
        "sgu_wT": i["sgu_w"][0].transpose(2, 0, 1),
        "sgu_b": rowP(i["sgu_b"][0]),
        "sgu_first": rowP(np.stack([i["sgu_w"][0][:, 0, 0], i["sgu_b"][0][:, 0]])),
        "keys": i["peer_keys"][0].reshape(2 * PH, P, P).transpose(2, 0, 1),
        "ln2_rows": rowP(np.stack([i["ln2_g"][0], i["ln2_b"][0]])),
        "peer_u": i["peer_u"][0],
        "peer_v": i["peer_v"][0],
    }
    arrays = {n: np.ascontiguousarray(v) for n, v in arrays.items()}
    nc = bacc.Bacc("TRN2", target_bir_lowering=False, num_devices=1)
    build_program(nc, arrays, OUTPUTS)
    r = run_bass_kernel_spmd(nc, [{"in_" + n: v for n, v in arrays.items()}], core_ids=[0]).results[0]
    r = {n: np.asarray(r["out_" + n]) for n in OUTPUTS}
    conv_s = conv_unlayout(r["conv_sample"].transpose(0, 1, 3, 4, 2).reshape(G, P, CT, NS * 3))
    ssm_p = r["ssm_prompt"].reshape(G, NST, HG, HD).transpose(0, 2, 3, 1).reshape(1, 1, NH, HD, NST)
    v = r["v_last"].transpose(2, 1, 0).reshape(P + NS, D)
    return (r["y_prompt"].reshape(1, TP, D), r["y_sample"].reshape(NS, 1, D),
            conv_unlayout(r["conv_prompt"]).reshape(1, 1, 3, -1), ssm_p,
            v[:P].reshape(1, 1, P, D), conv_s.reshape(1, NS, 3, -1),
            r["ssm_sample"][None], v[P:].reshape(1, NS, 1, D))
```

```python
from contextlib import ExitStack, contextmanager

import numpy as np

import concourse.bass as bass
from concourse import mybir

F32 = mybir.dt.float32
FR = mybir.dt.float32r
U32 = mybir.dt.uint32
ALU = mybir.AluOpType
ACT = mybir.ActivationFunctionType
AX_X = mybir.AxisListType.X

P = 128
D = 2048
KB = D // P
TP = 512
NS = 8
T = TP + NS
H2 = T // 2
CH = 4
G = 8
HG = 8
HD = 64
NH = G * HG
GT = HG * HD // P
NST = 128
CT = 2 + GT
FT = D // P
EPS = 1e-5
ALPHA = 2.0 ** 0.25
PH = 8
TOPK = 16
NB = 5
NEG = -3.0e38
WCOLS = KB * P

N_SSD = G * (CT + GT)
N_V = FT
N_U = FT
O_V = N_SSD
O_U = O_V + N_V
O_GATE = O_U + N_U
O_BR = O_GATE + 2 * FT
O_OUT = O_BR + 3 * FT
O_Q = O_OUT + FT
N_TILES = O_Q + FT
READY0 = 4

SSD_DVE = 4 * CT + 1 + 2 * CH + 3
SSD_POOL = 5 * GT

GP_B = CT * 4
GP_NW = GP_B + CT
GP_D = GP_NW + GT
GP_N = GP_D + GT


class Order:

    def __init__(self, eng, sem):
        self.eng, self.sem, self.base, self.n = eng, sem, 0, 0

    def __call__(self, ins):
        ins.then_inc(self.sem, 1)
        self.n += 1
        self.eng.wait_ge(self.sem, self.base + self.n)

    @contextmanager
    def body(self, i, count, per):
        before = self.base + self.n
        self.base, self.n = before + i * per, 0
        yield
        assert self.n == per, f"{self.n} counted in the body, {per} said"
        self.base, self.n = before + count * per, 0


def bc(ap, n):
    return ap.unsqueeze(ap.ndim).to_broadcast(list(ap.shape) + [n])


def mid(ap, axis, n):
    shape = list(ap.shape)
    return ap.unsqueeze(axis).to_broadcast(shape[:axis] + [n] + shape[axis:])


class Kernel:
    def __init__(self, nc, a, o):
        self.nc, self.a, self.o = nc, a, o

    def sem(self, name):
        handle = self.nc.alloc_semaphore(name=name)
        self.phase_sems.append(handle)
        return handle

    def alone(self, eng):
        key = str(eng.engine)
        if key not in self.ticks:
            self.ticks[key] = self.sem("tick_" + key.split(".")[-1] + str(len(self.nc.allocations)))
        eng.sem_inc(self.ticks[key], 1)

    def clear_sems(self):
        self.nc.clear_and_free_semaphores(self.phase_sems)
        self.nc.all_engine_barrier()
        self.phase_sems, self.ticks = [], {}

    def load_weight(self, sp, n, j):
        sp.wait_ge(self.w_split, n - 1)
        sp.dma_start(self.w_raw[:, j, :], self.a["w_tiles"][n]).then_inc(self.w_in[j], 16)

    def stream(self, sp, first, total):
        last = first + total == N_TILES
        with sp.Fori(0, total // 2 - (1 if last else 0)) as i:
            for j in range(2):
                self.load_weight(sp, 2 * i + (first + 2 + j), j)

    def hi(self, act, n):
        j, n, half = n
        act.wait_ge(self.w_in[j], half * 16 + 16)
        act.wait_ge(self.gemm_ready, 2 * n + READY0 - 2)
        act.copy(self.wh[:, j, :], self.w_raw[:, j, :]).then_inc(self.w_hi, 1)

    def lo(self, dve, n):
        j, n, half = n
        dve.wait_ge(self.w_hi, n + 1)
        dve.tensor_tensor(self.wl[:, j, :], self.w_raw[:, j, :], self.wh[:, j, :].bitcast(F32),
                          ALU.subtract).then_inc(self.w_split, 1)

    @staticmethod
    def next_tile(first, i, j):
        return j, 2 * i + (first + j + 2), i + (first // 2 + 1)

    def turns(self, eng, first, total, body):
        last = 1 if first + total == N_TILES else 0
        with eng.Fori(0, total // 2 - last) as i:
            for j in range(2):
                body(2 * i + j, j, self.next_tile(first, i, j))
        if last:
            for j in range(2):
                body(total - 2 + j, j, None)

    def gemm(self, pe, n, j, pair_ready=None, between=None):
        for h in range(2):
            pe.wait_ge(self.gemm_free, 2 * n + 1 + h)
            if h == 0:
                pe.wait_ge(self.w_split, n + 1)
            elif between:
                between()
            hs = slice(h * H2, (h + 1) * H2)
            for k in range(KB):
                if pair_ready and h == 0:
                    pe.wait_ge(pair_ready[0], pair_ready[1] + k + 1)
                ks = slice(k * P, (k + 1) * P)
                o = self.bank[h][:, 0:H2]
                pe.matmul(o, self.wh[:, j, ks], self.ah[:, k, hs], start=(k == 0), stop=False)
                pe.matmul(o, self.wh[:, j, ks], self.al[:, k, hs], start=False, stop=False)
                last = pe.matmul(o, self.wl[:, j, ks], self.ah[:, k, hs], start=False, stop=(k == KB - 1))
            last.then_inc(self.gemm_ready, 1)

    def gemms(self, pe, first, total, pair_ready=None, started=False):
        peel = 1 if pair_ready or started else 0
        if peel:
            if not started:
                self.gemm(pe, first, 0, pair_ready)
            self.gemm(pe, first + 1, 1)
        with pe.Fori(0, total // 2 - peel) as i:
            for j in range(2):
                self.gemm(pe, 2 * i + (first + 2 * peel + j), j)

    def build(self):
        nc = self.nc
        self.root = ExitStack()
        self.phase_sems, self.ticks = [], {}
        self.w_in = [nc.alloc_semaphore(name=f"w_in{j}") for j in range(2)]
        self.w_hi, self.w_split, self.gemm_ready, self.gemm_free = (
            nc.alloc_semaphore(name=n) for n in ("w_hi", "w_split", "gemm_ready", "gemm_free"))
        with self.root:
            sb = lambda name, shape, dt=F32: self.root.enter_context(nc.sbuf_tensor(name, shape, dt))
            self.ident = sb("ident", [P, P])
            self.ones = sb("ones", [P, P])
            self.triu = sb("triu", [P, P])
            self.onesD = sb("onesD", [P, P])
            self.onesG = sb("onesG", [P, P])
            self.eps = sb("eps", [P, 1])
            self.lnp = sb("lnp", [P, 4, FT])
            self.psum = self.root.enter_context(nc.psum_tensor("psum", [P, 8, 512], F32))
            self.bank = [self.psum[:, i, :] for i in range(8)]
            eid, gates = sb("expert", [P, NB, P], U32), sb("gates", [P, NB, P])
            eidT, gatesT = sb("expert_smp", [P, NS], U32), sb("gates_smp", [P, NS])
            self.sel = sb("selector", [NS, NS, P])
            self.onehot8 = sb("onehot8", [P, NS, NS])
            htok = sb("shared", [P, NB, D])
            self.shared = htok[:].rearrange("p b d -> p (b d)")
            full = self.shared[:, 0:KB * T].rearrange("p (k t) -> p k t", k=KB)
            with ExitStack() as gemm:
                gs = lambda name, shape, dt=F32: gemm.enter_context(nc.sbuf_tensor(name, shape, dt))
                self.ah, self.al = gs("acts_hi", [P, KB, T], FR), gs("acts_lo", [P, KB, T], FR)
                self.w_raw = gs("w_raw", [P, 2, WCOLS])
                self.wh, self.wl = gs("w_hi_ring", [P, 2, WCOLS], FR), gs("w_lo_ring", [P, 2, WCOLS], FR)
                with ExitStack() as st:
                    tabs = self.tables(st, full)
                    self.clear_sems()
                    self.ssd(st, tabs)
                    self.clear_sems()
                self.sgu(full)
                self.clear_sems()
                self.branches(full)
                self.clear_sems()
                self.project_out(full, htok)
                self.clear_sems()
                self.query(eid, gates, eidT, gatesT)
            self.clear_sems()
            self.experts(htok, eid, gates, eidT, gatesT)

    def split_hi(self, act, src, hi_done, ready=None):
        for k in range(KB):
            if ready:
                act.wait_ge(*ready(k))
            act.copy(self.ah[:, k, :], src[:, k, :]).then_inc(hi_done, 1)

    def split_lo(self, dve, src, hi_done, pair_ready, base=0):
        for k in range(KB):
            dve.wait_ge(hi_done, base + k + 1)
            dve.tensor_tensor(self.al[:, k, :], src[:, k, :], self.ah[:, k, :].bitcast(F32),
                              ALU.subtract).then_inc(pair_ready, 1)

    def tables(self, st, xT):
        nc, a = self.nc, self.a
        tab = st.enter_context(nc.sbuf_tensor("dt_tab", [P, G, 4, CH, HG], F32))
        stab = st.enter_context(nc.sbuf_tensor("dt_smp", [P, G, 2, GT, NS], F32))
        NC = CH * NH
        W = NC + NS
        with ExitStack() as tmp:
            sb = lambda name, shape, dt=F32: tmp.enter_context(nc.sbuf_tensor(name, shape, dt))
            wdt = sb("wdt", [P, KB, NH])
            rows = sb("dt_rows", [P, 2 * NH + 2])
            v = {n: sb("sp_" + n, [P, W]) for n in ("x", "n", "u", "w", "l", "d", "m", "t")}
            dtA, acum, dte = sb("dtA", [P, W]), sb("acum", [P, NC]), sb("dte", [P, NC])
            arow = sb("arow", [P, NH + 1])
            diag = sb("dt_diag", [NH, 2, NS, NH])
            eA = sb("smp_eA", [P, NS])
            dts = sb("dt_by_head", [NH, T])
            in_sem, x_in, made, dord, pord = (self.sem("t_" + n) for n in ("in", "x_in", "made", "dve", "pool"))
            head_done, head_copied, proj_done, sums_done, spread_done = (
                self.sem("t_" + n) for n in ("head", "head_copied", "proj", "sums", "spread"))
            rate_ready, u_ready, ln_ready, decay_ready = (self.sem("t_" + n) for n in ("rate", "u", "ln", "decay"))
            neg_ready, w_ready, dtA_ready, gap_ready, diag_ready, hi_done, split = (
                self.sem("t_" + n) for n in ("neg", "w", "dtA", "gap", "diag", "x_hi", "x_split"))
            dth, dtp, ac, bcs = self.bank[5:7], self.bank[7], self.bank[2], self.bank[3:5]

            with nc.Block() as block:
                @block.sync
                def _(sp):
                    sp.dma_start(xT, a["xT"]).then_inc(x_in, 16)
                    sp.dma_start(wdt[:], a["w_dt"]).then_inc(x_in, 16)
                    for j in range(2):
                        sp.dma_start(self.w_raw[:, j, :], a["w_tiles"][j]).then_inc(self.w_in[j], 16)
                    sp.dma_start(rows[:], a["dt_rows"]).then_inc(in_sem, 16)
                    sp.wait_ge(in_sem, 16)

                @block.gpsimd
                def _(pool):
                    o = Order(pool, pord)
                    pool.memset(self.ident[:], 0.0)
                    pool.memset(self.ones[:], 1.0)
                    pool.memset(self.onesD[:], 1.0 / D)
                    pool.memset(self.onesG[:], 1.0 / (GT * P))
                    o(pool.memset(self.eps[:], EPS))
                    pool.affine_select(out=self.ident[:], in_=self.ident[:], compare_op=ALU.not_equal,
                                       fill=1.0, base=0, pattern=[[1, P]], channel_multiplier=-1)
                    pool.affine_select(out=self.triu[:], in_=self.ones[:], compare_op=ALU.is_ge,
                                       fill=0.0, base=0, pattern=[[1, P]],
                                       channel_multiplier=-1).then_inc(made, 1)

                @block.tensor
                def _(pe):
                    pe.sem_inc(self.gemm_ready, READY0)
                    pe.wait_ge(x_in, 32)
                    for h in range(2):
                        for k in range(KB):
                            last = pe.matmul(dth[h][0:NH, 0:H2], wdt[:, k, :], xT[:, k, h * H2:(h + 1) * H2],
                                             start=(k == 0), stop=(k == KB - 1))
                        last.then_inc(head_done, 1)
                    pe.wait_ge(made, 1)
                    pe.wait_ge(head_copied, 2)
                    for c in range(CH):
                        last = pe.transpose(dtp[:, c * NH:(c + 1) * NH], dts[:, c * P:(c + 1) * P],
                                            self.ident[0:NH, 0:NH])
                    last.then_inc(proj_done, 1)

                    def sums():
                        pe.wait_ge(dtA_ready, 1)
                        pe.matmul(ac[:, 0:NC], self.triu[:], dtA[:, 0:NC], start=True, stop=True)
                        pe.matmul(ac[:, NC:2 * NC], self.ones[:], dtA[:, 0:NC],
                                  start=True, stop=True).then_inc(sums_done, 1)

                    self.gemm(pe, 0, 0, (split, 0), between=sums)
                    pe.wait_ge(diag_ready, 1)
                    for s in range(2):
                        last = pe.matmul(bcs[s][:, 0:NS * NH], self.ones[0:NH, :],
                                         diag[:, s].rearrange("p b h -> p (b h)"), start=True, stop=True)
                    last.then_inc(spread_done, 1)

                @block.scalar
                def _(act):
                    act.sem_inc(self.gemm_free, 2)
                    act.wait_ge(x_in, 32)
                    self.split_hi(act, xT, hi_done)
                    self.hi(act, (0, 0, 0))
                    for h in range(2):
                        act.wait_ge(head_done, h + 1)
                        act.copy(dts[:, h * H2:(h + 1) * H2], dth[h][0:NH, 0:H2]).then_inc(head_copied, 1)
                    self.hi(act, (1, 1, 0))
                    act.wait_ge(in_sem, 16)
                    act.activation(arow[:, 0:NH], rows[:, NH:2 * NH], ACT.Exp)
                    act.activation(arow[:, NH:NH + 1], rows[:, 2 * NH + 1:2 * NH + 2],
                                   ACT.Exp).then_inc(rate_ready, 1)
                    act.wait_ge(neg_ready, 1)
                    act.activation(v["u"][:], v["n"][:], ACT.Exp).then_inc(u_ready, 1)
                    act.wait_ge(w_ready, 1)
                    act.activation(v["l"][:], v["w"][:], ACT.Ln).then_inc(ln_ready, 1)
                    act.wait_ge(gap_ready, 1)
                    act.activation(dte[:], acum[:], ACT.Exp)
                    act.activation(eA[0:NH, :], dtA[0:NH, NC:W], ACT.Exp).then_inc(decay_ready, 1)

                @block.vector
                def _(dve):
                    o = Order(dve, dord)
                    x = v["x"]
                    o(dve.memset(x[:], 0.0))
                    self.split_lo(dve, xT, hi_done, split)
                    self.lo(dve, (0, 0, 0))
                    dve.wait_ge(split, KB)
                    dve.wait_ge(proj_done, 1)
                    dve.wait_ge(in_sem, 16)
                    dve.tensor_tensor(x[:, 0:NC].rearrange("p (c h) -> p c h", c=CH),
                                      dtp[:, 0:NC].rearrange("p (c h) -> p c h", c=CH),
                                      mid(rows[:, 0:NH], 1, CH), ALU.add)
                    o(dve.tensor_scalar(x[0:NH, NC:W], dts[:, TP:T], rows[0:NH, 2 * NH:2 * NH + 1],
                                        None, ALU.add))
                    dve.scalar_tensor_tensor(out=v["n"][:], in0=x[:], scalar=-1.0, in1=x[:],
                                             op0=ALU.mult, op1=ALU.min).then_inc(neg_ready, 1)
                    self.lo(dve, (1, 1, 0))
                    dve.wait_ge(u_ready, 1)
                    dve.tensor_scalar(v["w"][:], v["u"][:], 1.0, None, ALU.add).then_inc(w_ready, 1)
                    dve.wait_ge(w_ready, 1)
                    o(dve.tensor_scalar(v["d"][:], v["w"][:], -1.0, None, ALU.add))
                    o(dve.tensor_scalar(v["m"][:], v["d"][:], 0.0, None, ALU.is_equal))
                    dve.wait_ge(ln_ready, 1)
                    dve.tensor_tensor(v["l"][:], v["l"][:], v["m"][:], ALU.add)
                    o(dve.tensor_tensor(v["d"][:], v["d"][:], v["m"][:], ALU.add))
                    o(dve.reciprocal(v["t"][:], v["d"][:]))
                    o(dve.tensor_tensor(v["l"][:], v["l"][:], v["t"][:], ALU.mult))
                    o(dve.tensor_tensor(v["l"][:], v["l"][:], v["u"][:], ALU.mult))
                    dt = v["t"]
                    o(dve.scalar_tensor_tensor(out=dt[:], in0=x[:], scalar=0.0, in1=v["l"][:],
                                               op0=ALU.max, op1=ALU.add))
                    dve.wait_ge(rate_ready, 1)
                    o(dve.tensor_scalar(v["w"][:, 0:NH + 1], arow[:], -1.0, None, ALU.mult))
                    dve.tensor_scalar(dtA[0:NH, NC:W], dt[0:NH, NC:W], v["w"][0:NH, NH:NH + 1],
                                      None, ALU.mult)
                    dve.tensor_tensor(dtA[:, 0:NC].rearrange("p (c h) -> p c h", c=CH),
                                      dt[:, 0:NC].rearrange("p (c h) -> p c h", c=CH),
                                      mid(v["w"][:, 0:NH], 1, CH), ALU.mult).then_inc(dtA_ready, 1)
                    dve.wait_ge(sums_done, 1)
                    dve.wait_ge(dtA_ready, 1)
                    o(dve.tensor_copy(v["n"][:, 0:NC], ac[:, 0:NC]))
                    dve.tensor_tensor(acum[:], ac[:, NC:2 * NC], v["n"][:, 0:NC],
                                      ALU.subtract).then_inc(gap_ready, 1)
                    dve.wait_ge(decay_ready, 1)
                    o(dve.tensor_tensor(dte[:], dte[:], dt[:, 0:NC], ALU.mult))
                    for kind, src in enumerate((dt, dte, v["n"], dtA)):
                        for c in range(CH):
                            dve.tensor_copy(tab[:, :, kind, c, :],
                                            src[:, c * NH:(c + 1) * NH].rearrange("p (g h) -> p g h", g=G))
                    for s, src in enumerate((dt[0:NH, NC:W], eA[0:NH, :])):
                        last = dve.tensor_tensor(diag[:, s], mid(self.ident[0:NH, 0:NH], 1, NS),
                                                 bc(src, NH), ALU.mult)
                    last.then_inc(diag_ready, 1)
                    dve.wait_ge(spread_done, 1)
                    for s in range(2):
                        src = bcs[s][:, 0:NS * NH].rearrange("p (b g t w) -> p g t w b", b=NS, g=G, w=2)
                        for g in range(G):
                            for w in range(2):
                                last = dve.tensor_copy(stab[w * HD:(w + 1) * HD, g, s],
                                                       src[w * HD:(w + 1) * HD, g, :, w, :])
                    o(last)
        return tab, stab

    def ssd(self, st, tabs):
        nc, a, out = self.nc, self.a, self.o
        tab, stab = tabs
        NT = CT + GT
        HB = NS // 2
        NU = GT * 2
        sb = lambda name, shape, dt=F32: st.enter_context(nc.sbuf_tensor(name, shape, dt))
        used = [0]

        def region(*shape):
            n = int(np.prod(shape))
            part = self.shared[:, used[0]:used[0] + n]
            used[0] += n
            names = " ".join("abc"[:len(shape)])
            return part if len(shape) == 1 else part.rearrange(
                f"p ({names}) -> p {names}", **{"abc"[i]: d for i, d in enumerate(shape)})

        raw = sb("raw", [P, 2, TP + 3])
        acc = sb("conv_acc", [P, 2, TP + NS])
        scv = sb("smp_conv", [P, 4, CT, NS])
        gpar = sb("g_par", [P, GP_N])
        cpo = sb("conv_pr_out", [P, CT, 3])
        sprod = sb("smp_prod", [P, 4, NS])
        bT, cT, xg, yg = region(T), region(T), region(GT, T), region(GT, T)
        gt, gs = sb("g_tab", [P, 4, CH, HG]), sb("g_smp", [P, 2, GT, NS])
        xdt, xde = sb("xdt", [P, HG, HD]), sb("x_dt_decay", [P, HG, HD])
        btok, cbm = sb("b_tok", [P, P]), sb("cb_masked", [P, P])
        tri = region(HG, P)
        L, eA = region(HG, P), region(HG, P)
        cdec = sb("chunk_decay", [P, HG])
        S = sb("state", [P, HG, HD])
        sst = sb("smp_state", [P, 2, HB, NST])
        stmp = sb("smp_tmp", [P, HB, NST])
        Bb, Cb = region(NS, NST), sb("C_bcast", [P, NS, NST])
        ys = sb("smp_y", [P, GT, NS])
        gb, tpb, bcb, ab, yb, stb = (self.bank[0:2], self.bank[2], self.bank[3], self.bank[4:6],
                                     self.bank[6], self.bank[7])
        S_ = lambda *names: [self.sem("s_" + n) for n in names]
        gemm_ready, gemm_free = self.gemm_ready, self.gemm_free
        raw_ready, conv_done, silu_done, stored, y_out = S_(
            "raw_ready", "conv_done", "silu_done", "stored", "y_out")
        par_in, conv_in, conv_out = S_("par_in", "conv_in", "conv_out")
        diag_ready, spread_done, spread_read = S_("diag_ready", "spread_done", "spread_read")
        tri_ready, a_done, seg_done, exp_done, m_ready, b_done, y_done = S_(
            "tri_ready", "a_done", "seg_done", "exp_done", "m_ready", "b_done", "y_done")
        gated, squared, rms_done, root_ready, group_done = S_(
            "gated", "squared", "rms_done", "root_ready", "group_done")
        tabs_ready, prod_ready, prod_read, fin_ready, fin_out = S_(
            "tabs_ready", "prod_ready", "prod_read", "fin_ready", "fin_out")
        st_in = [self.sem(f"s_st_in{j}") for j in range(2)]
        st_out = [self.sem(f"s_st_out{j}") for j in range(2)]
        dord, pord = S_("dve", "pool")
        state_in = a["state_ssm"].rearrange("b (t w) p n -> t (w p) b n", w=2)
        state_out = out["ssm_sample"].rearrange("b (t w) p n -> t (w p) b n", w=2)

        with nc.Block() as block:
            @block.sync
            def _(sp):
                self.stream(sp, 0, N_SSD)

            @block.tensor
            def _(pe):
                with pe.Fori(0, G) as g:
                    def project(t):
                        self.gemm(pe, NT * g + t, t % 2)

                    def spread(n):
                        pe.wait_ge(diag_ready, 2 * g + n + 1)
                        pe.wait_ge(spread_read, 2 * g + n + 1)
                        for h in range(2):
                            last = pe.matmul(ab[h][:], self.ones[:],
                                             tri[:, 4 * h:4 * h + 4, :].rearrange("p a b -> p (a b)"),
                                             start=True, stop=True)
                        last.then_inc(spread_done, 1)

                    def chunk_a(q):
                        s = slice(q * P, (q + 1) * P)
                        pe.wait_ge(silu_done, CT * g + CT + 2)
                        pe.wait_ge(tri_ready, CH * g + q + 1)
                        if q == 0:
                            pe.wait_ge(spread_read, 2 * g + 3)
                        for t in range(GT):
                            pe.transpose(tpb[:, t * P:(t + 1) * P], xg[:, t, s], self.ident[:])
                        pe.transpose(bcb[:, 0:P], bT[:, s], self.ident[:])
                        pe.matmul(bcb[:, P:2 * P], bT[:, s], cT[:, s], start=True, stop=True)
                        for h in range(2):
                            last = pe.matmul(ab[h][:], self.ones[:],
                                             tri[:, 4 * h:4 * h + 4, :].rearrange("p a b -> p (a b)"),
                                             start=True, stop=True)
                        last.then_inc(a_done, 1)

                    def chunk_b(q):
                        pe.wait_ge(m_ready, CH * g + q + 2)
                        pe.wait_ge(y_done, CH * g + q + 1)
                        for t in range(GT):
                            for w in range(2):
                                h = 2 * t + w
                                o = yb[w * HD:(w + 1) * HD, t * P:(t + 1) * P]
                                pe.matmul(o, xdt[:, h, :], L[:, h, :], start=True, stop=False)
                                pe.matmul(o, S[:, h, :], eA[:, h, :], start=False, stop=True)
                        pe.matmul(stb[:], btok[:], xde[:].rearrange("p a b -> p (a b)"),
                                  start=True, stop=True).then_inc(b_done, 1)

                    for t in range(1, CT):
                        project(t)
                        if t in (2, 3):
                            spread(t - 2)
                    for q in range(CH + 1):
                        def chunks():
                            if q > 0:
                                chunk_b(q - 1)
                            if q < CH:
                                chunk_a(q)
                        self.gemm(pe, NT * g + CT + q, q % 2, between=chunks)
                    for t in range(GT):
                        pe.wait_ge(squared, GT * g + t + 1)
                        for h in range(2):
                            last = pe.matmul(ab[h][:, 0:H2], self.onesG[:], xg[:, t, h * H2:(h + 1) * H2],
                                             start=(t == 0), stop=(t == GT - 1))
                    last.then_inc(rms_done, 1)

            @block.scalar
            def _(act):
                act.sem_inc(silu_done, 2)
                act.sem_inc(spread_read, 1)
                with act.Fori(0, G) as g:
                    def evac(t):
                        r = raw[:, t % 2, :]
                        act.wait_ge(conv_done, CT * g + t + 1)
                        act.wait_ge(gemm_ready, READY0 + 2 * NT * g + 2 * t + 1)
                        act.copy(r[:, 3:3 + H2], gb[0][:, 0:H2]).then_inc(gemm_free, 1)
                        act.wait_ge(gemm_ready, READY0 + 2 * NT * g + 2 * t + 2)
                        act.copy(r[:, 3 + H2:3 + TP], gb[1][:, 0:TP - H2]).then_inc(raw_ready, 1)
                        act.copy(scv[:, 3, t, :], gb[1][:, TP - H2:H2]).then_inc(gemm_free, 1)

                    def silu(t):
                        dst = (bT, cT)[t] if t < 2 else xg[:, t - 2, :]
                        act.wait_ge(conv_done, CT * g + t + 3)
                        act.wait_ge(par_in, 16 * g + 16)
                        if t == 0:
                            act.wait_ge(group_done, g + 1)
                        act.activation(dst, acc[:, t % 2, :], ACT.Silu,
                                       bias=gpar[:, GP_B + t:GP_B + t + 1]).then_inc(silu_done, 1)

                    def spread_out(n):
                        act.wait_ge(spread_done, 2 * g + n + 1)
                        for h in range(2):
                            last = act.copy((Bb, Cb)[n][:, 4 * h:4 * h + 4, :].rearrange("p a b -> p (a b)"),
                                            ab[h][:])
                        last.then_inc(spread_read, 1)

                    act.wait_ge(stored, g + 1)
                    evac(0)
                    for t in range(1, CT):
                        self.hi(act, ((t + 1) % 2, NT * g + t + 1, NT // 2 * g + (t + 1) // 2))
                        if t in (3, 4):
                            spread_out(t - 3)
                        evac(t)
                        silu(t - 1)
                    silu(CT - 1)
                    act.wait_ge(y_out, 16 * g + 16)
                    self.hi(act, (1, NT * g + CT + 1, NT // 2 * g + (CT + 1) // 2))
                    for q in range(CH):
                        def silu_z(h):
                            act.wait_ge(gemm_ready, READY0 + 2 * NT * g + 2 * (CT + q) + 1 + h)
                            act.activation(yg[:, q, h * H2:(h + 1) * H2], gb[h][:, 0:H2],
                                           ACT.Silu).then_inc(gemm_free, 1)

                        silu_z(0)
                        act.wait_ge(m_ready, CH * g + q + 1)
                        act.wait_ge(seg_done, CH * g + q + 1)
                        for h in range(2):
                            act.activation(eA[:, 4 * h:4 * h + 4, :].rearrange("p a b -> p (a b)"),
                                           ab[h][:], ACT.Exp)
                        act.activation(L[:], L[:], ACT.Exp).then_inc(exp_done, 1)
                        silu_z(1)
                        t = CT + q + 2
                        self.hi(act, (t % 2, NT * g + t, NT // 2 * g + t // 2))
                    for t in range(GT):
                        act.wait_ge(gated, GT * g + t + 1)
                        act.activation(xg[:, t, :], yg[:, t, :], ACT.Square).then_inc(squared, 1)
                    act.wait_ge(rms_done, g + 1)
                    for h in range(2):
                        last = act.activation(acc[:, 0, h * H2:(h + 1) * H2], ab[h][:, 0:H2], ACT.Sqrt,
                                              bias=self.eps[:])
                    last.then_inc(root_ready, 1)

            @block.vector
            def _(dve):
                o = Order(dve, dord)
                dve.memset(raw[:, 0, 0:3], 0.0)
                o(dve.memset(raw[:, 1, 0:3], 0.0))
                dve.sem_inc(conv_done, 2)
                for s in (m_ready, y_done, group_done, prod_read):
                    dve.sem_inc(s, 1)
                with dve.Fori(0, G) as g, o.body(g, G, SSD_DVE):
                    def conv(t):
                        r, ac = raw[:, t % 2, :], acc[:, t % 2, 0:TP]
                        w = gpar[:, 4 * t:4 * t + 4]
                        dve.wait_ge(raw_ready, CT * g + t + 1)
                        dve.wait_ge(gemm_free, 2 * NT * g + 2 * t + 4)
                        dve.wait_ge(silu_done, CT * g + t + 1)
                        o(dve.tensor_scalar(ac, r[:, 0:TP], w[:, 0:1], None, ALU.mult))
                        for k in range(1, 4):
                            ins = dve.scalar_tensor_tensor(out=ac, in0=r[:, k:k + TP], scalar=w[:, k:k + 1],
                                                           in1=ac, op0=ALU.mult, op1=ALU.add)
                            if k < 3:
                                o(ins)
                        dve.tensor_copy(cpo[:, t, :], r[:, TP:TP + 3])
                        o(dve.tensor_tensor(sprod[:], scv[:, :, t, :], bc(w, NS), ALU.mult))
                        dve.tensor_reduce(acc[:, t % 2, TP:T], sprod[:].rearrange("p r b -> p b r"), AX_X,
                                          ALU.add).then_inc(conv_done, 1)
                        dve.wait_ge(conv_done, CT * g + t + 3)

                    def diagonal(n):
                        dve.wait_ge(silu_done, CT * g + n + 3)
                        if n:
                            dve.wait_ge(spread_done, 2 * g + n)
                        dve.tensor_tensor(tri[:], mid(self.ident[:], 1, NS), bc((bT, cT)[n][:, TP:T], P),
                                          ALU.mult).then_inc(diag_ready, 1)

                    def tri_rhs(q):
                        dve.tensor_tensor(tri[:], mid(self.triu[:], 1, HG), bc(gt[:, 3, q, :], P),
                                          ALU.mult).then_inc(tri_ready, 1)

                    def sum_smp(u):
                        dve.wait_ge(prod_ready, NU * g + u + 1)
                        dve.tensor_reduce(ys[:, u // 2, HB * (u % 2):HB * (u % 2) + HB], stmp[:], AX_X,
                                          ALU.add).then_inc(prod_read, 1)

                    self.lo(dve, (0, NT * g + 2, None))
                    dve.wait_ge(par_in, 16 * g + 16)
                    dve.tensor_copy(gs[:], stab[:, g])
                    dve.tensor_copy(gt[:], tab[:, g]).then_inc(tabs_ready, 1)
                    dve.wait_ge(tabs_ready, g + 1)
                    dve.wait_ge(stored, g + 1)
                    o(dve.memset(S[:], 0.0))
                    for t in range(CT):
                        if t > 1:
                            self.lo(dve, ((t + 1) % 2, NT * g + t + 1, None))
                        if t == 0:
                            dve.wait_ge(conv_in, 16 * g + 16)
                        conv(t)
                        if t in (1, 2):
                            diagonal(t - 1)
                    dve.wait_ge(spread_done, 2 * g + 2)
                    tri_rhs(0)
                    self.lo(dve, (1, NT * g + CT + 1, None))
                    for q in range(CH):
                        s = slice(q * P, (q + 1) * P)
                        dve.wait_ge(a_done, CH * g + q + 1)
                        xt = tpb[:].rearrange("p (h d) -> p h d", h=HG)
                        dve.tensor_tensor(xdt[:], xt, bc(gt[:, 0, q, :], HD), ALU.mult)
                        dve.tensor_tensor(xde[:], xt, bc(gt[:, 1, q, :], HD), ALU.mult)
                        dve.tensor_copy(btok[:], bcb[:, 0:P])
                        dve.tensor_tensor(cbm[:], bcb[:, P:2 * P], self.triu[:], ALU.mult)
                        for h in range(HG):
                            last = dve.tensor_scalar(L[:, h, :], ab[h // 4][:, (h % 4) * P:(h % 4 + 1) * P],
                                                     gt[:, 2, q, h:h + 1], 0.0, ALU.subtract, ALU.min)
                        last.then_inc(seg_done, 1)
                        if q < CH - 1:
                            tri_rhs(q + 1)
                            sum_smp(2 * q)
                        dve.wait_ge(exp_done, CH * g + q + 1)
                        o(dve.tensor_copy(cdec[:], eA[:, :, P - 1]))
                        dve.tensor_tensor(L[:], L[:], mid(cbm[:], 1, HG), ALU.mult)
                        dve.tensor_tensor(eA[:], eA[:], mid(cT[:, s], 1, HG), ALU.mult).then_inc(m_ready, 1)
                        if q == CH - 1:
                            sum_smp(2 * q)
                        self.lo(dve, (q % 2, NT * g + CT + q + 2, None))
                        dve.wait_ge(b_done, CH * g + q + 1)

                        def next_state():
                            o(dve.tensor_tensor(S[:], S[:], bc(cdec[:], HD), ALU.mult))
                            return dve.tensor_tensor(S[:], S[:], stb[:].rearrange("p (h d) -> p h d", h=HG), ALU.add)

                        if q < CH - 1:
                            next_state()
                        for t in range(GT):
                            last = dve.scalar_tensor_tensor(out=xg[:, t, s], in0=xg[:, t, s],
                                                            scalar=gpar[:, GP_D + t:GP_D + t + 1],
                                                            in1=yb[:, t * P:(t + 1) * P],
                                                            op0=ALU.mult, op1=ALU.add)
                        if q < CH - 1:
                            last.then_inc(y_done, 1)
                            dve.wait_ge(y_done, CH * g + q + 2)
                        else:
                            o(last)
                        sum_smp(2 * q + 1)
                    dve.wait_ge(prod_read, NU * g + NU + 1)
                    for t in range(GT):
                        last = dve.scalar_tensor_tensor(out=xg[:, t, TP:T], in0=xg[:, t, TP:T],
                                                        scalar=gpar[:, GP_D + t:GP_D + t + 1],
                                                        in1=ys[:, t, :], op0=ALU.mult, op1=ALU.add)
                    o(last)
                    for t in range(GT):
                        dve.wait_ge(gemm_free, 2 * NT * g + 2 * (CT + t) + 4)
                        dve.tensor_tensor(yg[:, t, :], yg[:, t, :], xg[:, t, :],
                                          ALU.mult).then_inc(gated, 1)
                    next_state().then_inc(y_done, 1)
                    dve.wait_ge(y_done, CH * g + CH + 1)
                    dve.sem_inc(fin_ready, 1)
                    dve.wait_ge(root_ready, g + 1)
                    o(dve.reciprocal(acc[:, 0, :], acc[:, 0, :]))
                    for t in range(GT):
                        last = dve.scalar_tensor_tensor(out=yg[:, t, :], in0=yg[:, t, :],
                                                        scalar=gpar[:, GP_NW + t:GP_NW + t + 1],
                                                        in1=acc[:, 0, :], op0=ALU.mult, op1=ALU.mult)
                    last.then_inc(group_done, 1)
                    dve.wait_ge(group_done, g + 2)

            @block.gpsimd
            def _(pool):
                o = Order(pool, pord)
                pool.sem_inc(stored, 1)
                pool.dma_start(self.lnp[:], a["ln_cols"]).then_inc(y_out, 16)
                with pool.Fori(0, G) as g, o.body(g, G, SSD_POOL):
                    def load(u):
                        if u >= 2:
                            pool.wait_ge(st_out[u % 2], 64 * g + 16 * (u // 2))
                        self.alone(pool)
                        pool.dma_start(sst[:, u % 2], state_in[GT * g + u // 2, :, HB * (u % 2):HB * (u % 2) + HB, :]
                                       ).then_inc(st_in[u % 2], 16)

                    pool.wait_ge(group_done, g + 1)
                    self.alone(pool)
                    pool.dma_start(gpar[:], a["g_par"][g]).then_inc(par_in, 16)
                    pool.dma_start(scv[:, 0:3], a["state_conv"][g]).then_inc(conv_in, 16)
                    load(0)
                    pool.wait_ge(tabs_ready, g + 1)
                    for u in range(NU):
                        t, b0 = u // 2, HB * (u % 2)
                        s = sst[:, u % 2]
                        if u < NU - 1:
                            load(u + 1)
                        if u == 4:
                            pool.wait_ge(conv_done, CT * g + CT + 2)
                            self.alone(pool)
                            pool.dma_start(out["conv_sample"][g], scv[:, 1:4]).then_inc(conv_out, 16)
                            pool.dma_start(out["conv_prompt"][g], cpo[:]).then_inc(conv_out, 16)
                        if u == 0:
                            pool.wait_ge(spread_read, 2 * g + 3)
                        if u % 2 == 0:
                            pool.wait_ge(silu_done, CT * g + t + 5)
                        pool.wait_ge(st_in[u % 2], 64 * g + 16 * (u // 2) + 16)
                        if u % 2 == 0:
                            o(pool.tensor_tensor(gs[:, 0, t, :], gs[:, 0, t, :], xg[:, t, TP:T], ALU.mult))
                        pool.tensor_tensor(s, s, bc(gs[:, 1, t, b0:b0 + HB], NST), ALU.mult)
                        pool.wait_ge(prod_read, NU * g + u + 1)
                        o(pool.tensor_tensor(stmp[:], Bb[:, b0:b0 + HB, :], bc(gs[:, 0, t, b0:b0 + HB], NST),
                                             ALU.mult))
                        o(pool.tensor_tensor(s, s, stmp[:], ALU.add))
                        self.alone(pool)
                        pool.dma_start(state_out[GT * g + t, :, b0:b0 + HB, :], s).then_inc(st_out[u % 2], 16)
                        pool.tensor_tensor(stmp[:], s, Cb[:, b0:b0 + HB, :], ALU.mult).then_inc(prod_ready, 1)
                        pool.wait_ge(prod_ready, NU * g + u + 1)
                    pool.wait_ge(fin_ready, g + 1)
                    self.alone(pool)
                    pool.dma_start(out["ssm_prompt"][g], S[:].rearrange("p h d -> p (h d)")).then_inc(fin_out, 16)
                    pool.wait_ge(fin_out, 16 * g + 16)
                    pool.wait_ge(conv_out, 32 * g + 32)
                    for j in range(2):
                        pool.wait_ge(st_out[j], 64 * g + 64)
                    pool.sem_inc(stored, 1)
                    pool.wait_ge(group_done, g + 2)
                    self.alone(pool)
                    y_tiles = self.ys.rearrange("n p t -> p n t")[:, bass.ds(GT * g, GT), :]
                    pool.dma_start(y_tiles, yg).then_inc(y_out, 16)
                pool.wait_ge(y_out, 16 * G + 16)

    def ln_pe(self, pe, v, square, s):
        mu, var = self.bank[2:4], self.bank[4:6]
        for n in range(FT):
            pe.wait_ge(s["in"], n + 1)
            for h in range(2):
                last = pe.matmul(mu[h][:, 0:H2], self.onesD[:], v[:, n, h * H2:(h + 1) * H2],
                                 start=(n == 0), stop=(n == FT - 1))
        last.then_inc(s["mean"], 1)
        for n in range(FT):
            pe.wait_ge(s["square"], n + 1)
            for h in range(2):
                last = pe.matmul(var[h][:, 0:H2], self.onesD[:], square[:, n % 2, h * H2:(h + 1) * H2],
                                 start=(n == 0), stop=(n == FT - 1))
            last.then_inc(s["summed"], 1)

    def ln_act(self, act, v, square, root, s):
        for n in range(FT):
            act.wait_ge(s["centred"], n + 1)
            if n >= 2:
                act.wait_ge(s["summed"], n - 1)
            act.activation(square[:, n % 2, :], v[:, n, :], ACT.Square).then_inc(s["square"], 1)
        act.wait_ge(s["summed"], FT)
        for h in range(2):
            last = act.activation(root[:, h * H2:(h + 1) * H2], self.bank[4 + h][:, 0:H2], ACT.Sqrt,
                                  bias=self.eps[:])
        last.then_inc(s["root"], 1)

    def ln_dve(self, dve, v, root, g, b, s, after=None):
        mu = self.bank[2:4]
        dve.wait_ge(s["mean"], 1)
        for n in range(FT):
            for h in range(2):
                last = dve.tensor_tensor(v[:, n, h * H2:(h + 1) * H2], v[:, n, h * H2:(h + 1) * H2],
                                         mu[h][:, 0:H2], ALU.subtract)
            last.then_inc(s["centred"], 1)
        dve.wait_ge(s["root"], 1)
        dve.reciprocal(root[:], root[:]).then_inc(s["inv"], 1)
        dve.wait_ge(s["inv"], 1)
        for n in range(FT):
            dve.tensor_tensor(v[:, n, :], v[:, n, :], root[:], ALU.mult).then_inc(s["inv"], 1)
            dve.wait_ge(s["inv"], n + 2)
            dve.tensor_scalar(v[:, n, :], v[:, n, :], g[:, n:n + 1], b[:, n:n + 1],
                              ALU.mult, ALU.add).then_inc(s["normed"], 1)
            if after:
                after(n)

    def ln_sems(self, name):
        names = ("in", "mean", "square", "summed", "centred", "root", "inv", "normed")
        return {n: self.sem(f"{name}_{n}") for n in names}

    def sgu(self, v):
        nc, a, out = self.nc, self.a, self.o
        with ExitStack() as st:
            sb = lambda name, shape, dt=F32: st.enter_context(nc.sbuf_tensor(name, shape, dt))
            ub = sb("u_gated", [P, 2, T])
            root = sb("v_root", [P, T])
            square = sb("v_square", [P, 2, T])
            vst = sb("v_staged", [P, TP])
            vtok = sb("v_tok", [P, CH, P])
            ws = sb("w_spatial", [P, FT, P])
            bs = sb("b_spatial", [P, FT, P])
            w0 = sb("w_spatial0", [P, 2, FT])
            S_ = lambda *names: [self.sem("g_" + n) for n in names]
            par_in, v_out, masked, staged, turned, tok_ready, mixed, mix_free, gate_done, y_out, ub_free = S_(
                "par_in", "v_out", "masked", "staged", "turned", "tok_ready", "mixed",
                "mix_free", "gate_done", "y_out", "ub_free")
            dord, = S_("dve")
            ln = self.ln_sems("vln")
            gb, tb, mb = self.bank[0:2], self.bank[6], self.bank[7]
            with nc.Block() as block:
                @block.sync
                def _(sp):
                    sp.dma_start(w0[:], a["sgu_first"]).then_inc(par_in, 16)
                    sp.dma_start(ws[:], a["sgu_wT"]).then_inc(par_in, 16)
                    sp.dma_start(bs[:], a["sgu_b"]).then_inc(par_in, 16)
                    self.stream(sp, O_V, 2 * FT)

                @block.gpsimd
                def _(pool):
                    pool.sem_inc(ub_free, 2)
                    pool.wait_ge(ln["normed"], FT)
                    pool.dma_start(out["v_last"], v[:, :, TP - P:T]).then_inc(v_out, 16)
                    with pool.Fori(0, FT // 2) as i:
                        for j in range(2):
                            n = 2 * i + j
                            pool.wait_ge(gate_done, n + 1)
                            self.alone(pool)
                            pool.dma_start(self.ys[n + G * GT], ub[:, j, :]).then_inc(y_out, 16)
                            pool.wait_ge(y_out, 16 * n + 16)
                            pool.sem_inc(ub_free, 1)
                    pool.wait_ge(v_out, 16)

                @block.tensor
                def _(pe):
                    pe.sem_inc(mixed, 1)
                    pe.sem_inc(turned, 1)
                    self.gemms(pe, O_V, FT, started=True)
                    self.ln_pe(pe, v, square, ln)
                    with pe.Fori(0, FT // 2) as i:
                        for j in range(2):
                            n = 2 * i + j

                            def turn():
                                pe.wait_ge(staged, n + 1)
                                for c in range(CH):
                                    last = pe.transpose(tb[:, c * P:(c + 1) * P], vst[:, c * P:(c + 1) * P],
                                                        self.ident[:])
                                last.then_inc(turned, 1)

                            self.gemm(pe, 2 * i + (O_U + j), j, between=turn)
                            pe.wait_ge(tok_ready, n + 1)
                            pe.wait_ge(masked, 1)
                            pe.wait_ge(mix_free, n + 1)
                            for c in range(CH):
                                last = pe.matmul(mb[:, c * P:(c + 1) * P], vtok[:, c, :],
                                                 ws[:, n, :], start=True, stop=True)
                            last.then_inc(mixed, 1)

                @block.scalar
                def _(act):
                    def gelu_v(n, j, nxt):
                        for h in range(2):
                            act.wait_ge(self.gemm_ready, 2 * n + (READY0 + 2 * O_V + 1 + h))
                            self.alone(act)
                            act.activation(v[:, n, h * H2:(h + 1) * H2], gb[h][:, 0:H2],
                                           ACT.Gelu).then_inc(self.gemm_free, 1)
                        act.wait_ge(self.gemm_free, 2 * n + (2 * O_V + 4))
                        act.sem_inc(ln["in"], 1)
                        self.hi(act, nxt)

                    def gelu_u(n, j, nxt):
                        act.wait_ge(ub_free, n + 1)
                        for h in range(2):
                            act.wait_ge(self.gemm_ready, 2 * n + (READY0 + 2 * O_U + 1 + h))
                            act.activation(ub[:, j, h * H2:(h + 1) * H2], gb[h][:, 0:H2],
                                           ACT.Gelu).then_inc(self.gemm_free, 1)
                            if h == 0:
                                act.wait_ge(turned, n + 2)
                                act.wait_ge(mixed, n + 1)
                                act.copy(vtok[:].rearrange("p c d -> p (c d)"), tb[:]).then_inc(tok_ready, 1)
                        self.hi(act, nxt)

                    self.turns(act, O_V, FT, gelu_v)
                    self.ln_act(act, v, square, root, ln)
                    self.turns(act, O_U, FT, gelu_u)

                @block.vector
                def _(dve):
                    dve.sem_inc(mix_free, 1)
                    dve.wait_ge(par_in, 48)
                    dve.tensor_tensor(ws[:], ws[:], mid(self.triu[:], 1, FT), ALU.mult).then_inc(masked, 1)
                    self.turns(dve, O_V, FT, lambda n, j, nxt: self.lo(dve, nxt))

                    def stage(n):
                        dve.wait_ge(turned, n + 1)
                        dve.tensor_copy(vst[:], v[:, n, 0:TP]).then_inc(staged, 1)

                    def after(n):
                        if n == 0:
                            dve.wait_ge(ln["normed"], 1)
                            stage(0)

                    self.ln_dve(dve, v, root, self.lnp[:, 0, :], self.lnp[:, 1, :], ln, after)
                    dve.wait_ge(ln["normed"], FT)
                    o = Order(dve, dord)

                    def gate(n, j, nxt, more=True):
                        if more:
                            stage(n + 1)
                        o(dve.tensor_tensor(root[:, TP:T], v[:, n, TP:T],
                                            w0[:, 0, bass.ds(n, 1)].to_broadcast([P, NS]), ALU.mult))
                        dve.tensor_tensor(root[:, TP:T], root[:, TP:T],
                                          w0[:, 1, bass.ds(n, 1)].to_broadcast([P, NS]), ALU.add)
                        dve.wait_ge(mixed, n + 2)
                        dve.tensor_tensor(root[:, 0:TP].rearrange("p (c i) -> p c i", c=CH),
                                          mb.rearrange("p (c i) -> p c i", c=CH),
                                          bs[:, bass.ds(n, 1), :].to_broadcast([P, CH, P]),
                                          ALU.add).then_inc(mix_free, 1)
                        dve.wait_ge(mix_free, n + 2)
                        dve.wait_ge(self.gemm_free, 2 * n + (2 * O_U + 4))
                        dve.tensor_tensor(ub[:, j, :], ub[:, j, :], root[:], ALU.mult).then_inc(gate_done, 1)
                        dve.wait_ge(gate_done, n + 1)
                        self.lo(dve, nxt)

                    with dve.Fori(0, FT // 2 - 1) as i, o.body(i, FT // 2 - 1, 2):
                        for j in range(2):
                            gate(2 * i + j, j, self.next_tile(O_U, i, j))
                    for j in range(2):
                        gate(FT - 2 + j, j, self.next_tile(O_U, FT // 2 - 1, j), more=(j == 0))

    def branches(self, merged):
        nc = self.nc
        with ExitStack() as st:
            sb = lambda name, shape: st.enter_context(nc.sbuf_tensor(name, shape, F32))
            stage = sb("gate_stage", [P, 2, T])
            y = sb("branch_in", [P, KB, T])
            gate = sb("gate_ring", [P, 2, T])
            S_ = lambda *names: [self.sem("b_" + n) for n in names]
            gate_out, stage_free, hi_done, split, gate_used = S_("gate_out", "stage_free", "y_hi", "y_split",
                                                                 "gate_used")
            NQ = 4
            y_in = [self.sem(f"b_y_in{i}") for i in range(NQ)]
            gate_in = [self.sem(f"b_gate_in{j}") for j in range(2)]
            passes = range(3)
            with nc.Block() as block:
                @block.sync
                def _(sp):
                    self.stream(sp, O_GATE, 5 * FT)

                @block.gpsimd
                def _(pool):
                    def load_y(p):
                        for i in range(NQ):
                            s = slice(NQ * i, NQ * (i + 1))
                            src = self.ys[FT * p + NQ * i:FT * p + NQ * (i + 1)]
                            pool.dma_start(y[:, s, :], src.rearrange("k p t -> p k t")).then_inc(y_in[i], 16)

                    load_y(0)
                    pool.sem_inc(stage_free, 2)
                    with pool.Fori(0, FT) as i:
                        for j in range(2):
                            n = 2 * i + j
                            pool.wait_ge(self.gemm_free, 2 * n + (2 * O_GATE + 4))
                            self.alone(pool)
                            pool.dma_start(self.gates_dram[n], stage[:, j, :]).then_inc(gate_out, 16)
                            pool.wait_ge(gate_out, 16 * n + 16)
                            pool.sem_inc(stage_free, 1)
                    for p in passes:
                        if p > 0:
                            pool.wait_ge(split, KB * p)
                            load_y(p)
                        with pool.Fori(0, FT // 2) as i:
                            for j in range(2):
                                pool.wait_ge(gate_used, 2 * i + (FT * p + j + 1))
                                self.alone(pool)
                                src = self.gates_dram[2 * i + (j if p < 2 else FT + j)]
                                pool.dma_start(gate[:, j, :], src).then_inc(gate_in[j], 16)

                @block.tensor
                def _(pe):
                    self.gemms(pe, O_GATE, 2 * FT)
                    for p in passes:
                        self.gemms(pe, O_BR + FT * p, FT, (split, KB * p))

                @block.scalar
                def _(act):
                    def sigmoid(n, j, nxt):
                        act.wait_ge(stage_free, n + 1)
                        for h in range(2):
                            act.wait_ge(self.gemm_ready, 2 * n + (READY0 + 2 * O_GATE + 1 + h))
                            act.activation(stage[:, j, h * H2:(h + 1) * H2], self.bank[h][:, 0:H2],
                                           ACT.Sigmoid).then_inc(self.gemm_free, 1)
                        self.hi(act, nxt)

                    self.turns(act, O_GATE, 2 * FT, sigmoid)
                    for p in passes:
                        act.wait_ge(self.gemm_ready, READY0 + 2 * (O_BR + FT * p))
                        self.split_hi(act, y, hi_done, lambda k: (y_in[k // NQ], 16 * p + 16))
                        self.turns(act, O_BR + FT * p, FT, lambda n, j, nxt: self.hi(act, nxt))

                @block.vector
                def _(dve):
                    dve.sem_inc(gate_used, 2)
                    self.turns(dve, O_GATE, 2 * FT, lambda n, j, nxt: self.lo(dve, nxt))
                    for p in passes:
                        self.split_lo(dve, y, hi_done, split, KB * p)
                        first = O_BR + FT * p
                        with dve.Fori(0, FT // 2) as i:
                            for j in range(2):
                                n = 2 * i + j
                                dve.wait_ge(gate_in[j], 16 * i + (8 * FT * p + 16))
                                for h in range(2):
                                    s = slice(h * H2, (h + 1) * H2)
                                    m = merged[:, n, s]
                                    dve.wait_ge(self.gemm_ready, 2 * n + (READY0 + 2 * first + 1 + h))
                                    dve.tensor_tensor(m if p == 0 else gate[:, j, s], gate[:, j, s],
                                                      self.bank[h][:, 0:H2], ALU.mult).then_inc(self.gemm_free, 1)
                                    dve.wait_ge(self.gemm_free, 2 * n + (2 * first + 3 + h))
                                    if p:
                                        last = dve.tensor_tensor(m, m, gate[:, j, s], ALU.add)
                                if p:
                                    last.then_inc(gate_used, 1)
                                    dve.wait_ge(gate_used, n + (FT * p + 3))
                                else:
                                    dve.sem_inc(gate_used, 1)
                                self.lo(dve, self.next_tile(first, i, j))

    def project_out(self, merged, htok):
        nc = self.nc
        with ExitStack() as st:
            sb = lambda name, shape: st.enter_context(nc.sbuf_tensor(name, shape, F32))
            h = sb("h", [P, KB, T])
            root = sb("h_root", [P, T])
            square = sb("h_square", [P, 2, T])
            S_ = lambda *names: [self.sem("o_" + n) for n in names]
            x_in, hi_done, split, turned, turn_read = S_("x_in", "hi", "split", "turned", "turn_read")
            gb, tb = self.bank[0:2], self.bank[6:8]
            ln = self.ln_sems("hln")
            tokens = lambda b: slice(b * P, min((b + 1) * P, T))
            rows = lambda b: min((b + 1) * P, T) - b * P
            with nc.Block() as block:
                @block.sync
                def _(sp):
                    sp.dma_start(h[:], self.a["xT"]).then_inc(x_in, 16)
                    self.stream(sp, O_OUT, FT)

                @block.tensor
                def _(pe):
                    self.gemms(pe, O_OUT, FT, (split, 0))
                    self.ln_pe(pe, h, square, ln)
                    for c in range(FT // 4):
                        pe.wait_ge(ln["normed"], 4 * c + 4)
                        for b in range(NB):
                            m = NB * c + b
                            if m >= 2:
                                pe.wait_ge(turn_read, m - 1)
                            for t in range(4):
                                last = pe.transpose(tb[m % 2][0:rows(b), t * P:(t + 1) * P],
                                                    h[:, 4 * c + t, tokens(b)], self.ident[:])
                            last.then_inc(turned, 1)

                @block.scalar
                def _(act):
                    self.split_hi(act, merged, hi_done)
                    self.turns(act, O_OUT, FT, lambda n, j, nxt: self.hi(act, nxt))
                    self.ln_act(act, h, square, root, ln)
                    for c in range(FT // 4):
                        for k in range(4 * c, 4 * c + 4):
                            act.wait_ge(ln["normed"], k + 1)
                            act.copy(self.ah[:, k, :], h[:, k, :]).then_inc(hi_done, 1)
                        for b in range(NB):
                            m = NB * c + b
                            act.wait_ge(turned, m + 1)
                            act.copy(htok[0:rows(b), b, 512 * c:512 * (c + 1)],
                                     tb[m % 2][0:rows(b), :]).then_inc(turn_read, 1)

                @block.vector
                def _(dve):
                    self.split_lo(dve, merged, hi_done, split)
                    dve.wait_ge(x_in, 16)
                    with dve.Fori(0, FT // 2) as i:
                        for j in range(2):
                            n = 2 * i + j
                            for hf in range(2):
                                m = h[:, n, hf * H2:(hf + 1) * H2]
                                dve.wait_ge(self.gemm_ready, 2 * n + (READY0 + 2 * O_OUT + 1 + hf))
                                dve.scalar_tensor_tensor(out=m, in0=m, scalar=ALPHA, in1=gb[hf][:, 0:H2],
                                                         op0=ALU.mult, op1=ALU.add).then_inc(self.gemm_free, 1)
                            dve.wait_ge(self.gemm_free, 2 * n + (2 * O_OUT + 4))
                            dve.sem_inc(ln["in"], 1)
                            self.lo(dve, self.next_tile(O_OUT, i, j))

                    def lo_h(n):
                        dve.wait_ge(hi_done, KB + n + 1)
                        dve.tensor_tensor(self.al[:, n, :], h[:, n, :], self.ah[:, n, :].bitcast(F32),
                                          ALU.subtract).then_inc(split, 1)

                    LAG = 6
                    self.ln_dve(dve, h, root, self.lnp[:, 2, :], self.lnp[:, 3, :], ln,
                                lambda n: lo_h(n - LAG) if n >= LAG else None)
                    for n in range(FT - LAG, FT):
                        lo_h(n)

    def query(self, eid, gates, eidT, gatesT):
        nc, a = self.nc, self.a
        HH = 2 * PH
        with ExitStack() as st:
            sb = lambda name, shape, dt=F32: st.enter_context(nc.sbuf_tensor(name, shape, dt))
            keys = sb("keys", [P, HH, P])
            qb = sb("q", [P, 2, T])
            work, cand = sb("work", [P, NB, P]), sb("cand", [P, NB, TOPK * TOPK])
            tv, ti = sb("top_s", [P, NB, 2, TOPK]), sb("top_i", [P, NB, 2, TOPK], U32)
            bv, bi = sb("best_s", [P, NB, TOPK]), sb("best_c", [P, NB, TOPK], U32)
            bvs = sb("best_s_all", [P, NB, PH, TOPK])
            tif, code = sb("top_i_f32", [P, NB, 2, TOPK]), sb("code", [P, NB, 2, TOPK], U32)
            pick, side = sb("pick", [P, NB, 2, TOPK]), sb("side", [P, NB, 2, TOPK])
            hot = sb("one_hot", [P, NB * 2 * TOPK, TOPK])
            number = sb("number", [P, NB, PH + 1, TOPK])
            gsum = sb("gate_sum", [P, NB, PH])
            iota = sb("iota16", [P, TOPK])
            S_ = lambda *names: [self.sem("q_" + n) for n in names]
            gemm_ready, gemm_free = self.gemm_ready, self.gemm_free
            (keys_in, q_ready, scored, score_read, pick_ready,
             hot_ready, exp_ready, exp_done, smp_ready, smp_turned) = S_(
                "keys_in", "q_ready", "scored",
                "score_read", "pick_ready", "hot_ready", "exp_ready", "exp_done", "smp_ready", "smp_turned")
            dord, pord = S_("dve", "pool")
            gb = self.bank[0:2]
            tokens = lambda b: slice(b * P, min((b + 1) * P, T))
            rows = lambda b: min((b + 1) * P, T) - b * P

            with nc.Block() as block:
                @block.sync
                def _(sp):
                    sp.dma_start(keys[:], a["keys"]).then_inc(keys_in, 16)
                    self.stream(sp, O_Q, FT)

                @block.gpsimd
                def _(pool):
                    o = Order(pool, pord)
                    pool.memset(side[:], 0.0)
                    o(pool.iota(iota[:], pattern=[[1, TOPK]], base=0, channel_multiplier=0,
                                allow_small_or_imprecise_dtypes=True))
                    pool.sem_inc(hot_ready, 1)

                    sel, onehot = self.sel, self.onehot8
                    pool.memset(sel[:], 0.0)
                    o(pool.memset(onehot[:], 0.0))
                    pool.affine_select(out=sel[:], in_=sel[:], compare_op=ALU.not_equal, fill=1.0, base=0,
                                       pattern=[[1, NS], [0, P]], channel_multiplier=-1)
                    o(pool.affine_select(out=onehot[:], in_=onehot[:], compare_op=ALU.not_equal, fill=1.0,
                                         base=0, pattern=[[1, NS], [-1, NS]], channel_multiplier=0))

                    def decode(h):
                        pool.wait_ge(pick_ready, h + 1)
                        h4 = hot[:].rearrange("p (b k) i -> p b k i", k=TOPK)
                        o(pool.tensor_tensor(h4, h4, mid(tif[:].rearrange("p b s i -> p (b s) i"), 2, TOPK),
                                             ALU.mult))
                        for w in (TOPK // 2, TOPK // 4, TOPK // 8):
                            o(pool.tensor_tensor(hot[:, :, 0:w], hot[:, :, 0:w], hot[:, :, w:2 * w], ALU.add))
                        pool.tensor_tensor(side[:].rearrange("p b s k -> p (b s k)").unsqueeze(2),
                                           hot[:, :, 0:1], hot[:, :, 1:2], ALU.add).then_inc(hot_ready, 1)

                    for j in range(2):
                        self.lo(pool, self.next_tile(O_Q, 0, j))
                    with pool.Fori(0, PH - 2) as h, o.body(h, PH - 2, 4):
                        for j in range(2):
                            self.lo(pool, self.next_tile(O_Q + 2, h, j))
                        decode(h)
                    for h in range(PH - 2, PH):
                        decode(h)

                @block.tensor
                def _(pe):
                    pe.sem_inc(scored, 2)
                    pe.wait_ge(keys_in, 16)

                    def score(n, j):
                        pe.wait_ge(q_ready, 2 * n + 2)
                        pe.wait_ge(score_read, n + 1)
                        s = self.bank[2 + 2 * j:4 + 2 * j]
                        for b in range(NB):
                            o = s[0][:, b * P:(b + 1) * P] if b < CH else s[1][0:NS, 0:P]
                            last = pe.matmul(o, qb[:, j, tokens(b)], keys[:, n, :],
                                             start=True, stop=True)
                        last.then_inc(scored, 1)

                    self.gemm(pe, O_Q, 0)
                    self.gemm(pe, O_Q + 1, 1, between=lambda: score(0, 0))
                    with pe.Fori(0, FT // 2 - 1) as i:
                        for j in range(2):
                            self.gemm(pe, 2 * i + (O_Q + 2 + j), j,
                                      between=lambda: score(2 * i + (1 + j), (1 + j) % 2))
                    score(HH - 1, 1)
                    pe.wait_ge(smp_ready, 1)
                    pe.transpose(self.bank[6][:, 0:NS], number[0:NS, CH, 1:, :].rearrange("p h k -> p (h k)"), self.ident[0:NS, 0:NS])
                    pe.transpose(self.bank[6][:, NS:2 * NS], gates[0:NS, CH, :],
                                 self.ident[0:NS, 0:NS]).then_inc(smp_turned, 1)

                @block.scalar
                def _(act):
                    def queries(n, j, nxt):
                        act.wait_ge(scored, n + 1)
                        for h in range(2):
                            act.wait_ge(gemm_ready, 2 * n + (READY0 + 2 * O_Q + 1 + h))
                            act.copy(qb[:, j, h * H2:(h + 1) * H2], gb[h][:, 0:H2]).then_inc(q_ready, 1)
                        act.wait_ge(q_ready, 2 * n + 2)
                        act.sem_inc(gemm_free, 2)
                        if nxt:
                            self.hi(act, nxt)

                    self.turns(act, O_Q, FT, queries)
                    act.wait_ge(exp_ready, 1)
                    act.activation(gates[:], work[:], ACT.Exp
                                   ).then_inc(exp_done, 1)

                @block.vector
                def _(dve):
                    o = Order(dve, dord)
                    for x in (tv, ti, bv, bi, work, cand):
                        ins = dve.memset(x[:], 0)
                    o(ins)
                    dve.sem_inc(score_read, 2)

                    def after(ins):
                        o(ins)
                        self.alone(dve)

                    def top16(src, wk, vals, idx):
                        for s_, w_, v_, x_ in zip(src, wk, vals, idx):
                            ins = dve.max(v_[:, 0:8], s_)
                        after(ins)
                        for s_, w_, v_, x_ in zip(src, wk, vals, idx):
                            dve.max_index(x_[:, 0:8], v_[:, 0:8], s_)
                            ins = dve.match_replace(w_, v_[:, 0:8], s_, NEG)
                        after(ins)
                        for s_, w_, v_, x_ in zip(src, wk, vals, idx):
                            ins = dve.max(v_[:, 8:16], w_)
                        after(ins)
                        for s_, w_, v_, x_ in zip(src, wk, vals, idx):
                            ins = dve.max_index(x_[:, 8:16], v_[:, 8:16], w_)
                        return ins

                    def numbers(slot):
                        o(dve.scalar_tensor_tensor(out=number[:, :, slot, :], in0=side[:, :, 0, :],
                                                   scalar=float(P), in1=side[:, :, 1, :],
                                                   op0=ALU.mult, op1=ALU.add))

                    with dve.Fori(0, PH) as h, o.body(h, PH, 14):
                        for s in range(2):
                            dve.wait_ge(scored, 2 * h + s + 3)
                            self.alone(dve)
                            bk = self.bank[2 + 2 * s:4 + 2 * s]
                            top16([bk[0][:, b * P:(b + 1) * P] if b < CH else bk[1][0:NS, 0:P] for b in range(NB)],
                                  [work[0:rows(b), b, :] for b in range(NB)],
                                  [tv[0:rows(b), b, s, :] for b in range(NB)],
                                  [ti[0:rows(b), b, s, :] for b in range(NB)]).then_inc(score_read, 1)
                            dve.wait_ge(score_read, 2 * h + s + 3)
                        for b in range(NB):
                            ins = dve.tensor_tensor(cand[:, b].rearrange("p (i j) -> p i j", i=TOPK),
                                                    bc(tv[:, b, 0, :], TOPK), mid(tv[:, b, 1, :], 1, TOPK), ALU.add)
                        after(ins)
                        after(top16([cand[0:rows(b), b, :] for b in range(NB)],
                                    [cand[0:rows(b), b, :] for b in range(NB)],
                                    [bv[0:rows(b), b, :] for b in range(NB)],
                                    [bi[0:rows(b), b, :] for b in range(NB)]))
                        dve.tensor_copy(bvs[:, :, h, :], bv[:])
                        for s, (op, by) in enumerate(((ALU.logical_shift_right, 4), (ALU.bitwise_and, TOPK - 1))):
                            ins = dve.tensor_scalar(code[:, :, s, :], bi[:], by, None, op)
                        o(ins)
                        dve.wait_ge(hot_ready, h + 1)
                        numbers(h)
                        dve.tensor_copy(tif[:], ti[:])
                        o(dve.tensor_copy(pick[:], code[:]))
                        dve.tensor_tensor(hot[:], bc(pick[:].rearrange("p b s k -> p (b s k)"), TOPK),
                                          mid(iota[:], 1, NB * 2 * TOPK), ALU.is_equal).then_inc(pick_ready, 1)
                        dve.wait_ge(pick_ready, h + 1)

                    for b in range(NB):
                        ins = dve.tensor_tensor(work[:, b].rearrange("p (h k) -> p h k", h=PH), bvs[:, b],
                                                bvs[:, b, :, 0:1].to_broadcast([P, PH, TOPK]), ALU.subtract)
                    ins.then_inc(exp_ready, 1)
                    dve.wait_ge(exp_done, 1)
                    gv = gates[:].rearrange("p b (h k) -> p b h k", h=PH)
                    for b in range(NB):
                        ins = dve.tensor_reduce(gsum[:, b], gv[:, b], AX_X, ALU.add)
                    o(ins)
                    o(dve.reciprocal(gsum[:], gsum[:]))
                    for b in range(NB):
                        ins = dve.tensor_tensor(gv[:, b], gv[:, b], bc(gsum[:, b], TOPK), ALU.mult)
                    o(ins)
                    dve.wait_ge(hot_ready, PH + 1)
                    numbers(PH)
                    dve.tensor_copy(eid[:].rearrange("p b (h k) -> p b h k", h=PH),
                                    number[:, :, 1:, :]).then_inc(smp_ready, 1)
                    dve.wait_ge(smp_turned, 1)
                    dve.tensor_copy(eidT[:], self.bank[6][:, 0:NS])
                    o(dve.tensor_copy(gatesT[:], self.bank[6][:, NS:2 * NS]))

    def experts(self, htok, eid, gates, eidT, gatesT):
        nc, a, out = self.nc, self.a, self.o
        NR = 8
        HR = NR // 2
        NJ = P // NR
        with ExitStack() as st:
            sb = lambda name, shape, dt=F32: st.enter_context(nc.sbuf_tensor(name, shape, dt))
            rows = sb("rows", [P, 2 * NR, D])
            urow = [rows[:, i, :] for i in range(NR)]
            vrow = [rows[:, NR + i, :] for i in range(NR)]
            acc = sb("acc", [P, D])
            ln2 = sb("ln2", [P, 2, D])
            dots, ge, coef = sb("dots", [P, NR]), sb("gelu", [P, NR]), sb("coef", [P, NR])
            iu, iv = sb("index_u", [P, NR], U32), sb("index_v", [P, NR], U32)
            sel, onehot = self.sel, self.onehot8
            coefm = sb("coef_smp", [P, NS, NS])
            stats, mv = sb("bn_stats", [P, 4, 6]), sb("bn_mv", [P, 2])
            rstd = sb("rstd", [P, 1])
            S_ = lambda *names: [self.sem("e_" + n) for n in names]
            u_in = [self.sem(f"e_u{j}") for j in range(NR)]
            v_in = [self.sem(f"e_v{j}") for j in range(NR)]
            (ln2_in, h_spread, smp_dots, smp_gelu, smp_coef, smp_mixed, dot_done, gelu_done, acc_done,
             var_ready, root_ready, y_ready, y_out) = S_(
                "ln2_in", "h_spread", "smp_dots", "smp_gelu", "smp_coef", "smp_mixed", "dot_done",
                "gelu_done", "acc_done", "var_ready", "root_ready", "y_ready", "y_out")
            dord, lord, pord, qord = S_("dve", "dve_ln", "pool", "pool_idx")
            gather = lambda pool, dst, table, idx: pool.indirect_dma_start(
                out=dst, out_offset=None, in_=table, in_offset=bass.IndirectOffsetOnAxis(ap=idx, axis=0))

            def norm(dve, o, rows, n, y):
                x = acc[0:rows, :]
                for c in range(4):
                    ins = dve.bn_stats(stats[0:rows, c, :], x[:, 512 * c:512 * (c + 1)])
                o(ins)
                self.alone(dve)
                dve.bn_aggr(mv[0:rows, :], stats[0:rows]).then_inc(var_ready, 1)
                dve.wait_ge(root_ready, n + 1)
                o(dve.reciprocal(rstd[0:rows, :], rstd[0:rows, :]))
                o(dve.tensor_scalar(x, x, mv[0:rows, 0:1], rstd[0:rows, :], ALU.subtract, ALU.mult))
                o(dve.tensor_tensor(x, x, ln2[0:rows, 0, :], ALU.mult))
                dve.tensor_tensor(y, x, ln2[0:rows, 1, :], ALU.add).then_inc(y_ready, 1)
                dve.wait_ge(y_ready, n + 1)

            with nc.Block() as block:
                @block.sync
                def _(sp):
                    sp.dma_start(ln2[:], a["ln2_rows"]).then_inc(ln2_in, 16)
                    with sp.Fori(0, CH - 1) as b:
                        sp.wait_ge(y_ready, b + 1)
                        sp.dma_start(out["y_prompt"][b], htok[:, b, :]).then_inc(y_out, 16)
                    sp.wait_ge(y_ready, CH)
                    sp.dma_start(out["y_sample"], htok[0:NS, CH, :]).then_inc(y_out, 16)
                    sp.wait_ge(y_ready, CH + 1)
                    sp.dma_start(out["y_prompt"][CH - 1], htok[:, CH - 1, :]).then_inc(y_out, 16)
                    sp.wait_ge(y_out, 16 * (CH + 1))

                @block.gpsimd
                def _(pool):
                    for b in range(NS):
                        gather(pool, urow[b], a["peer_u"], eidT[:, b:b + 1]).then_inc(u_in[b], 16)
                    for b in range(NS):
                        gather(pool, vrow[b], a["peer_v"], eidT[:, b:b + 1]).then_inc(v_in[b], 16)
                    o = Order(pool, qord)
                    with pool.Fori(0, CH) as b:
                        with pool.Fori(0, NJ) as j:
                            it = b * NJ + j
                            for table, slots, sem, idx, free in ((a["peer_u"], urow, u_in, iu, dot_done),
                                                                (a["peer_v"], vrow, v_in, iv, acc_done)):
                                for half in range(2):
                                    s = slice(HR * half, HR * (half + 1))
                                    pool.wait_ge(free, 2 * it + half + 1)
                                    self.alone(pool)
                                    ins = pool.tensor_copy(idx[:, s], eid[:, b, bass.ds(NR * j + HR * half, HR)])
                                    ins.then_inc(qord, 1)
                                    n = (0 if table is a["peer_u"] else 2) + half
                                    pool.wait_ge(qord, 4 * it + n + 1)
                                    self.alone(pool)
                                    for k in range(HR * half, HR * (half + 1)):
                                        gather(pool, slots[k], table, idx[:, k:k + 1]).then_inc(sem[k], 16)

                @block.tensor
                def _(pe):
                    for b in range(NS):
                        if b >= 2:
                            pe.wait_ge(smp_dots, b - 1)
                        for c in range(4):
                            last = pe.matmul(self.bank[4 * (b % 2) + c], sel[:, b, :], htok[0:NS, CH, 512 * c:512 * (c + 1)],
                                             start=True, stop=True)
                        last.then_inc(h_spread, 1)
                    pe.wait_ge(smp_coef, 1)
                    for b in range(NS):
                        pe.wait_ge(v_in[b], 16)
                        for c in range(4):
                            last = pe.matmul(self.bank[4 + c][0:NS, :], coefm[:, b, :],
                                             vrow[b][:, 512 * c:512 * (c + 1)], start=(b == 0), stop=(b == NS - 1))
                        if b == HR - 1:
                            last.then_inc(acc_done, 1)
                    last.then_inc(smp_mixed, 1)
                    pe.wait_ge(smp_mixed, 1)
                    pe.sem_inc(acc_done, 1)

                @block.scalar
                def _(act):
                    def root(rows, n):
                        act.wait_ge(var_ready, n + 1)
                        act.activation(rstd[0:rows, :], mv[0:rows, 1:2], ACT.Sqrt,
                                       bias=self.eps[0:rows, :]).then_inc(root_ready, 1)

                    act.wait_ge(smp_dots, NS)
                    act.activation(ge[:], dots[:], ACT.Gelu).then_inc(smp_gelu, 1)
                    def gelus(b):
                        with act.Fori(0, NJ) as j:
                            for half in range(2):
                                s = slice(HR * half, HR * (half + 1))
                                act.wait_ge(dot_done, 2 * (b * NJ + j) + half + 3)
                                act.activation(ge[:, s], dots[:, s], ACT.Gelu).then_inc(gelu_done, 1)

                    with act.Fori(0, CH - 1) as b:
                        gelus(b)
                        root(P, b)
                    root(NS, CH - 1)
                    gelus(CH - 1)
                    root(P, CH)

                @block.vector
                def _(dve):
                    o = Order(dve, dord)
                    for b in range(NS):
                        dve.wait_ge(u_in[b], 16)
                        dve.wait_ge(h_spread, b + 1)
                        dve.scalar_tensor_tensor(out=urow[b], in0=urow[b], scalar=1.0,
                                                 in1=self.psum[:, 4 * (b % 2):4 * (b % 2) + 4, :].rearrange("p a b -> p (a b)"),
                                                 op0=ALU.mult, op1=ALU.mult,
                                                 accum_out=dots[:, b:b + 1]).then_inc(smp_dots, 1)
                        if b % HR == HR - 1:
                            dve.wait_ge(smp_dots, b + 1)
                            dve.sem_inc(dot_done, 1)
                    dve.wait_ge(smp_gelu, 1)
                    o(dve.tensor_tensor(coef[:], ge[:], gatesT[:], ALU.mult))
                    dve.tensor_tensor(coefm[:], onehot[:], bc(coef[:], NS), ALU.mult).then_inc(smp_coef, 1)
                    dve.wait_ge(ln2_in, 16)
                    lo = Order(dve, lord)
                    acc_order = self.sem("e_acc_order")

                    def prompt_block(b):
                        lo(dve.tensor_scalar(acc[:], htok[:, b, :], ALPHA, None, ALU.mult))
                        self.alone(dve)
                        with dve.Fori(0, NJ) as j:
                            it = b * NJ + j
                            for half in range(2):
                                for k in range(HR * half, HR * (half + 1)):
                                    dve.wait_ge(u_in[k], 16 * it + 32)
                                    last = dve.scalar_tensor_tensor(out=urow[k], in0=urow[k], scalar=1.0,
                                                                    in1=htok[:, b, :], op0=ALU.mult, op1=ALU.mult,
                                                                    accum_out=dots[:, k:k + 1])
                                last.then_inc(dot_done, 1)
                            for half in range(2):
                                s = slice(HR * half, HR * (half + 1))
                                dve.wait_ge(gelu_done, 2 * it + half + 1)
                                dve.wait_ge(acc_done, 2 * it + half + 2)
                                dve.tensor_tensor(coef[:, s], ge[:, s], gates[:, b, bass.ds(NR * j + HR * half, HR)],
                                                  ALU.mult).then_inc(acc_order, 1)
                                n = (HR) * half
                                dve.wait_ge(acc_order, NR * it + n + 1)
                                for m, k in enumerate(range(HR * half, HR * (half + 1))):
                                    dve.wait_ge(v_in[k], 16 * it + 32)
                                    ins = dve.scalar_tensor_tensor(out=acc[:], in0=vrow[k], scalar=coef[:, k:k + 1],
                                                                   in1=acc[:], op0=ALU.mult, op1=ALU.add)
                                    if m < HR - 1:
                                        ins.then_inc(acc_order, 1)
                                        dve.wait_ge(acc_order, NR * it + n + m + 2)
                                    else:
                                        ins.then_inc(acc_done, 1)
                                        dve.wait_ge(acc_done, 2 * it + half + 3)

                    with dve.Fori(0, CH - 1) as b, lo.body(b, CH - 1, 5):
                        prompt_block(b)
                        norm(dve, lo, P, b, htok[:, b, :])
                    dve.wait_ge(smp_mixed, 1)
                    o(dve.scalar_tensor_tensor(out=acc[0:NS, :], in0=htok[0:NS, CH, :], scalar=ALPHA,
                                               in1=self.psum[0:NS, 4:8, :].rearrange("p a b -> p (a b)"),
                                               op0=ALU.mult, op1=ALU.add))
                    norm(dve, o, NS, CH - 1, htok[0:NS, CH, :])
                    prompt_block(CH - 1)
                    norm(dve, lo, P, CH, htok[:, CH - 1, :])


def build_program(nc, arrays, outputs):
    a = {n: nc.dram_tensor("in_" + n, v.shape, F32, kind="ExternalInput").ap() for n, v in arrays.items()}
    o = {n: nc.dram_tensor("out_" + n, shape, F32, kind="ExternalOutput").ap() for n, shape in outputs.items()}
    k = Kernel(nc, a, o)
    k.ys = nc.dram_tensor("branch_acts", [G * GT + FT, P, T], F32).ap()
    k.gates_dram = nc.dram_tensor("branch_gates", [2 * FT, P, T], F32).ap()
    k.build()


OUTPUTS = {
    "y_prompt": (CH, P, D), "y_sample": (NS, D),
    "conv_prompt": (G, P, CT, 3), "ssm_prompt": (G, P, HG * HD), "v_last": (P, FT, P + NS),
    "conv_sample": (G, P, 3, CT, NS), "ssm_sample": (NS, NH, HD, NST),
}


def conv_layout(w):
    rows, inner = w.shape[0], G * GT * P
    x = w[:, :inner].reshape(rows, G, GT, P)
    b = w[:, inner:inner + G * P].reshape(rows, G, 1, P)
    c = w[:, inner + G * P:].reshape(rows, G, 1, P)
    return np.concatenate([b, c, x], 2).transpose(1, 3, 2, 0)


def conv_unlayout(y):
    rows = y.shape[3]
    y = y.transpose(3, 0, 2, 1)
    return np.concatenate([y[:, :, 2:].reshape(rows, -1), y[:, :, 0].reshape(rows, -1), y[:, :, 1].reshape(rows, -1)], 1)


def weight_tiles(i):
    w_in, wa, wb, wo, wq = (i[n][0] for n in ("w_in", "w_branch_a", "w_branch_b", "w_out", "peer_wq"))
    inner, gn = G * GT * P, G * NST
    z0, x0, b0, c0 = 0, inner, 2 * inner, 2 * inner + gn
    u0 = c0 + gn + NH
    v0, ga0, gb0 = u0 + D, u0 + 2 * D, u0 + 3 * D
    cols = []
    for g in range(G):
        cols += [(w_in, 0, b0 + g * P), (w_in, 0, c0 + g * P)]
        cols += [(w_in, 0, x0 + (GT * g + t) * P) for t in range(GT)]
        cols += [(w_in, 0, z0 + (GT * g + t) * P) for t in range(GT)]
    cols += [(w_in, 0, v0 + n * P) for n in range(FT)]
    cols += [(w_in, 0, u0 + n * P) for n in range(FT)]
    for n in range(FT):
        cols.append((w_in, 0, ga0 + n * P))
    for n in range(FT):
        cols.append((w_in, 0, gb0 + n * P))
    for w, r in ((wa, 0), (wa, D), (wb, 0)):
        cols += [(w, r, n * P) for n in range(FT)]
    cols += [(wo, 0, n * P) for n in range(FT)]
    cols += [(wq, 0, n * P) for n in range(FT)]
    out = np.empty((len(cols), P, WCOLS), np.float32)
    for n, (w, r, c) in enumerate(cols):
        out[n].reshape(P, KB, P)[:] = w[r:r + D, c:c + P].reshape(KB, P, P).transpose(1, 0, 2)
    return out


def kernel(**inputs):
    import concourse.bacc as bacc
    from concourse.bass_utils import run_bass_kernel_spmd

    i = {n: np.asarray(v) for n, v in inputs.items()}
    x = np.concatenate([i["x_prompt"][0], i["x_sample"][:, 0]], 0)
    cols = lambda v: v.reshape(FT, P).T
    dt0 = 2 * G * GT * P + 2 * G * NST
    wdt = i["w_in"][0][:, dt0:dt0 + NH]
    per_head = np.broadcast_to(i["d_skip"][0].reshape(G, GT, 2, 1), (G, GT, 2, HD)).reshape(G, GT, P)
    twice = lambda v: np.concatenate([v, v])[:, None]
    rowP = lambda v: np.broadcast_to(v[None], (P,) + v.shape)
    taps = conv_layout(i["conv_w"][0])
    arrays = {
        "w_tiles": weight_tiles(i),
        "xT": x.T.reshape(KB, P, T).transpose(1, 0, 2),
        "w_dt": wdt.reshape(KB, P, NH).transpose(1, 0, 2),
        "dt_rows": np.concatenate([rowP(i["dt_bias"][0]), rowP(i["a_log"][0]),
                                   twice(i["dt_bias"][0]), twice(i["a_log"][0])], 1),
        "ln_cols": np.stack([cols(i[n][0]) for n in ("sgu_ln_g", "sgu_ln_b", "ln1_g", "ln1_b")], 1),
        "g_par": np.concatenate([taps.reshape(G, P, CT * 4), conv_layout(i["conv_b"])[..., 0],
                                 i["ssd_norm_w"][0].reshape(G, GT, P).transpose(0, 2, 1),
                                 per_head.transpose(0, 2, 1)], 2),
        "state_conv": conv_layout(i["state_conv"][0].reshape(NS * 3, -1)).reshape(G, P, CT, NS, 3)
                      .transpose(0, 1, 4, 2, 3),
        "state_ssm": i["state_ssm"][0],
        "sgu_wT": i["sgu_w"][0].transpose(2, 0, 1),
        "sgu_b": rowP(i["sgu_b"][0]),
        "sgu_first": rowP(np.stack([i["sgu_w"][0][:, 0, 0], i["sgu_b"][0][:, 0]])),
        "keys": i["peer_keys"][0].reshape(2 * PH, P, P).transpose(2, 0, 1),
        "ln2_rows": rowP(np.stack([i["ln2_g"][0], i["ln2_b"][0]])),
        "peer_u": i["peer_u"][0],
        "peer_v": i["peer_v"][0],
    }
    arrays = {n: np.ascontiguousarray(v) for n, v in arrays.items()}
    nc = bacc.Bacc("TRN2", target_bir_lowering=False, num_devices=1)
    build_program(nc, arrays, OUTPUTS)
    r = run_bass_kernel_spmd(nc, [{"in_" + n: v for n, v in arrays.items()}], core_ids=[0]).results[0]
    r = {n: np.asarray(r["out_" + n]) for n in OUTPUTS}
    conv_s = conv_unlayout(r["conv_sample"].transpose(0, 1, 3, 4, 2).reshape(G, P, CT, NS * 3))
    ssm_p = r["ssm_prompt"].reshape(G, NST, HG, HD).transpose(0, 2, 3, 1).reshape(1, 1, NH, HD, NST)
    v = r["v_last"].transpose(2, 1, 0).reshape(P + NS, D)
    return (r["y_prompt"].reshape(1, TP, D), r["y_sample"].reshape(NS, 1, D),
            conv_unlayout(r["conv_prompt"]).reshape(1, 1, 3, -1), ssm_p,
            v[:P].reshape(1, 1, P, D), conv_s.reshape(1, NS, 3, -1),
            r["ssm_sample"][None], v[P:].reshape(1, NS, 1, D))
```
